# Optimizing a Trainium2 kernel written in Bass

```python
import math
import jax, jax.numpy as jnp
from jax import lax
import numpy as np

'''One layer of a hybrid diffusion / flow-matching backbone over latent tokens.

Inputs:  x (BATCH, SEQ, D_MODEL) noisy latent tokens on a GRID_W-wide grid,
         c (BATCH, D_MODEL) per-sample conditioning vector,
         ctx (BATCH, CTX_LEN, D_MODEL) context tokens (un-noised prefix of the same trunk),
         c_ctx (D_MODEL,) learned constant conditioning vector for the context tokens,
         plus per-layer weights (leading DEPTH axis).
Output:  (BATCH, SEQ, D_MODEL) final RMSNorm of the latent residual stream.

Per layer: adaLN-modulated RMSNorm -> single combined input projection partitioned into two
parallel head groups (differential attention | sliding-window GQA with sink), both with 2-D
axial rotary on latent tokens, head-group RMSNorm, concatenation, one output projection,
gated residual; then adaLN-modulated RMSNorm -> PEER product-key single-neuron experts, gated residual.
'''

D_MODEL = 2048
BATCH = 1
SEQ = 256
DEPTH = 1

GRID_W = 64
CTX_LEN = 256
EPS = 1e-6
NEG_INF = -1e30
ROPE_THETA = 10000.0

DIFF_DH = 64
DIFF_DV = 2 * DIFF_DH
DIFF_HEADS = D_MODEL // (2 * DIFF_DV)
DIFF_WIDTH = DIFF_HEADS * DIFF_DV
Q_BLOCK = 128

SWA_DH = 64
SWA_HEADS = D_MODEL // (2 * SWA_DH)
SWA_KV = 4
SWA_GROUP = SWA_HEADS // SWA_KV
SWA_WIDTH = SWA_HEADS * SWA_DH
WINDOW = 128
BAND_BLOCK = 128

MIX_WIDTH = DIFF_WIDTH + SWA_WIDTH
ROPE_PAIRS = 16

W_DQ = DIFF_HEADS * 2 * DIFF_DH
W_DK = DIFF_HEADS * 2 * DIFF_DH
W_DV = DIFF_WIDTH
W_SQ = SWA_HEADS * SWA_DH
W_SK = SWA_KV * SWA_DH
W_SV = SWA_KV * SWA_DH
PROJ_OFFSETS = (W_DQ, W_DQ + W_DK, W_DQ + W_DK + W_DV, W_DQ + W_DK + W_DV + W_SQ,
                W_DQ + W_DK + W_DV + W_SQ + W_SK)
PROJ_WIDTH = W_DQ + W_DK + W_DV + W_SQ + W_SK + W_SV

PEER_HEADS = 8
PEER_TOPK = 16
N_KEYS = 128
N_EXPERTS = N_KEYS * N_KEYS
PEER_DQ = 256
PEER_DHALF = PEER_DQ // 2
TOKEN_CHUNK = 128

kernel_name = 'hymba_diffattn_swa_peer_dit_block'

def rms_norm(x, g):
    xf = x.astype(jnp.float32)
    y = xf * lax.rsqrt(jnp.mean(xf * xf, axis=-1, keepdims=True) + EPS)
    return y.astype(x.dtype) * g

def modulate(h, shift, scale):
    return h * (1 + scale) + shift

def head_rms(x, gain):
    xf = x.astype(jnp.float32)
    y = xf * lax.rsqrt(jnp.mean(xf * xf, axis=-1, keepdims=True) + EPS)
    return y.astype(x.dtype).reshape(x.shape[:2] + (-1,)) * gain

def axial_rope_tables(rows, dtype):
    row = jnp.repeat(jnp.arange(rows, dtype=jnp.float32), GRID_W)
    col = jnp.tile(jnp.arange(GRID_W, dtype=jnp.float32), rows)
    freqs = ROPE_THETA ** (-jnp.arange(ROPE_PAIRS, dtype=jnp.float32) / ROPE_PAIRS)
    ang = jnp.stack([row[:, None] * freqs, col[:, None] * freqs], axis=1)
    return jnp.cos(ang).astype(dtype), jnp.sin(ang).astype(dtype)

def apply_rope(x, cos, sin):
    xr = x.reshape(x.shape[:-1] + (2, 2, ROPE_PAIRS))
    x1, x2 = xr[..., 0, :], xr[..., 1, :]
    shape = (cos.shape[0],) + (1,) * (x.ndim - 3) + (2, ROPE_PAIRS)
    cs, sn = cos.reshape(shape), sin.reshape(shape)
    out = jnp.stack([x1 * cs - x2 * sn, x2 * cs + x1 * sn], axis=-2)
    return out.reshape(x.shape)

def split_heads(p):
    B, T = p.shape[:2]
    dq, dk, dv, sq, sk, sv = jnp.split(p, list(PROJ_OFFSETS), axis=-1)
    return (dq.reshape(B, T, DIFF_HEADS, 2, DIFF_DH), dk.reshape(B, T, DIFF_HEADS, 2, DIFF_DH),
            dv.reshape(B, T, DIFF_HEADS, DIFF_DV), sq.reshape(B, T, SWA_HEADS, SWA_DH),
            sk.reshape(B, T, SWA_KV, SWA_DH), sv.reshape(B, T, SWA_KV, SWA_DH))

def diff_attend(q, k, v, lam):
    s = jnp.einsum('bqhid,bkhid->bhiqk', q, k).astype(jnp.float32) * (DIFF_DH ** -0.5)
    a = jax.nn.softmax(s, axis=-1)
    a = a[:, :, 0] - lam * a[:, :, 1]
    return jnp.einsum('bhqk,bkhe->bqhe', a.astype(v.dtype), v)

def diff_latent(q, k, v, kc, vc, lam):
    B, S = q.shape[:2]
    nq = S // Q_BLOCK
    k_all = jnp.concatenate([kc, k], axis=1)
    v_all = jnp.concatenate([vc, v], axis=1)
    qb = jnp.moveaxis(q.reshape((B, nq, Q_BLOCK) + q.shape[2:]), 1, 0)
    o = lax.map(lambda qblk: diff_attend(qblk, k_all, v_all, lam), qb)
    return jnp.moveaxis(o, 0, 1).reshape(B, S, DIFF_HEADS, DIFF_DV)

def swa_latent(q, k, v, kc, vc, sink):
    B, S = q.shape[:2]
    nb = S // BAND_BLOCK
    scale = SWA_DH ** -0.5
    qb = q.reshape(B, nb, BAND_BLOCK, SWA_KV, SWA_GROUP, SWA_DH)

    def pad_blocks(t):
        t = jnp.pad(t, ((0, 0), (BAND_BLOCK, BAND_BLOCK), (0, 0), (0, 0)))
        return t.reshape(B, nb + 2, BAND_BLOCK, SWA_KV, SWA_DH)

    def band(t):
        return jnp.concatenate([t[:, :-2], t[:, 1:-1], t[:, 2:]], axis=2)

    kb, vb = band(pad_blocks(k)), band(pad_blocks(v))
    qi = jnp.arange(BAND_BLOCK)[:, None]
    ki = jnp.arange(3 * BAND_BLOCK)[None, :]
    rel_ok = jnp.abs(qi + BAND_BLOCK - ki) <= WINDOW
    sink_l = sink.reshape(SWA_KV, SWA_GROUP).astype(jnp.float32)
    n_band = 3 * BAND_BLOCK

    def one_block(args):
        qn, kn, vn, n = args
        kpos = (n - 1) * BAND_BLOCK + ki
        ok = rel_ok & (kpos >= 0) & (kpos < S)
        s_band = jnp.einsum('bqhgd,bkhd->bhgqk', qn, kn).astype(jnp.float32) * scale
        s_band = jnp.where(ok, s_band, NEG_INF)
        s_ctx = jnp.einsum('bqhgd,bkhd->bhgqk', qn, kc).astype(jnp.float32) * scale
        s_sink = jnp.broadcast_to(sink_l[None, :, :, None, None], s_band.shape[:-1] + (1,))
        p = jax.nn.softmax(jnp.concatenate([s_sink, s_band, s_ctx], axis=-1), axis=-1)
        pb = p[..., 1:1 + n_band].astype(vn.dtype)
        pc = p[..., 1 + n_band:].astype(vc.dtype)
        return (jnp.einsum('bhgqk,bkhd->bqhgd', pb, vn)
                + jnp.einsum('bhgqk,bkhd->bqhgd', pc, vc))

    xs = (jnp.moveaxis(qb, 1, 0), jnp.moveaxis(kb, 1, 0), jnp.moveaxis(vb, 1, 0),
          jnp.arange(nb, dtype=jnp.int32))
    o = lax.map(one_block, xs)
    return jnp.moveaxis(o, 0, 1).reshape(B, S, SWA_HEADS, SWA_DH)

def swa_context(qc, kc, vc, sink):
    B, L = qc.shape[:2]
    qg = qc.reshape(B, L, SWA_KV, SWA_GROUP, SWA_DH)
    s = jnp.einsum('bqhgd,bkhd->bhgqk', qg, kc).astype(jnp.float32) * (SWA_DH ** -0.5)
    sink_l = sink.reshape(SWA_KV, SWA_GROUP).astype(jnp.float32)
    s_sink = jnp.broadcast_to(sink_l[None, :, :, None, None], s.shape[:-1] + (1,))
    p = jax.nn.softmax(jnp.concatenate([s_sink, s], axis=-1), axis=-1)[..., 1:]
    o = jnp.einsum('bhgqk,bkhd->bqhgd', p.astype(vc.dtype), vc)
    return o.reshape(B, L, SWA_HEADS, SWA_DH)

def token_mixers(h, hc, w_in, w_out, lam, lam_init, diff_norm, sink, swa_norm, cos, sin, with_ctx_out):
    dq, dk, dv, sq, sk, sv = split_heads(h @ w_in)
    dqc, dkc, dvc, sqc, skc, svc = split_heads(hc @ w_in)
    dq, dk = apply_rope(dq, cos, sin), apply_rope(dk, cos, sin)
    sq, sk = apply_rope(sq, cos, sin), apply_rope(sk, cos, sin)

    def merge(o_diff, o_swa):
        return jnp.concatenate([head_rms(o_diff, diff_norm) * (1.0 - lam_init),
                                head_rms(o_swa, swa_norm)], axis=-1) @ w_out

    out = merge(diff_latent(dq, dk, dv, dkc, dvc, lam), swa_latent(sq, sk, sv, skc, svc, sink))
    out_c = None
    if with_ctx_out:
        out_c = merge(diff_attend(dqc, dkc, dvc, lam), swa_context(sqc, skc, svc, sink))
    return out, out_c

def peer(h, w_q, sub_keys, u, v):
    B, T, D = h.shape
    q = (h @ w_q).reshape(B, T, PEER_HEADS, 2, PEER_DHALF)
    s = jnp.einsum('bshid,hikd->bshik', q, sub_keys).astype(jnp.float32)
    s1, i1 = lax.top_k(s[..., 0, :], PEER_TOPK)
    s2, i2 = lax.top_k(s[..., 1, :], PEER_TOPK)
    cand = (s1[..., :, None] + s2[..., None, :]).reshape(B, T, PEER_HEADS, PEER_TOPK * PEER_TOPK)
    cidx = (i1[..., :, None] * N_KEYS + i2[..., None, :]).reshape(B, T, PEER_HEADS, PEER_TOPK * PEER_TOPK)
    top_s, pos = lax.top_k(cand, PEER_TOPK)
    idx = jnp.take_along_axis(cidx, pos, axis=-1)
    g = jax.nn.softmax(top_s, axis=-1)
    n_chunks = (B * T) // TOKEN_CHUNK
    hf = h.reshape(n_chunks, TOKEN_CHUNK, D)
    idx = idx.reshape(n_chunks, TOKEN_CHUNK, PEER_HEADS * PEER_TOPK)
    g = g.reshape(n_chunks, TOKEN_CHUNK, PEER_HEADS * PEER_TOPK)

    def one_chunk(args):
        hc, ic, gc = args
        u_sel = u[ic]
        act = jax.nn.gelu(jnp.einsum('cd,ced->ce', hc, u_sel))
        wts = (gc * act.astype(jnp.float32)).astype(v.dtype)
        return jnp.einsum('ce,ced->cd', wts, v[ic])

    return lax.map(one_chunk, (hf, idx, g)).reshape(B, T, D)

def setup_inputs(seed: int = 0) -> dict:
    key = jax.random.key(seed)
    ks = jax.random.split(key, 22)

    def nrm(k, shape, s):
        return jax.random.normal(k, shape, jnp.float32) * s

    D = D_MODEL
    return {
        'x': nrm(ks[0], (BATCH, SEQ, D), 1.0),
        'c': nrm(ks[1], (BATCH, D), 1.0),
        'ctx': nrm(ks[2], (BATCH, CTX_LEN, D), 1.0),
        'c_ctx': nrm(ks[3], (D,), 1.0),
        'w_ada': nrm(ks[4], (DEPTH, D, 6 * D), D ** -0.5),
        'b_ada': nrm(ks[5], (DEPTH, 6 * D), 0.02),
        'norm_attn': 1.0 + nrm(ks[6], (DEPTH, D), 0.02),
        'w_in': nrm(ks[7], (DEPTH, D, PROJ_WIDTH), D ** -0.5),
        'diff_lambda_q1': nrm(ks[8], (DEPTH, DIFF_DH), 0.1),
        'diff_lambda_k1': nrm(ks[9], (DEPTH, DIFF_DH), 0.1),
        'diff_lambda_q2': nrm(ks[10], (DEPTH, DIFF_DH), 0.1),
        'diff_lambda_k2': nrm(ks[11], (DEPTH, DIFF_DH), 0.1),
        'diff_norm': 1.0 + nrm(ks[12], (DEPTH, DIFF_WIDTH), 0.02),
        'swa_sink': nrm(ks[13], (DEPTH, SWA_HEADS), 1.0),
        'swa_norm': 1.0 + nrm(ks[14], (DEPTH, SWA_WIDTH), 0.02),
        'w_out': nrm(ks[15], (DEPTH, MIX_WIDTH, D), MIX_WIDTH ** -0.5),
        'norm_ffn': 1.0 + nrm(ks[16], (DEPTH, D), 0.02),
        'peer_w_q': nrm(ks[17], (DEPTH, D, PEER_HEADS * PEER_DQ), D ** -0.5),
        'peer_sub_keys': nrm(ks[18], (DEPTH, PEER_HEADS, 2, N_KEYS, PEER_DHALF), PEER_DHALF ** -0.5),
        'peer_u': nrm(ks[19], (DEPTH, N_EXPERTS, D), D ** -0.5),
        'peer_v': nrm(ks[20], (DEPTH, N_EXPERTS, D), 1.0),
        'final_norm': 1.0 + nrm(ks[21], (D,), 0.02),
    }

def reference(x, c, ctx, c_ctx, w_ada, b_ada, norm_attn, w_in, diff_lambda_q1, diff_lambda_k1,
              diff_lambda_q2, diff_lambda_k2, diff_norm, swa_sink, swa_norm, w_out, norm_ffn,
              peer_w_q, peer_sub_keys, peer_u, peer_v, final_norm):
    B, S, D = x.shape
    ROWS = S // GRID_W
    cos, sin = axial_rope_tables(ROWS, x.dtype)
    xc = ctx
    for l in range(DEPTH):
        last = l == DEPTH - 1
        mod = jax.nn.silu(c) @ w_ada[l] + b_ada[l]
        mod_c = jax.nn.silu(c_ctx) @ w_ada[l] + b_ada[l]
        sh1, sc1, g1, sh2, sc2, g2 = [m[:, None, :] for m in jnp.split(mod, 6, axis=-1)]
        sh1c, sc1c, g1c, sh2c, sc2c, g2c = jnp.split(mod_c, 6, axis=-1)

        lam_init = 0.8 - 0.6 * math.exp(-0.3 * l)
        lam = (jnp.exp(jnp.sum(diff_lambda_q1[l].astype(jnp.float32) * diff_lambda_k1[l].astype(jnp.float32)))
               - jnp.exp(jnp.sum(diff_lambda_q2[l].astype(jnp.float32) * diff_lambda_k2[l].astype(jnp.float32)))
               + lam_init)

        h = modulate(rms_norm(x, norm_attn[l]), sh1, sc1)
        hc = modulate(rms_norm(xc, norm_attn[l]), sh1c, sc1c)
        a, a_c = token_mixers(h, hc, w_in[l], w_out[l], lam, lam_init, diff_norm[l], swa_sink[l],
                              swa_norm[l], cos, sin, not last)
        x = x + g1 * a
        h2 = modulate(rms_norm(x, norm_ffn[l]), sh2, sc2)
        x = x + g2 * peer(h2, peer_w_q[l], peer_sub_keys[l], peer_u[l], peer_v[l])
        if not last:
            xc = xc + g1c * a_c
            h2c = modulate(rms_norm(xc, norm_ffn[l]), sh2c, sc2c)
            xc = xc + g2c * peer(h2c, peer_w_q[l], peer_sub_keys[l], peer_u[l], peer_v[l])
    return rms_norm(x, final_norm)


_drawn_inputs = setup_inputs


def setup_inputs(seed=0):
    import zlib

    import numpy as np

    out = dict(_drawn_inputs(seed))
    spreads = {}
    factors = {'diff_lambda_k1': 4.318, 'diff_lambda_q2': 4.484, 'swa_sink': 8.0, 'final_norm': 2.75}
    for name, (base, spread) in spreads.items():
        noise = np.random.default_rng([zlib.crc32(name.encode()), seed]).standard_normal(out[name].shape)
        drawn = base * np.exp(spread * noise) if base else spread * noise
        out[name] = __import__('jax').numpy.asarray(drawn.astype(out[name].dtype))
    for name, factor in factors.items():
        out[name] = (out[name] * factor).astype(out[name].dtype)
    return out
```

```python
from contextlib import ExitStack

import numpy as np
import concourse.bass as bass
from concourse import mybir

F32 = mybir.dt.float32
F32R = mybir.dt.float32r
BF16 = mybir.dt.bfloat16
U32 = mybir.dt.uint32
ALU = mybir.AluOpType
ACT = mybir.ActivationFunctionType
AX = mybir.AxisListType.X

P = 128
D = 2048
KT = D // P
T = 256
QT = T // P
NTOK = 2 * QT
DIFF_HEADS, SWA_HEADS, DH, SWA_KV = 8, 16, 64, 4
GRID_W, ROPE_PAIRS, ROPE_THETA, WINDOW = 64, 16, 10000.0, 128
HEADS, TOPK, NKEYS = 8, 16, 128
NE_TILES = NKEYS
EPS = 1e-6
SCALE = DH ** -0.5
LAM_INIT = 0.2
NEG = -1e30
LOWEST = -3.0e38
UNIT = 1024
RAW, SPLIT, ADA = 4, 2, 4

N_IN, N_OUT, N_Q, N_U, N_V = 72, 32, 32, 256, 256
U_IN, U_OUT = 0, N_IN
U_Q = U_OUT + N_OUT
U_U = U_Q + N_Q
U_V = U_U + N_U
U_END = U_V + N_V

PARAMS = [("cc", KT * 2), ("b_ada", 96), ("norm_attn", KT), ("norm_ffn", KT), ("final_norm", KT),
          ("head_gain", KT), ("sink", SWA_HEADS), ("lam_qk", 4 * DH)]
CONSTS = [("ident", P), ("iota", P), ("iota16", 16), ("cos", QT * DH), ("sin", QT * DH), ("mask", QT * P)]


def offsets(cols):
    at, out = 0, {}
    for name, n in cols:
        out[name] = (at, at + n)
        at += n
    return out, at


PAR, NPAR = offsets(PARAMS)
CON, NCON = offsets(CONSTS)

CHUNKS = ["k", "k", "kv", "v", "v", "q", "q", "q", "q"]
BANKS = [(0, 1, 2, 3), (4, 5, 6, 7), (0, 1, 2, 3), (4, 5, 6, 7), (0, 1, 2, 3), (4, 5), (6, 7), (4, 5), (6, 7)]
ADA_AT = {1: 7, 2: 3, 3: 7, 4: 3, 5: 5}


def block_program(nc, x_lat, x_ctx, par, con, w_ada, w_in, w_out, w_q, sk, u, v, x2_dram, out):
    with ExitStack() as ctx:
        sem_names = ("par_in con_in x_in xc_in keys_in x2_in x2_out out_done "
                     "silu ada1_used ada2_used ada_row_kept ada_col ada_col_kept ada_zeroed ada_sum "
                     "mod_ready sq_ready norm_sum norm_sqrt norm_y norm_h norm_l tail_y "
                     "dve act pool const_ready lam_ready lam_exp "
                     "w_high w_low w_free evac_a evac_d turn_k turn_k_kept turn_q turn_q_kept "
                     "scored biased exp_done combined turned turned_kept pv_done o_stored o_squared "
                     "head_sum head_sqrt head_scaled o_turned o_high o_low "
                     "attn_out x2_ready qp_done qp_kept sc_done sc_kept "
                     "top_s_ready top_exp gates_ready gates_turned gates_kept gelu_done "
                     "dist_b dist_b2 hot_a hot_b routed route_used p_high p_low v_done x3_ready").split()
        S = {n: ctx.enter_context(nc.semaphore(n)) for n in sem_names}
        raw_in = [ctx.enter_context(nc.semaphore(f"raw_in{i}")) for i in range(RAW)]
        ada_in = [ctx.enter_context(nc.semaphore(f"ada_in{i}")) for i in range(ADA)]

        base = 16512
        KB = 1024
        slab = nc.sbuf_usable_end - base - 64
        names = {}

        def at(name, shape, dt, offset):
            names[name] = offset
            return nc.alloc_sbuf_tensor_at(name, shape, dt, offset=base + offset)

        raw = at("raw", [P, RAW, UNIT], F32, 0)
        w_hi = at("w_hi", [P, SPLIT, UNIT], F32R, 16 * KB)
        w_lo = at("w_lo", [P, SPLIT, UNIT], F32R, 24 * KB)
        o = 32 * KB
        small = {}
        for name, shape, dt in [("ident", [P, P], F32), ("iota", [P, P], F32), ("iota16", [P, 16], F32),
                                ("b_ada", [P, 96], F32), ("norms", [P, 4 * KT], F32), ("mod", [P, 96], F32),
                                ("modc", [P, 32], F32), ("eps", [P, 1], F32), ("scl", [P, 4 * KT], F32),
                                ("i1T", [P, T], F32), ("i2T", [P, T], F32), ("gT", [P, T], F32),
                                ("rstd", [P, T], F32), ("ones", [P, 1], F32)]:
            small[name] = at(name, shape, dt, o)
            o += 4 * int(np.prod(shape[1:]))
            o = (o + 31) // 32 * 32
        ident, iota, iota16, b_ada, norms, mod, modc, eps, scl, i1T, i2T, gT, rstd, ones = (
            small[n] for n in ("ident iota iota16 b_ada norms mod modc eps scl i1T i2T gT rstd ones").split())
        R = (o + 1023) // 1024 * 1024
        assert base + R + 168 * KB <= nc.sbuf_usable_end, (R, nc.sbuf_usable_end - base - R)

        hc_h = at("hc_h", [P, KT, T], F32R, R)
        hc_l = at("hc_l", [P, KT, T], F32R, R + 16 * KB)
        kT = at("kT", [P, 10, NTOK * P], F32, R)
        qTd = at("qTd", [P, 8, T], F32, R + 20 * KB)
        Kt = at("Kt", [P, NTOK, 1280], F32, R + 32 * KB)
        O = at("O", [P, QT, D], F32, R + 32 * KB)
        V = at("V", [P, NTOK, 1280], F32, R + 52 * KB)
        Qt = at("Qt", [P, 2, QT, 512], F32, R + 72 * KB)
        qTs = at("qTs", [P, 8, T], F32, R + 80 * KB)
        x_c = at("x_c", [P, KT, T], F32, R + 32 * KB)
        sq = at("sq", [P, KT, T], F32, R + 48 * KB)
        modrow = at("modrow", [2, 4096], F32, R + 64 * KB)
        yb = at("yb", [P, 4, T], F32, R + 80 * KB)
        ada = at("ada", [P, ADA, UNIT], F32, R + 88 * KB)
        acc = at("acc", [P, 2, UNIT], F32, R + 104 * KB)
        x = at("x", [P, KT, T], F32, R + 112 * KB)
        hl_h = at("hl_h", [P, KT, T], F32R, R + 128 * KB)
        hl_l = at("hl_l", [P, KT, T], F32R, R + 144 * KB)
        pr = at("pr", [P, 2, 4, 512], F32, R + 128 * KB)
        pT = at("pT", [P, 4, 4, P], F32, R + 144 * KB)
        oT_h = at("oT_h", [P, KT, T], F32R, R + 128 * KB)
        oT_l = at("oT_l", [P, KT, T], F32R, R + 144 * KB)
        cs = at("cs", [P, 2, QT, DH], F32, R + 160 * KB)
        mask = at("mask", [P, QT, P], F32, R + 161 * KB)
        rt = at("rt", [P, 2, 512], F32, R + 162 * KB)
        silu_c = at("silu_c", [P, KT, 2], F32, R + 166 * KB)
        lam_v = at("lam_v", [P, 4, DH], F32, R + 166 * KB + 128)
        st = at("st", [P, 8, 64], F32, R + 52 * KB + 20 * KB)
        nsink = at("nsink", [P, 2, SWA_HEADS], F32, R + 167 * KB + 128)
        lam = at("lam", [P, 8], F32, R + 167 * KB + 256)
        zeros = at("zeros", [P, 512], BF16, R + 162 * KB)

        sq2 = at("sq2", [P, KT, T], F32, R + 32 * KB)
        yb2 = at("yb2", [P, 4, T], F32, R + 80 * KB)
        h2_h = at("h2_h", [P, KT, T], F32R, R + 128 * KB)
        h2_l = at("h2_l", [P, KT, T], F32R, R + 144 * KB)
        qpT = at("qpT", [P, KT, T], F32, R)
        skT = at("skT", [P, KT, P], F32, R + 24 * KB)
        sc = at("sc", [P, QT, KT, P], F32, R + 64 * KB)

        A = at("A", [P, NE_TILES, T], F32, R)
        tk = 80 * KB + R
        sc2 = at("sc2", [P, P], F32, tk)
        v16 = at("v16", [P, KT, TOPK], F32, tk + 1 * KB)
        ix16 = at("ix16", [P, KT, TOPK], U32, tk + 2 * KB)
        if16 = at("if16", [P, KT, TOPK], F32, tk + 3 * KB)
        cand = at("cand", [P, HEADS, 256], F32, tk + 4 * KB)
        cand2 = at("cand2", [P, 256], F32, tk + 12 * KB)
        tops = at("tops", [P, QT, HEADS, TOPK], F32, tk + 13 * KB)
        pos = at("pos", [P, HEADS, TOPK], U32, tk + 14 * KB)
        pab = at("pab", [P, 2, HEADS * TOPK], U32, tk + 15 * KB)
        pabf = at("pabf", [P, 2, HEADS * TOPK], F32, tk + 16 * KB)
        hit = at("hit", [P, HEADS * TOPK, 16], F32, tk + 17 * KB)
        sel = at("sel", [P, QT, 3, HEADS * TOPK], F32, tk + 25 * KB)
        gs = at("gs", [P, QT, 2, HEADS], F32, tk + 28 * KB)
        ge = at("ge", [P, QT, HEADS, TOPK], F32, tk + 29 * KB)
        hotA = at("hotA", [P, 2, 4, P], F32, R + 128 * KB)
        hotB = at("hotB", [P, 2, 4, P], F32, R + 132 * KB)
        x2 = at("x2", [P, KT, T], F32, R + 136 * KB)
        p_hi = at("p_hi", [P, 2, T], F32R, R + 152 * KB)
        p_lo = at("p_lo", [P, 2, T], F32R, R + 154 * KB)
        x3 = at("x3", [P, KT, T], F32, R)
        sq3 = at("sq3", [P, KT, T], F32, R + 16 * KB)
        ot = at("ot", [P, KT, T], F32, R + 32 * KB)
        ones_sq = at("ones_sq", [P, P], F32, R + 167 * KB + 512)
        PS = ctx.enter_context(nc.psum_tensor("PS", [P, 8, 512], F32))

        def region(dt):
            return PS[:, dt // 2, (dt % 2) * T:(dt % 2) * T + T]

        parv = {n: par[:, a:b] for n, (a, b) in PAR.items()}
        conv = {n: con[:, a:b] for n, (a, b) in CON.items()}
        SMALL_LOADS = [(silu_c[:], parv["cc"].rearrange("p (k c) -> p k c", c=2)), (b_ada[:], parv["b_ada"]),
                       (norms[:], par[:, PAR["norm_attn"][0]:PAR["head_gain"][1]]),
                       (nsink[:, 0, :], parv["sink"]), (lam_v[:], parv["lam_qk"].rearrange("p (a d) -> p a d", a=4)),
                       (ident[:], conv["ident"]), (iota[:], conv["iota"]), (iota16[:], conv["iota16"]),
                       (cs[:, 0], conv["cos"].rearrange("p (q d) -> p q d", q=QT)),
                       (cs[:, 1], conv["sin"].rearrange("p (q d) -> p q d", q=QT)),
                       (mask[:], conv["mask"].rearrange("p (q d) -> p q d", q=QT))]
        N_SMALL = 16 * len(SMALL_LOADS)

        block = ctx.enter_context(nc.Block())

        @block.sync
        def _(sp):
            for dst, src in SMALL_LOADS:
                sp.dma_start(dst, src).then_inc(S["par_in"], 16)

            def load_ada(n_slot, chunk, kt):
                sp.dma_start(ada[:, n_slot, :], w_ada[chunk, kt]).then_inc(ada_in[n_slot], 16)

            def load_unit(src, slot):
                sp.dma_start(raw[:, slot, :], src).then_inc(raw_in[slot], 16)

            w_ada_flat = w_ada.rearrange("c k p n -> (c k) p n")
            for j in range(ADA):
                sp.dma_start(ada[:, j, :], w_ada_flat[j]).then_inc(ada_in[j], 16)
            sp.dma_start(x[:], x_lat).then_inc(S["x_in"], 16)
            sp.dma_start(x_c[:], x_ctx).then_inc(S["xc_in"], 16)
            with sp.Fori(1, 16) as b:
                for j in range(ADA):
                    sp.wait_ge(S["ada1_used"], 4 * b + (j - 3))
                    sp.dma_start(ada[:, j, :], w_ada_flat[4 * b + j]).then_inc(ada_in[j], 16)

            def ada2(b, first=False):
                for j in range(ADA):
                    if first:
                        sp.wait_ge(S["ada1_used"], 61 + j)
                    else:
                        sp.wait_ge(S["ada2_used"], 4 * b + (j - 3))
                    sp.dma_start(ada[:, j, :], w_ada_flat[4 * b + 64 + j]).then_inc(ada_in[j], 16)

            def units(src, b, first_unit, first=False):
                for j in range(RAW):
                    if not first:
                        sp.wait_ge(S["w_low"], 4 * b + (first_unit + j - 3))
                    sp.dma_start(raw[:, j, :], src[4 * b + j]).then_inc(raw_in[j], 16)

            units(w_in, 0, U_IN, first=True)
            ada2(0, first=True)
            ada2(1)
            with sp.Fori(1, 10) as b:
                units(w_in, b, U_IN)
                ada2(2 * b)
                ada2(2 * b + 1)
            with sp.Fori(0, 4) as b:
                ada2(b + 20)
                units(w_in, 2 * b + 10, U_IN)
                units(w_in, 2 * b + 11, U_IN)
            with sp.Fori(0, 4) as b:
                ada2(b + 24)
                units(w_out, 2 * b, U_OUT)
                units(w_out, 2 * b + 1, U_OUT)
            with sp.Fori(0, 4) as b:
                ada2(b + 28)
                units(w_q, 2 * b, U_Q)
                units(w_q, 2 * b + 1, U_Q)
            sp.wait_ge(S["attn_out"], 1)
            sp.dma_start(skT[:], sk).then_inc(S["keys_in"], 16)
            sp.wait_ge(S["x2_ready"], KT)
            sp.dma_start(x2_dram, x[:]).then_inc(S["x2_out"], 16)
            with sp.Fori(0, N_U // 4) as b:
                units(u, b, U_U)
            sp.wait_ge(S["x2_out"], 16)
            sp.wait_ge(S["w_free"], U_V + SPLIT)
            sp.dma_start(x2[:], x2_dram).then_inc(S["x2_in"], 16)
            with sp.Fori(0, N_V // 4) as b:
                units(v, b, U_V)
            for g in range(4):
                sp.wait_ge(S["tail_y"], 4 * g + 4)
                sp.dma_start(out[:, 4 * g:4 * g + 4, :], ot[:, 4 * g:4 * g + 4, :]).then_inc(S["out_done"], 16)
            sp.wait_ge(S["out_done"], 64)

        @block.gpsimd
        def _(pool):
            nc.gpsimd.memset(eps[:], EPS).then_inc(S["const_ready"], 1)
            nc.gpsimd.memset(ones[:], 1.0).then_inc(S["const_ready"], 1)
            nc.gpsimd.memset(ones_sq[:], 1.0).then_inc(S["const_ready"], 1)
            for c in range(8):
                if c == 7:
                    pool.wait_ge(S["evac_d"], EVAC_D)
                    nc.gpsimd.memset(zeros[:], 0.0).then_inc(S["const_ready"], 1)
                if c >= 2:
                    pool.wait_ge(S["ada_col"], c)
                nc.gpsimd.memset(acc[:, c % 2, :], 0.0).then_inc(S["ada_zeroed"], 1)
            pool.wait_ge(S["gates_kept"], 6)
            pool.wait_ge(S["w_free"], U_V + SPLIT)

            def distance(t0, s):
                nc.gpsimd.tensor_tensor(hotB[:, s], iota[:].unsqueeze(1).broadcast_to([P, 4, P]),
                                        i2T[:, bass.ds(t0, 4)].unsqueeze(2).broadcast_to([P, 4, P]),
                                        ALU.subtract).then_inc(S["dist_b"], 1)

            distance(0, 0)
            distance(4, 1)
            with pool.Fori(1, T // 8) as b:
                for s in range(2):
                    pool.wait_ge(S["route_used"], 2 * b + (s - 1))
                    distance(8 * b + 4 * s, s)

        @block.scalar
        def _(act):
            def split_high(b, j):
                act.wait_ge(raw_in[j], 16 * b + 16)
                act.wait_ge(S["w_free"], 4 * b + (j + 1))
                nc.scalar.activation(w_hi[:, j % SPLIT, :], raw[:, j, :], ACT.Copy).then_inc(S["w_high"], 1)

            act.wait_ge(S["par_in"], N_SMALL)
            nc.scalar.activation(silu_c[:], silu_c[:], ACT.Silu).then_inc(S["silu"], 1)

            def squares(xin, dst, waits):
                for k in range(KT):
                    waits(k)
                    nc.scalar.activation(dst[:, k, :], xin[:, k, :], ACT.Square).then_inc(S["sq_ready"], 1)

            def inv_root(r):
                act.wait_ge(S["norm_sum"], r + 1)
                nc.scalar.activation(rstd[:], PS[:, NORM_BANK[r], 0:T], ACT.Sqrt, bias=eps[:, 0:1],
                                     scale=1.0 / D).then_inc(S["norm_sqrt"], 1)

            def shift_high(r, out_h, shift, yb_):
                for k in range(KT):
                    act.wait_ge(S["norm_y"], KT * r + k + 1)
                    nc.scalar.activation(out_h[:, k, :], yb_[:, k % 4, :], ACT.Identity,
                                         bias=shift[:, k:k + 1]).then_inc(S["norm_h"], 1)

            act.wait_ge(S["lam_ready"], 1)
            nc.scalar.activation(lam[:, 2:4], lam[:, 0:2], ACT.Exp).then_inc(S["lam_exp"], 1)
            act.wait_ge(S["xc_in"], 16)
            squares(x_c, sq, lambda k: None)
            act.wait_ge(S["const_ready"], 3)
            inv_root(0)
            act.wait_ge(S["x_in"], 16)
            squares(x, sq, lambda k: None)
            for c in range(4):
                act.wait_ge(S["ada1_used"], KT * (c + 1))
                nc.scalar.activation(modrow[:, c * UNIT:(c + 1) * UNIT].rearrange("p (a n) -> p a n", a=2),
                                     PS[0:2, 2 * (c % 2):2 * (c % 2) + 2, :], ACT.Copy).then_inc(S["ada_row_kept"], 1)
            split_high(0, 0)
            split_high(0, 1)
            shift_high(0, hc_h, modc, yb)
            inv_root(1)
            shift_high(1, hl_h, mod, yb)

            def evac_copy(dst, src):
                nc.scalar.activation(dst, src, ACT.Copy).then_inc(S["evac_a"], 1)

            def evac(c):
                act.wait_ge(S["w_free"], 8 * (c + 1) + SPLIT)
                kind, banks = CHUNKS[c], BANKS[c]
                for t in range(NTOK if kind != "q" else 0):
                    src = PS[:, banks[t], :]
                    if kind == "k" and t < QT:
                        evac_copy(Kt[:, t, c * 512:c * 512 + 512], src)
                    if kind == "kv":
                        if t < QT:
                            evac_copy(Kt[:, t, 1024:1280], src[:, 0:256])
                        evac_copy(V[:, t, 1024:1280], src[:, 256:512])
                    if kind == "v":
                        evac_copy(V[:, t, (c - 3) * 512:(c - 3) * 512 + 512], src)

            def keep_k(k):
                act.wait_ge(S["turn_k"], k + 1)
                nc.scalar.activation(kT[:, k, :], PS[:, k % 4, :], ACT.Copy).then_inc(S["turn_k_kept"], 1)

            def keep_q(c):
                dst = (qTd, qTs)[c // 2]
                for a in range(2):
                    act.wait_ge(S["turn_q"], 2 * c + a + 1)
                    at_ = 4 * (c % 2) + 2 * a
                    nc.scalar.activation(dst[:, at_:at_ + 2, :],
                                         PS[:, TURN_Q_BANK[c] + a, :].rearrange("p (a t) -> p a t", a=2),
                                         ACT.Copy).then_inc(S["turn_q_kept"], 1)

            for c in range(9):
                for b in (2 * c, 2 * c + 1):
                    for j in range(RAW):
                        if b or j > 1:
                            split_high(b, j)
                        if c and b == 2 * c and j == 1:
                            evac(c - 1)
                        if c >= 6 and b == 2 * c and j == 1:
                            if c == 6:
                                for k in range(10):
                                    keep_k(k)
                            else:
                                keep_q(c - 7)
            split_high(18, 0)
            split_high(18, 1)
            evac(8)
            keep_q(2)
            keep_q(3)

            def exp_tile(n):
                m, slot = n // 4, n % 4
                act.wait_ge(S["biased"], n + 1)
                if m >= 2 and slot == 0:
                    act.wait_ge(S["turned"], turned_after(m - 2))
                nc.scalar.activation(pr[:, m % 2, slot, :], PS[:, slot, :], ACT.Exp, bias=st[:, 1, n:n + 1],
                                     scale=SCALE, accum_out=st[:, 2, n:n + 1]).then_inc(S["exp_done"], 1)
                if m >= 8:
                    h = swa_head(m, n % 2)
                    nc.scalar.activation(st[:, 3, n:n + 1], nsink[:, 0, h:h + 1], ACT.Exp,
                                         bias=st[:, 1, n:n + 1]).then_inc(S["exp_done"], 1)

            def keep_turned(s):
                act.wait_ge(S["turned"], s + 1)
                if s >= 4:
                    act.wait_ge(S["pv_done"], s - 3)
                nc.scalar.activation(pT[:, s % 4], PS[:, 4 + s % 2, :].rearrange("p (a q) -> p a q", a=4),
                                     ACT.Copy).then_inc(S["turned_kept"], 1)

            def square_out(s):
                act.wait_ge(S["o_stored"], s + 1)
                m, slot = turned_tile(s)
                if s < 16:
                    cols, w = slice(m * P, (m + 1) * P), P
                else:
                    h = swa_head(m, slot % 2)
                    cols, w = slice(1024 + h * DH, 1024 + (h + 1) * DH), DH
                if s >= 4:
                    act.wait_ge(S["o_squared"], s - 3)
                nc.scalar.activation(rt[:, 1, (s % 4) * P:(s % 4) * P + w], O[:, slot // 2, cols], ACT.Square,
                                     accum_out=st[:, 6, s:s + 1]).then_inc(S["o_squared"], 1)

            for m in range(17):
                if m < 16:
                    for n in range(4 * m, 4 * m + 4):
                        exp_tile(n)
                if m >= 1:
                    for s in heads_seq(m - 1):
                        keep_turned(s)
                    for s in heads_seq(m - 1):
                        square_out(s)
            act.wait_ge(S["head_sum"], 1)
            nc.scalar.activation(st[:, 6, 0:48], st[:, 6, 0:48], ACT.Sqrt).then_inc(S["head_sqrt"], 1)
            for k in range(KT):
                act.wait_ge(S["o_turned"], k // 2 + 1)
                nc.scalar.activation(oT_h[:, k, :], region(k), ACT.Copy, scale=norms[:, 3 * KT + k:3 * KT + k + 1]
                                     ).then_inc(S["o_high"], 1)

            def stream_high(b0, n):
                with act.Fori(0, n) as b:
                    split_high(b + b0, 2)
                    split_high(b + b0, 3)
                    split_high(b + (b0 + 1), 0)
                    split_high(b + (b0 + 1), 1)

            stream_high(18, 8)
            squares(x, sq2, lambda k: act.wait_ge(S["x2_ready"], k + 1))
            inv_root(2)
            shift_high(2, h2_h, mod[:, 3 * KT:], yb2)
            stream_high(26, 8)
            for k in range(KT // 2):
                act.wait_ge(S["qp_done"], 1)
                nc.scalar.activation(qpT[:, 2 * k:2 * k + 2, :], PS[:, k, :].rearrange("p (a t) -> p a t", a=2),
                                     ACT.Copy).then_inc(S["qp_kept"], 1)
            for k in range(8):
                act.wait_ge(S["sc_done"], k + 1)
                nc.scalar.activation(sc[:, k // 4, 4 * (k % 4):4 * (k % 4) + 4, :],
                                     PS[:, k, :].rearrange("p (a n) -> p a n", a=4), ACT.Copy
                                     ).then_inc(S["sc_kept"], 1)

            def gelu(i, bank):
                act.wait_ge(S["w_free"], 2 * i + (U_U + 2 + SPLIT))
                nc.scalar.activation(A[:, bass.ds(i, 1), :].rearrange("p a t -> p (a t)"), PS[:, bank, 0:T],
                                     ACT.Gelu_apprx_tanh).then_inc(S["gelu_done"], 1)

            def u_tiles(b0, n):
                with act.Fori(b0, b0 + n) as b:
                    split_high(b + 34, 2)
                    split_high(b + 34, 3)
                    gelu(2 * b, 0)
                    split_high(b + 35, 0)
                    split_high(b + 35, 1)
                    gelu(2 * b + 1, 1)

            u_tiles(0, GATES_AT)
            act.wait_ge(S["top_s_ready"], 1)
            nc.scalar.activation(ge[:], tops[:], ACT.Exp).then_inc(S["top_exp"], 1)
            u_tiles(GATES_AT, 30 - GATES_AT)
            act.wait_ge(S["gates_ready"], 1)
            act.wait_ge(S["x2_out"], 16)
            u_tiles(30, 34)

            def p_high(i, s):
                act.wait_ge(S["w_free"], 2 * i + U_V)
                nc.scalar.activation(p_hi[:, s, :], A[:, bass.ds(i, 1), :].rearrange("p a t -> p (a t)"),
                                     ACT.Copy).then_inc(S["p_high"], 1)

            with act.Fori(0, T // 8) as b:
                for s in range(2):
                    act.wait_ge(S["dist_b"], 2 * b + (s + 1))
                    nc.scalar.activation(hotB[:, s], hotB[:, s], ACT.Square).then_inc(S["dist_b2"], 1)
                    act.wait_ge(S["dist_b2"], 2 * b + (s + 1))
                    nc.scalar.activation(hotB[:, s], hotB[:, s], ACT.Relu, scale=-1.0, bias=ones[:, 0:1]
                                         ).then_inc(S["hot_b"], 1)
            act.wait_ge(S["routed"], T // 4 + 2)
            p_high(0, 0)
            p_high(1, 1)
            with act.Fori(0, N_V // 4 - 1) as b:
                split_high(b + 98, 2)
                split_high(b + 98, 3)
                p_high(2 * b + 2, 0)
                split_high(b + 99, 0)
                split_high(b + 99, 1)
                p_high(2 * b + 3, 1)
            split_high(161, 2)
            split_high(161, 3)
            squares(x3, sq3, lambda k: act.wait_ge(S["x3_ready"], k + 1))
            inv_root(3)

        @block.tensor
        def _(pe):
            mm = nc.tensor.matmul

            def used(ins):
                ins.then_inc(S["w_free"], 1)

            pe.sem_inc(S["w_free"], SPLIT)

            def sum_squares(r, s, n0):
                for k in range(KT):
                    pe.wait_ge(S["sq_ready"], n0 + k + 1)
                    ins = mm(PS[:, NORM_BANK[r], 0:T], ones_sq[:], s[:, k, :], start=(k == 0), stop=(k == KT - 1))
                ins.then_inc(S["norm_sum"], 1)

            pe.wait_ge(S["const_ready"], 3)
            sum_squares(0, sq, 0)
            pe.wait_ge(S["silu"], 1)
            for c in range(4):
                if c >= 2:
                    pe.wait_ge(S["ada_row_kept"], c - 1)
                for kt in range(KT):
                    pe.wait_ge(ada_in[kt % ADA], 16 * (4 * c + kt // 4 + 1))
                    for half in range(2):
                        ins = mm(PS[0:2, 2 * (c % 2) + half, :], silu_c[:, kt, :], ada[:, kt % ADA, half * 512:half * 512 + 512],
                                 start=(kt == 0), stop=(kt == KT - 1))
                    ins.then_inc(S["ada1_used"], 1)
            sum_squares(1, sq, KT)
            pe.wait_ge(S["ada_row_kept"], 4)
            pe.wait_ge(S["par_in"], N_SMALL)
            for k in range(32):
                ins = nc.tensor.transpose(PS[:, 4, 2 * k:2 * k + 2], modrow[:, k * P:(k + 1) * P], ident[0:2, 0:2])
            ins.then_inc(S["ada_col"], 1)

            def three(out_, a_h, a_l, w, s, lhs_is_w, start, stop=False, check=False):
                wh, wl = w_hi[:, s, w], w_lo[:, s, w]
                pairs = ((a_h, wh), (a_h, wl), (a_l, wh)) if not lhs_is_w else ((wh, a_h), (wh, a_l), (wl, a_h))
                for q, (l_, r_) in enumerate(pairs):
                    ins = mm(out_, l_, r_, start=(start and q == 0), stop=(stop and q == 2), skip_group_check=check)
                return ins

            def ada_columns(c, bank):
                pe.wait_ge(S["ada_sum"], c + 1)
                for k in range(8):
                    ins = mm(PS[:, bank, k:k + 1], acc[:, c % 2, k * P:(k + 1) * P], ones[:], start=True, stop=True)
                ins.then_inc(S["ada_col"], 1)

            def turn_keys():
                pe.wait_ge(S["evac_a"], EVAC_A[5])
                pe.wait_ge(S["evac_d"], EVAC_DK)
                for k in range(10):
                    if k >= 4:
                        pe.wait_ge(S["turn_k_kept"], k - 3)
                    for t in range(NTOK):
                        ins = nc.tensor.transpose(PS[:, k % 4, t * P:(t + 1) * P], Kt[:, t, k * P:(k + 1) * P], ident[:])
                    ins.then_inc(S["turn_k"], 1)

            def turn_queries(c):
                pe.wait_ge(S["evac_d"], EVAC_DQ[c])
                if c == 0:
                    pe.wait_ge(S["turn_k_kept"], 10)
                if c >= 2:
                    pe.wait_ge(S["turn_q_kept"], 2 * (c - 1))
                for a in range(2):
                    for k in range(2):
                        for t in range(QT):
                            blk = 2 * a + k
                            ins = nc.tensor.transpose(PS[:, TURN_Q_BANK[c] + a, k * T + t * P:k * T + (t + 1) * P],
                                                      Qt[:, c % 2, t, blk * P:(blk + 1) * P], ident[:])
                    ins.then_inc(S["turn_q"], 1)

            for c in range(9):
                kind, banks = CHUNKS[c], BANKS[c]
                if c >= 2:
                    prev = 3 if c == 6 else c - 2
                    pe.wait_ge(S["evac_a"], EVAC_A[prev + 1])
                    pe.wait_ge(S["evac_d"], EVAC_DC[prev + 1])
                if c in ADA_AT:
                    ada_columns(c - 1, ADA_AT[c])
                    pe.wait_ge(S["ada_col_kept"], c)
                for u_ in range(8):
                    n = 8 * c + u_
                    if c == 0:
                        pe.wait_ge(S["norm_l"], 2 * u_ + 2)
                    pe.wait_ge(S["w_low"], n + 1)
                    for r in range(2):
                        k = 2 * u_ + r
                        for t in range(len(banks)):
                            tok = t if kind != "q" else t + QT
                            if c == 0 and tok == QT and r == 0:
                                pe.wait_ge(S["norm_l"], KT + 2 * u_ + 2)
                            h_, l_ = (hc_h, hc_l) if tok < QT else (hl_h, hl_l)
                            cols = slice((tok % QT) * P, (tok % QT + 1) * P)
                            ins = three(PS[:, banks[t], :], h_[:, k, cols], l_[:, k, cols],
                                        slice(r * 512, r * 512 + 512), n % SPLIT, False, k == 0, k == KT - 1)
                    used(ins)
                if c == 5:
                    turn_keys()
                if c >= 6:
                    turn_queries(c - 6)
            turn_queries(3)

            def score(n):
                m, qt, sub = n // 4, n // 2 % 2, n % 2
                if n >= 4:
                    pe.wait_ge(S["exp_done"], exps_after(n - 4))
                q = (qTd if m < 8 else qTs)[sub * DH:(sub + 1) * DH, m % 8, qt * P:(qt + 1) * P]
                k = m if m < 8 else 8 + (m - 8) // 4
                mm(PS[:, n % 4, :], q, kT[sub * DH:(sub + 1) * DH, k, :], start=True, stop=True
                   ).then_inc(S["scored"], 1)

            def turn_probs(s):
                m, slot = turned_tile(s)
                if s < 16:
                    pe.wait_ge(S["combined"], s + 1)
                else:
                    pe.wait_ge(S["exp_done"], exps_after(4 * m + slot))
                if s >= 2:
                    pe.wait_ge(S["turned_kept"], s - 1)
                for k in range(NTOK):
                    ins = nc.tensor.transpose(PS[:, 4 + s % 2, k * P:(k + 1) * P], pr[:, m % 2, slot, k * P:(k + 1) * P],
                                              ident[:])
                ins.then_inc(S["turned"], 1)

            def weigh_values(s):
                m, slot = turned_tile(s)
                pe.wait_ge(S["turned_kept"], s + 1)
                if s >= 2:
                    pe.wait_ge(S["o_stored"], s - 1)
                if s < 16:
                    cols, w = slice(m * P, (m + 1) * P), P
                else:
                    kv = 2 * ((m - 8) // 4) + slot % 2
                    cols, w = slice(1024 + kv * DH, 1024 + (kv + 1) * DH), DH
                for k in range(NTOK):
                    ins = mm(PS[:, 6 + s % 2, 0:w], pT[:, s % 4, k, :], V[:, k, cols], start=(k == 0), stop=(k == NTOK - 1))
                ins.then_inc(S["pv_done"], 1)

            pe.wait_ge(S["turn_q_kept"], 8)
            for m in range(17):
                if m < 16:
                    for n in range(4 * m, 4 * m + 4):
                        score(n)
                if m >= 1:
                    seq = heads_seq(m - 1)
                    turn_probs(seq[0])
                    for a, s in enumerate(seq):
                        if a + 1 < len(seq):
                            turn_probs(seq[a + 1])
                        weigh_values(s)
            for k in range(KT):
                pe.wait_ge(S["head_scaled"], 1 if k < 8 else 2)
                for t in range(QT):
                    ins = nc.tensor.transpose(PS[:, k // 2, (k % 2) * T + t * P:(k % 2) * T + (t + 1) * P],
                                              O[:, t, k * P:(k + 1) * P], ident[:])
                if k % 2:
                    ins.then_inc(S["o_turned"], 1)

            pe.wait_ge(S["const_ready"], 4)

            def open_banks(ready):
                for k in range(8):
                    ready(k)
                    mm(PS[:, k, :], zeros[:, 0:P], zeros[:], start=True, stop=False)

            def close_banks():
                for k in range(8):
                    ins = mm(PS[:, k, :], zeros[:, 0:P], zeros[:], start=False, stop=True)
                return ins

            def project(b0, a_h, a_l, n):
                with pe.Fori(0, n) as b:
                    for j in range(4):
                        pe.wait_ge(S["w_low"], 4 * b + (4 * b0 + j + 1))
                        k = 2 * b + j // 2
                        for q in range(8):
                            ins = three(region(8 * (j % 2) + q), a_h[:, bass.ds(k, 1), :].rearrange("p a t -> p (a t)"),
                                        a_l[:, bass.ds(k, 1), :].rearrange("p a t -> p (a t)"),
                                        slice(q * P, (q + 1) * P), j % SPLIT, True, False, check=True)
                        used(ins)

            def head_rows_out(k):
                pe.wait_ge(S["o_high"], 2 * k + 2)
                pe.wait_ge(S["o_low"], 2 * k + 2)

            open_banks(head_rows_out)
            project(18, oT_h, oT_l, 8)
            close_banks().then_inc(S["attn_out"], 1)
            pe.wait_ge(S["x2_ready"], 2)
            sum_squares(2, sq2, 2 * KT)
            ada_cols = ((5, 1), (6, 2))
            for c, bank in ada_cols:
                pe.wait_ge(S["x2_ready"], 2 * bank + 2)
                ada_columns(c, bank)

            def norm_out(k):
                pe.wait_ge(S["x2_ready"], 2 * k + 2)
                if k == 0:
                    pe.wait_ge(S["norm_sqrt"], 3)
                if k in (1, 2):
                    pe.wait_ge(S["ada_col_kept"], 5 + k)

            open_banks(norm_out)
            pe.wait_ge(S["norm_l"], 3 * KT)
            project(26, h2_h, h2_l, 8)
            close_banks().then_inc(S["qp_done"], 1)
            pe.wait_ge(S["keys_in"], 16)
            for t in range(QT):
                for k in range(KT):
                    n = t * 4 + k // 4
                    if k % 4 == 0:
                        pe.wait_ge(S["qp_kept"], 8)
                    ins = mm(PS[:, n, (k % 4) * P:(k % 4 + 1) * P], qpT[:, k, t * P:(t + 1) * P], skT[:, k, :],
                             start=True, stop=True)
                    if k % 4 == 3:
                        ins.then_inc(S["sc_done"], 1)
            pe.wait_ge(S["sc_kept"], 8)
            ada_columns(7, 7)

            def first_product(b0, n):
                with pe.Fori(b0, b0 + n) as b:
                    for j in range(4):
                        i = j // 2
                        pe.wait_ge(S["w_low"], 4 * b + (U_U + j + 1))
                        if j % 2 == 0:
                            pe.wait_ge(S["gelu_done"], 2 * b + (i + 1))
                        for q in range(8):
                            k = 8 * (j % 2) + q
                            ins = three(PS[:, i, 0:T], h2_h[:, k, :], h2_l[:, k, :], slice(q * P, (q + 1) * P),
                                        j % SPLIT, True, k == 0, k == KT - 1)
                        used(ins)

            pe.sem_inc(S["gelu_done"], 2)
            first_product(0, 48)
            pe.wait_ge(S["gates_ready"], 1)
            for t in range(QT):
                for q in range(3):
                    ins = nc.tensor.transpose(PS[:, 2 + t, q * P:(q + 1) * P], sel[:, t, q, :], ident[:])
            ins.then_inc(S["gates_turned"], 1)
            first_product(48, 16)

            pe.sem_inc(S["routed"], 2)
            with pe.Fori(0, T // 8) as b:
                for s in range(2):
                    pe.wait_ge(S["hot_a"], 2 * b + (s + 1))
                    pe.wait_ge(S["hot_b"], 2 * b + (s + 1))
                    pe.wait_ge(S["routed"], 2 * b + (s + 1))
                    for q in range(4):
                        ins = mm(PS[:, 4 + s, q * P:(q + 1) * P], hotB[:, s, q, :], hotA[:, s, q, :],
                                 start=True, stop=True)
                    ins.then_inc(S["route_used"], 1)

            open_banks(lambda k: pe.wait_ge(S["routed"], T // 4 + 2))
            with pe.Fori(0, N_V // 4) as b:
                for j in range(4):
                    i = j // 2
                    pe.wait_ge(S["w_low"], 4 * b + (U_V + j + 1))
                    if j % 2 == 0:
                        pe.wait_ge(S["p_low"], 2 * b + (i + 1))
                    for q in range(8):
                        ins = three(region(8 * (j % 2) + q), p_hi[:, i, :], p_lo[:, i, :], slice(q * P, (q + 1) * P),
                                    j % SPLIT, True, False, check=True)
                    used(ins)
            close_banks().then_inc(S["v_done"], 1)
            pe.wait_ge(S["x3_ready"], 2)
            sum_squares(3, sq3, 3 * KT)

        @block.vector
        def _(dve):
            V_ = nc.vector
            chain = {"n": 0}

            def link(ins):
                ins.then_inc(S["dve"], 1)
                chain["n"] += 1
                dve.wait_ge(S["dve"], chain["n"])

            def split_low(b, j):
                dve.wait_ge(S["w_high"], 4 * b + (j + 1))
                dve.wait_ge(S["w_free"], 4 * b + (j + 1))
                V_.tensor_tensor(w_lo[:, j % SPLIT, :], raw[:, j, :], w_hi[:, j % SPLIT, :].bitcast(F32),
                                 ALU.subtract).then_inc(S["w_low"], 1)

            def ada_add(c, kt, last):
                n = 16 * c + kt
                dve.wait_ge(ada_in[kt % ADA], 16 * (16 + n // 4 + 1))
                if kt == 0:
                    dve.wait_ge(S["ada_zeroed"], c + 1)
                else:
                    dve.wait_ge(S["ada2_used"], n)
                ins = V_.scalar_tensor_tensor(acc[:, c % 2, :], ada[:, kt % ADA, :], silu_c[:, kt, 0:1],
                                              acc[:, c % 2, :], ALU.mult, ALU.add)
                ins.then_inc(S["ada2_used"], 1)
                if last:
                    dve.wait_ge(S["ada2_used"], n + 1)
                    dve.sem_inc(S["ada_sum"], 1)

            def norm_inverse(r):
                dve.wait_ge(S["norm_sqrt"], r + 1)
                link(V_.reciprocal(rstd[:], rstd[:]))

            def scale_and_low(r, xin, scale, shift, out_h, out_l, yb_):
                def low(k):
                    dve.wait_ge(S["norm_h"], KT * r + k + 1)
                    V_.scalar_tensor_tensor(out_l[:, k, :], yb_[:, k % 4, :], shift[:, k:k + 1],
                                            out_h[:, k, :].bitcast(F32), ALU.add, ALU.subtract
                                            ).then_inc(S["norm_l"], 1)
                for k in range(KT):
                    if k >= 4:
                        dve.wait_ge(S["norm_l"], KT * r + k - 3)
                    elif r == 1:
                        dve.wait_ge(S["norm_l"], KT * r)
                    V_.scalar_tensor_tensor(yb_[:, k % 4, :], xin[:, k, :], scale[:, k:k + 1], rstd[:],
                                            ALU.mult, ALU.mult).then_inc(S["norm_y"], 1)
                    if k >= 2:
                        low(k - 2)
                low(KT - 2)
                low(KT - 1)

            dve.wait_ge(S["par_in"], N_SMALL)
            link(V_.tensor_tensor(lam_v[:, 0, :], lam_v[:, 0, :], lam_v[:, 1, :], ALU.mult))
            link(V_.tensor_tensor(lam_v[:, 2, :], lam_v[:, 2, :], lam_v[:, 3, :], ALU.mult))
            link(V_.reduce_sum(lam[:, 0:1], lam_v[:, 0, :], AX))
            V_.reduce_sum(lam[:, 1:2], lam_v[:, 2, :], AX).then_inc(S["lam_ready"], 1)
            link(V_.tensor_scalar(nsink[:, 1, :], nsink[:, 0, :], -1.0, None, ALU.mult))
            link(V_.tensor_scalar(norms[:, 3 * KT:3 * KT + 8], norms[:, 3 * KT:3 * KT + 8], 1.0 - LAM_INIT, None,
                                  ALU.mult))
            dve.wait_ge(S["silu"], 1)
            norm_inverse(0)
            dve.wait_ge(S["ada_col"], 1)
            cols = PS[:, 4, 0:64].rearrange("p (k c) -> p k c", c=2)
            link(V_.tensor_tensor(mod[:, 0:32], cols[:, :, 0], b_ada[:, 0:32], ALU.add))
            link(V_.tensor_tensor(modc[:], cols[:, :, 1], b_ada[:, 0:32], ALU.add))
            link(V_.scalar_tensor_tensor(scl[:, 0:KT], mod[:, KT:2 * KT], 1.0, norms[:, 0:KT], ALU.add, ALU.mult))
            link(V_.scalar_tensor_tensor(scl[:, KT:2 * KT], modc[:, KT:2 * KT], 1.0, norms[:, 0:KT], ALU.add, ALU.mult))
            split_low(0, 0)
            split_low(0, 1)
            scale_and_low(0, x_c, scl[:, KT:2 * KT], modc, hc_h, hc_l, yb)
            norm_inverse(1)
            scale_and_low(1, x, scl[:, 0:KT], mod, hl_h, hl_l, yb)

            def rope(dst, src, q, n):
                hv = src.rearrange("p (h d) -> p h d", d=DH)
                t0 = rt[:, 0, 0:n]
                t1 = rt[:, 1, 0:n]
                cosb = cs[:, 0, q, :].unsqueeze(1).broadcast_to([P, n // DH, DH])
                V_.tensor_tensor(t0.rearrange("p (h d) -> p h d", d=DH), hv, cosb, ALU.mult)
                s4 = src.rearrange("p (h s d) -> p h s d", s=2, d=ROPE_PAIRS)
                d4 = t1.rearrange("p (h s d) -> p h s d", s=2, d=ROPE_PAIRS)
                sn = cs[:, 1, q, :].rearrange("p (a s d) -> p a s d", s=2, d=ROPE_PAIRS)
                for s in range(2):
                    for a in range(2):
                        sv = s4.rearrange("p (h a) s d -> p h a s d", a=2)[:, :, a, 1 - s, :]
                        dv = d4.rearrange("p (h a) s d -> p h a s d", a=2)[:, :, a, s, :]
                        ins = V_.tensor_tensor(dv, sv, sn[:, a, s, :].unsqueeze(1).broadcast_to([P, n // DH, ROPE_PAIRS]),
                                               ALU.mult)
                link(ins)
                link(V_.tensor_tensor(dst, t0, t1, ALU.add))
                dve.sem_inc(S["evac_d"], 1)

            def evac(c):
                kind, banks = CHUNKS[c], BANKS[c]
                dve.wait_ge(S["w_free"], 8 * (c + 1) + SPLIT)
                if kind == "k":
                    for q in range(QT):
                        rope(Kt[:, QT + q, c * 512:c * 512 + 512], PS[:, banks[QT + q], :], q, 512)
                if kind == "kv":
                    dve.wait_ge(S["evac_a"], EVAC_A[c + 1])
                    for q in range(QT):
                        rope(Kt[:, QT + q, 1024:1280], PS[:, banks[QT + q], 0:256], q, 256)
                if kind == "q":
                    if c - 5 >= 2:
                        dve.wait_ge(S["turn_q"], 2 * (c - 5 - 1))
                    for q in range(QT):
                        rope(Qt[:, (c - 5) % 2, q, :], PS[:, banks[q], :], q, 512)

            def ada_keep(c, bank):
                dve.wait_ge(S["ada_col"], c + 2)
                V_.tensor_tensor(mod[:, 32 + 8 * c:40 + 8 * c], PS[:, bank, 0:8], b_ada[:, 32 + 8 * c:40 + 8 * c],
                                 ALU.add).then_inc(S["ada_col_kept"], 1)

            for c in range(9):
                n_ada = 0
                for b in (2 * c, 2 * c + 1):
                    for j in range(RAW):
                        if b or j > 1:
                            split_low(b, j)
                        if c < 5:
                            for _ in range(2):
                                ada_add(c, n_ada, n_ada == 15)
                                n_ada += 1
                        elif j % 2 == 1:
                            kt = 4 * (c - 5) + (b % 2) * 2 + j // 2
                            ada_add(5, kt, kt == 15)
                        if c and b == 2 * c and j == 1:
                            if c in ADA_AT:
                                ada_keep(c - 1, ADA_AT[c])
                            evac(c - 1)
            split_low(18, 0)
            split_low(18, 1)
            evac(8)

            dve.wait_ge(S["lam_exp"], 1)
            link(V_.scalar_tensor_tensor(lam[:, 4:5], lam[:, 3:4], -LAM_INIT, lam[:, 2:3], ALU.add, ALU.subtract))

            def stats(n):
                m, qt, slot = n // 4, n // 2 % 2, n % 4
                dve.wait_ge(S["scored"], n + 1)
                if m >= 8:
                    keys = slice(T + P, T + 2 * P) if qt == 0 else slice(T, T + P)
                    link(V_.tensor_tensor(PS[:, slot, keys], PS[:, slot, keys], mask[:, qt, :], ALU.add))
                link(V_.reduce_max(st[:, 0, n:n + 1], PS[:, slot, :], AX))
                if m < 8:
                    V_.tensor_scalar(st[:, 1, n:n + 1], st[:, 0, n:n + 1], -SCALE, None, ALU.mult).then_inc(S["biased"], 1)
                else:
                    h = swa_head(m, n % 2)
                    V_.tensor_scalar(st[:, 1, n:n + 1], st[:, 0, n:n + 1], -SCALE, nsink[:, 1, h:h + 1],
                                     ALU.mult, ALU.min).then_inc(S["biased"], 1)

            def combine(s):
                m, slot = turned_tile(s)
                n = 4 * m + slot
                if s < 16:
                    dve.wait_ge(S["exp_done"], exps_after(n + 1))
                    link(V_.reciprocal(st[:, 4, n:n + 2], st[:, 2, n:n + 2]))
                    link(V_.tensor_scalar(st[:, 4, n + 1:n + 2], st[:, 4, n + 1:n + 2], lam[:, 4:5], None, ALU.mult))
                    link(V_.tensor_scalar(pr[:, m % 2, slot, :], pr[:, m % 2, slot, :], st[:, 4, n:n + 1], None, ALU.mult))
                    V_.scalar_tensor_tensor(pr[:, m % 2, slot, :], pr[:, m % 2, slot + 1, :], st[:, 4, n + 1:n + 2],
                                            pr[:, m % 2, slot, :], ALU.mult, ALU.add).then_inc(S["combined"], 1)
                else:
                    dve.wait_ge(S["exp_done"], exps_after(n))
                    link(V_.tensor_tensor(st[:, 4, n:n + 1], st[:, 2, n:n + 1], st[:, 3, n:n + 1], ALU.add))
                    V_.reciprocal(st[:, 4, n:n + 1], st[:, 4, n:n + 1]).then_inc(S["combined"], 1)

            def store_out(s):
                m, slot = turned_tile(s)
                n, qt = 4 * m + slot, slot // 2
                dve.wait_ge(S["pv_done"], s + 1)
                if s < 16:
                    V_.tensor_copy(O[:, qt, m * P:(m + 1) * P], PS[:, 6 + s % 2, 0:P]).then_inc(S["o_stored"], 1)
                else:
                    h = swa_head(m, slot % 2)
                    dve.wait_ge(S["combined"], s + 1)
                    V_.tensor_scalar(O[:, qt, 1024 + h * DH:1024 + (h + 1) * DH], PS[:, 6 + s % 2, 0:DH],
                                     st[:, 4, n:n + 1], None, ALU.mult).then_inc(S["o_stored"], 1)

            for m in range(17):
                if m < 16:
                    for n in range(4 * m, 4 * m + 4):
                        stats(n)
                    for s in heads_seq(m):
                        combine(s)
                if m >= 1:
                    for s in heads_seq(m - 1):
                        store_out(s)
            dve.wait_ge(S["o_squared"], 48)
            link(V_.tensor_scalar(st[:, 6, 0:16], st[:, 6, 0:16], 1.0 / P, EPS, ALU.mult, ALU.add))
            link(V_.tensor_scalar(st[:, 6, 16:48], st[:, 6, 16:48], 1.0 / DH, EPS, ALU.mult, ALU.add))
            dve.sem_inc(S["head_sum"], 1)
            dve.wait_ge(S["head_sqrt"], 1)
            link(V_.reciprocal(st[:, 7, 0:48], st[:, 6, 0:48]))
            dve.wait_ge(S["o_stored"], 48)
            for part in range(2):
                for t in range(QT):
                    if part == 0:
                        ov = O[:, t, 0:1024].rearrange("p (h d) -> p h d", d=P)
                        rs = st[:, 7, 0:16].rearrange("p (h t) -> p h t", t=2)[:, :, t].unsqueeze(2).broadcast_to([P, 8, P])
                        link(V_.tensor_tensor(ov, ov, rs, ALU.mult))
                    else:
                        for g in range(2):
                            for sub in range(2):
                                h0 = 8 * g + 4 * sub
                                ov = O[:, t, 1024 + h0 * DH:1024 + (h0 + 4) * DH].rearrange("p (h d) -> p h d", d=DH)
                                rs = st[:, 7, 16:48].rearrange("p (m t s) -> p m t s", t=2, s=2)[
                                    :, 4 * g:4 * g + 4, t, sub].unsqueeze(2).broadcast_to([P, 4, DH])
                                link(V_.tensor_tensor(ov, ov, rs, ALU.mult))
                dve.sem_inc(S["head_scaled"], 1)
            for k in range(KT):
                dve.wait_ge(S["o_high"], 2 * (k // 2) + 2)
                V_.scalar_tensor_tensor(oT_l[:, k, :], region(k), norms[:, 3 * KT + k:3 * KT + k + 1],
                                        oT_h[:, k, :].bitcast(F32), ALU.mult, ALU.subtract).then_inc(S["o_low"], 1)

            def stream_low(b0, n_turns, c):
                dve.wait_ge(S["ada_zeroed"], c + 1)
                with dve.Fori(0, n_turns) as b:
                    for q in range(4):
                        dve.wait_ge(ada_in[q], 16 * b + 16 * (16 + 4 * c + 1))
                        dve.wait_ge(S["ada2_used"], 4 * b + (16 * c + q))
                        V_.scalar_tensor_tensor(acc[:, c % 2, :], ada[:, q, :],
                                                silu_c[:, bass.ds(4 * b + q, 1), 0:1].rearrange("p a c -> p (a c)"),
                                                acc[:, c % 2, :], ALU.mult, ALU.add).then_inc(S["ada2_used"], 1)
                        for j in ((2, 3), (4, 5))[q % 2]:
                            split_low(2 * b + (b0 + q // 2 + j // RAW), j % RAW)
                dve.wait_ge(S["ada2_used"], 16 * c + 16)
                dve.sem_inc(S["ada_sum"], 1)

            stream_low(18, 4, 6)
            dve.wait_ge(S["attn_out"], 1)
            for k in range(KT):
                V_.scalar_tensor_tensor(x[:, k, :], region(k), mod[:, 32 + k:33 + k], x[:, k, :],
                                        ALU.mult, ALU.add).then_inc(S["x2_ready"], 1)
            ada_keep(5, 1)
            ada_keep(6, 2)
            dve.wait_ge(S["ada_col_kept"], 7)
            link(V_.scalar_tensor_tensor(scl[:, 2 * KT:3 * KT], mod[:, 4 * KT:5 * KT], 1.0, norms[:, KT:2 * KT],
                                         ALU.add, ALU.mult))
            norm_inverse(2)
            scale_and_low(2, x, scl[:, 2 * KT:3 * KT], mod[:, 3 * KT:4 * KT], h2_h, h2_l, yb2)
            stream_low(26, 4, 7)

            ada_keep(7, 7)

            def top16(vals, idx, src, tmp):
                link(V_.max(vals[:, 0:8], src))
                V_.max_index(idx[:, 0:8], vals[:, 0:8], src)
                link(V_.match_replace(tmp, vals[:, 0:8], src, LOWEST))
                link(V_.max(vals[:, 8:16], tmp))
                link(V_.max_index(idx[:, 8:16], vals[:, 8:16], tmp))

            unit = [U_U + 2]

            def next_low():
                n = unit[0]
                split_low(n // 4, n % 4)
                unit[0] += 1

            dve.wait_ge(S["sc_kept"], 8)
            for t in range(QT):
                for k in range(KT):
                    top16(v16[:, k, :], ix16[:, k, :], sc[:, t, k, :], sc2[:])
                    next_low()
                link(V_.tensor_copy(if16[:], ix16[:]))
                for h in range(HEADS):
                    link(V_.tensor_tensor(cand[:, h, :].rearrange("p (a b) -> p a b", b=TOPK),
                                          v16[:, 2 * h, :].unsqueeze(2).broadcast_to([P, TOPK, TOPK]),
                                          v16[:, 2 * h + 1, :].unsqueeze(1).broadcast_to([P, TOPK, TOPK]), ALU.add))
                    top16(tops[:, t, h, :], pos[:, h, :], cand[:, h, :], cand2[:])
                    next_low()
                pf = pos[:].rearrange("p h k -> p (h k)")
                V_.tensor_scalar(pab[:, 0, :], pf, 4, None, ALU.logical_shift_right)
                link(V_.tensor_scalar(pab[:, 1, :], pf, 15, None, ALU.bitwise_and))
                link(V_.tensor_copy(pabf[:], pab[:]))
                for half in range(2):
                    link(V_.tensor_tensor(hit[:], pabf[:, half, :].unsqueeze(2).broadcast_to([P, P, 16]),
                                          iota16[:].unsqueeze(1).broadcast_to([P, P, 16]), ALU.is_equal))
                    next_low()
                    hv = hit[:].rearrange("p (h k) a -> p h k a", h=HEADS)
                    iv = if16[:].rearrange("p (h c) a -> p h c a", c=2)[:, :, half, :].unsqueeze(2).broadcast_to(
                        [P, HEADS, TOPK, 16])
                    link(V_.tensor_tensor(hv, hv, iv, ALU.mult))
                    next_low()
                    link(V_.reduce_sum(sel[:, t, half, :], hit[:], AX))
                    next_low()
            for t in range(QT):
                link(V_.tensor_copy(gs[:, t, 0, :], tops[:, t, :, 0]))
                link(V_.tensor_tensor(tops[:, t], tops[:, t], gs[:, t, 0, :].unsqueeze(2).broadcast_to([P, HEADS, TOPK]),
                                      ALU.subtract))
            dve.sem_inc(S["top_s_ready"], 1)
            while unit[0] < U_U + 2 + 4 * GATES_AT + 4:
                next_low()
            dve.wait_ge(S["top_exp"], 1)
            for t in range(QT):
                link(V_.reduce_sum(gs[:, t, 1, :], ge[:, t], AX))
                link(V_.reciprocal(gs[:, t, 1, :], gs[:, t, 1, :]))
                link(V_.tensor_tensor(sel[:, t, 2, :].rearrange("p (h k) -> p h k", h=HEADS), ge[:, t],
                                      gs[:, t, 1, :].unsqueeze(2).broadcast_to([P, HEADS, TOPK]), ALU.mult))
            dve.sem_inc(S["gates_ready"], 1)

            def low_turns(b0, n):
                with dve.Fori(b0, b0 + n) as b:
                    split_low(b, 2)
                    split_low(b, 3)
                    split_low(b + 1, 0)
                    split_low(b + 1, 1)

            while unit[0] < U_U + 2 + 4 * 24:
                next_low()
            low_turns(34 + 24, 24)
            dve.wait_ge(S["gates_turned"], 1)
            for t in range(QT):
                for q, dst in enumerate((i1T, i2T, gT)):
                    V_.tensor_copy(dst[:, t * P:(t + 1) * P], PS[:, 2 + t, q * P:(q + 1) * P]).then_inc(S["gates_kept"], 1)
            low_turns(34 + 48, 16)
            dve.wait_ge(S["gates_kept"], 6)
            dve.wait_ge(S["w_free"], U_V + SPLIT)
            dve.wait_ge(S["gelu_done"], NE_TILES + 2)

            def hot_a(t0, s):
                for q in range(4):
                    ins = V_.tensor_scalar(hotA[:, s, q, :], iota[:], i1T[:, bass.ds(t0 + q, 1)], gT[:, bass.ds(t0 + q, 1)],
                                           ALU.is_equal, ALU.mult)
                ins.then_inc(S["hot_a"], 1)

            def route(t0, s, n):
                dve.wait_ge(S["route_used"], n)
                av = A[:, :, bass.ds(t0, 4)].rearrange("p i t -> p t i")
                V_.tensor_tensor(av, av, PS[:, 4 + s, :].rearrange("p (t i) -> p t i", t=4), ALU.mult
                                 ).then_inc(S["routed"], 1)

            hot_a(0, 0)
            hot_a(4, 1)
            with dve.Fori(0, T // 8 - 1) as b:
                route(8 * b, 0, 2 * b + 1)
                hot_a(8 * b + 8, 0)
                route(8 * b + 4, 1, 2 * b + 2)
                hot_a(8 * b + 12, 1)
            route(T - 8, 0, T // 4 - 1)
            route(T - 4, 1, T // 4)

            def p_low(i, s):
                dve.wait_ge(S["p_high"], i + 1)
                V_.tensor_tensor(p_lo[:, s, :], A[:, bass.ds(i, 1), :].rearrange("p a t -> p (a t)"),
                                 p_hi[:, s, :].bitcast(F32), ALU.subtract).then_inc(S["p_low"], 1)

            dve.wait_ge(S["routed"], T // 4 + 2)
            p_low(0, 0)
            p_low(1, 1)
            with dve.Fori(0, N_V // 4 - 1) as b:
                split_low(b + 98, 2)
                split_low(b + 98, 3)
                p_low(2 * b + 2, 0)
                split_low(b + 99, 0)
                split_low(b + 99, 1)
                p_low(2 * b + 3, 1)
            split_low(161, 2)
            split_low(161, 3)

            dve.wait_ge(S["v_done"], 1)
            dve.wait_ge(S["x2_in"], 16)
            for k in range(KT):
                V_.scalar_tensor_tensor(x3[:, k, :], region(k), mod[:, 5 * KT + k:5 * KT + k + 1], x2[:, k, :],
                                        ALU.mult, ALU.add).then_inc(S["x3_ready"], 1)
            norm_inverse(3)
            for k in range(KT):
                V_.scalar_tensor_tensor(ot[:, k, :], x3[:, k, :], norms[:, 2 * KT + k:2 * KT + k + 1], rstd[:],
                                        ALU.mult, ALU.mult).then_inc(S["tail_y"], 1)


def heads_seq(m):
    return list(range(2 * m, 2 * m + 2)) if m < 8 else list(range(16 + 4 * (m - 8), 20 + 4 * (m - 8)))


def turned_tile(s):
    return (s // 2, 2 * (s % 2)) if s < 16 else (8 + (s - 16) // 4, (s - 16) % 4)


def turned_after(m):
    return heads_seq(m)[-1] + 1


def swa_head(m, sub):
    return 8 * ((m - 8) // 4) + 4 * sub + (m - 8) % 4


def swa_tile(s):
    m, slot = turned_tile(s)
    return 4 * m + slot


def exps_after(n):
    return n + 1 if n < 32 else 32 + 2 * (n - 31)


GATES_AT = 18
NORM_BANK = [5, 6, 0, 0]
TURN_Q_BANK = [0, 2, 0, 2]
EVAC_A = [0]
EVAC_DC = [0]
for _c in CHUNKS:
    EVAC_A.append(EVAC_A[-1] + {"k": 2, "kv": 6, "v": 4, "q": 0}[_c])
    EVAC_DC.append(EVAC_DC[-1] + {"k": 2, "kv": 2, "v": 0, "q": 2}[_c])
EVAC_DK = EVAC_DC[3]
EVAC_DQ = [EVAC_DC[6 + _c] for _c in range(4)]
EVAC_D = EVAC_DC[-1]


def rope_tables():
    pos = np.arange(T, dtype=np.float32)
    row, col = np.floor(pos / GRID_W), pos % GRID_W
    freqs = np.float32(ROPE_THETA) ** (-np.arange(ROPE_PAIRS, dtype=np.float32) / np.float32(ROPE_PAIRS))
    cos, sin = np.zeros((T, DH), np.float32), np.zeros((T, DH), np.float32)
    for a, p in enumerate((row, col)):
        ang = (p[:, None] * freqs).astype(np.float32)
        for s in range(2):
            at = slice(32 * a + 16 * s, 32 * a + 16 * s + 16)
            cos[:, at] = np.cos(ang)
            sin[:, at] = np.sin(ang) * (-1.0 if s == 0 else 1.0)
    return cos, sin


def constants():
    cos, sin = rope_tables()
    tiles = lambda a: np.concatenate([a[q * P:(q + 1) * P] for q in range(QT)], axis=1)
    a = np.arange(P)
    mask = np.concatenate([np.where(a[None, :] > a[:, None], NEG, 0.0), np.where(a[:, None] > a[None, :], NEG, 0.0)], 1)
    row = lambda n: np.tile(np.arange(n, dtype=np.float32), (P, 1))
    return np.ascontiguousarray(np.concatenate([np.eye(P), row(P), row(16), tiles(cos), tiles(sin), mask], 1).astype(np.float32))


def kernel(**inp):
    import concourse.bacc as bacc
    from concourse.bass_utils import run_bass_kernel_spmd as run

    g = {k: np.asarray(a) for k, a in inp.items()}
    col = lambda a: a.reshape(-1, P).T
    feat = lambda a: np.ascontiguousarray(a.reshape(T, KT, P).transpose(2, 1, 0))
    wide = lambda a: np.broadcast_to(a.reshape(1, -1), (P, a.size))
    cc = np.stack([col(g["c"][0]), col(g["c_ctx"])], 2).reshape(P, -1)
    par = np.concatenate([
        cc, col(g["b_ada"][0]), col(g["norm_attn"][0]), col(g["norm_ffn"][0]), col(g["final_norm"]),
        col(np.concatenate([g["diff_norm"][0], g["swa_norm"][0]])), wide(g["swa_sink"][0]),
        wide(g["diff_lambda_q1"][0]), wide(g["diff_lambda_k1"][0]), wide(g["diff_lambda_q2"][0]),
        wide(g["diff_lambda_k2"][0])], 1)
    w = g["w_in"][0]
    dq, dk, dv, sq_, sk_, sv = np.split(w, [1024, 2048, 3072, 4096, 4352], axis=1)
    heads = [8 * (m // 4) + 4 * sub + m % 4 for m in range(8) for sub in range(2)]
    sq_ = np.concatenate([sq_[:, h * DH:(h + 1) * DH] for h in heads], 1)
    w = np.concatenate([dk, sk_, sv, dv, dq, sq_], 1)
    arrays = {
        "x_lat": feat(g["x"][0]), "x_ctx": feat(g["ctx"][0]),
        "par": np.ascontiguousarray(par), "con": constants(),
        "w_ada": np.ascontiguousarray(g["w_ada"][0].reshape(KT, P, 12, UNIT).transpose(2, 0, 1, 3)),
        "w_in": np.ascontiguousarray(w.reshape(8, 2, P, 9, 512).transpose(3, 0, 2, 1, 4)).reshape(N_IN, P, UNIT),
        "w_out": np.ascontiguousarray(g["w_out"][0].reshape(KT, P, 2, UNIT).transpose(0, 2, 1, 3)).reshape(N_OUT, P, UNIT),
        "w_q": np.ascontiguousarray(g["peer_w_q"][0].reshape(KT, P, 2, UNIT).transpose(0, 2, 1, 3)).reshape(N_Q, P, UNIT),
        "sk": np.ascontiguousarray(g["peer_sub_keys"][0].reshape(16, P, P).transpose(2, 0, 1)),
        "u": np.ascontiguousarray(g["peer_u"][0].reshape(NE_TILES, P, 2, 8, P).transpose(0, 2, 4, 3, 1)).reshape(N_U, P, UNIT),
        "v": np.ascontiguousarray(g["peer_v"][0].reshape(NE_TILES, P, 2, UNIT).transpose(0, 2, 1, 3)).reshape(N_V, P, UNIT),
    }
    nc = bacc.Bacc("TRN2", target_bir_lowering=False, num_devices=1)
    args = [nc.dram_tensor(n, a.shape, F32, kind="ExternalInput").ap() for n, a in arrays.items()]
    x2_dram = nc.dram_tensor("x2_scratch", [P, KT, T], F32, kind="Internal").ap()
    out = nc.dram_tensor("outT", [P, KT, T], F32, kind="ExternalOutput").ap()
    block_program(nc, *args, x2_dram, out)
    r = run(nc, [arrays], core_ids=[0])
    o = r.results[0]["outT"]
    return np.ascontiguousarray(o.transpose(2, 1, 0).reshape(1, T, D))
```

```python
from contextlib import ExitStack

import numpy as np
import concourse.bass as bass
from concourse import mybir

F32 = mybir.dt.float32
F32R = mybir.dt.float32r
BF16 = mybir.dt.bfloat16
U32 = mybir.dt.uint32
ALU = mybir.AluOpType
ACT = mybir.ActivationFunctionType
AX = mybir.AxisListType.X

P = 128
D = 2048
KT = D // P
T = 256
QT = T // P
NTOK = 2 * QT
DIFF_HEADS, SWA_HEADS, DH, SWA_KV = 8, 16, 64, 4
GRID_W, ROPE_PAIRS, ROPE_THETA, WINDOW = 64, 16, 10000.0, 128
HEADS, TOPK, NKEYS = 8, 16, 128
NE_TILES = NKEYS
EPS = 1e-6
SCALE = DH ** -0.5
LAM_INIT = 0.2
NEG = -1e30
LOWEST = -3.0e38
UNIT = 1024
HALF = UNIT // 2
RAW, SPLIT, ADA = 4, 4, 4

N_IN, N_OUT, N_Q, N_U, N_V = 72, 32, 32, 256, 256
U_IN, U_OUT = 0, N_IN
U_Q = U_OUT + N_OUT
U_U = U_Q + N_Q
U_V = U_U + N_U
U_END = U_V + N_V

PARAMS = [("cc", KT * 2), ("b_ada", 96), ("norm_attn", KT), ("norm_ffn", KT), ("final_norm", KT),
          ("head_gain", KT), ("sink", SWA_HEADS), ("lam_qk", 4 * DH)]
CONSTS = [("ident", P), ("iota", P), ("iota16", 16), ("cos", QT * DH), ("sin", QT * DH), ("mask", QT * P)]


def offsets(cols):
    at, out = 0, {}
    for name, n in cols:
        out[name] = (at, at + n)
        at += n
    return out, at


PAR, NPAR = offsets(PARAMS)
CON, NCON = offsets(CONSTS)

CHUNKS = ["k", "k", "kv", "v", "v", "q", "q", "q", "q"]
BANKS = [(0, 1, 2, 3), (4, 5, 6, 7), (0, 1, 2, 3), (4, 5, 6, 7), (0, 1, 2, 3), (4, 5), (6, 7), (4, 5), (6, 7)]
ADA_AT = {1: 7, 2: 3, 3: 7, 4: 3, 5: 5}


def block_program(nc, x_lat, x_ctx, par, con, w_ada, w_in, w_out, w_q, sk, u, v, x2_dram, out):
    with ExitStack() as ctx:
        sem_names = ("cc_in par_in x_in xc_in keys_in x2_in x2_out out_done "
                     "silu ada1_used ada2_used ada_row_kept ada_col ada_col_kept ada_zeroed ada_sum "
                     "mod_ready sq_ready norm_sum norm_sqrt norm_y norm_h norm_l norm_t tail_y kt_summed xhat_ready scl_ready sink_in sink_exp "
                     "dve act pool const_ready lam_ready lam_exp "
                     "w_high w_low w_free evac_a evac_d turn_k turn_k_kept turn_q turn_q_kept "
                     "scored biased exp_done combined turned turned_kept pv_done o_stored o_squared "
                     "head_sum head_sqrt head_scaled o_turned o_high o_low "
                     "attn_out x2_ready qp_done qp_kept sc_done sc_kept "
                     "top_s_ready top_exp gates_ready gates_turned gates_kept gelu_done gelu_in tiles_one "
                     "dist_b dist_b2 hot_a hot_b routed route_used p_high p_low v_done x3_ready").split()
        S = {n: ctx.enter_context(nc.semaphore(n)) for n in sem_names}
        raw_in = [ctx.enter_context(nc.semaphore(f"raw_in{i}")) for i in range(RAW)]
        ada_in = [ctx.enter_context(nc.semaphore(f"ada_in{i}")) for i in range(ADA)]

        base = 16512
        KB = 1024
        slab = nc.sbuf_usable_end - base - 64
        names = {}

        def at(name, shape, dt, offset):
            names[name] = offset
            return nc.alloc_sbuf_tensor_at(name, shape, dt, offset=base + offset)

        raw = at("raw", [P, RAW, UNIT], F32, 0)
        w_hi = at("w_hi", [P, SPLIT, HALF], F32R, 16 * KB)
        w_lo = at("w_lo", [P, SPLIT, HALF], F32R, 24 * KB)
        o = 32 * KB
        small = {}
        for name, shape, dt in [("ident", [P, P], F32), ("iota", [P, P], F32), ("iota16", [P, 16], F32),
                                ("b_ada", [P, 96], F32), ("norms", [P, 4 * KT], F32), ("mod", [P, 96], F32),
                                ("modc", [P, 32], F32), ("eps", [P, 1], F32), ("scl", [P, 4 * KT], F32),
                                ("i1T", [P, T], F32), ("i2T", [P, T], F32), ("gT", [P, T], F32),
                                ("rstd", [P, T], F32), ("ones", [P, 1], F32)]:
            small[name] = at(name, shape, dt, o)
            o += 4 * int(np.prod(shape[1:]))
            o = (o + 31) // 32 * 32
        ident, iota, iota16, b_ada, norms, mod, modc, eps, scl, i1T, i2T, gT, rstd, ones = (
            small[n] for n in ("ident iota iota16 b_ada norms mod modc eps scl i1T i2T gT rstd ones").split())
        R = (o + 1023) // 1024 * 1024
        assert base + R + 168 * KB <= nc.sbuf_usable_end, (R, nc.sbuf_usable_end - base - R)

        hc_h = at("hc_h", [P, KT, T], F32R, R)
        hc_l = at("hc_l", [P, KT, T], F32R, R + 16 * KB)
        kT = at("kT", [P, 10, NTOK * P], F32, R)
        qTd = at("qTd", [P, 8, T], F32, R + 20 * KB)
        Kt = at("Kt", [P, NTOK, 1280], F32, R + 32 * KB)
        O = at("O", [P, QT, D], F32, R + 32 * KB)
        V = at("V", [P, NTOK, 1280], F32, R + 52 * KB)
        Qt = at("Qt", [P, 2, QT, 512], F32, R + 72 * KB)
        qTs = at("qTs", [P, 8, T], F32, R + 80 * KB)
        x_c = at("x_c", [P, KT, T], F32, R + 32 * KB)
        sq = at("sq", [P, KT, T], F32, R + 48 * KB)
        modrow = at("modrow", [2, 4096], F32, R + 64 * KB)
        ksum = at("ksum", [P, 2, T], F32, R + 84 * KB)
        yb = at("yb", [P, 4, T], F32, R + 80 * KB)
        ada = at("ada", [P, ADA, UNIT], F32, R + 88 * KB)
        acc = at("acc", [P, 2, UNIT], F32, R + 104 * KB)
        x = at("x", [P, KT, T], F32, R + 112 * KB)
        hl_h = at("hl_h", [P, KT, T], F32R, R + 128 * KB)
        hl_l = at("hl_l", [P, KT, T], F32R, R + 144 * KB)
        pr = at("pr", [P, 2, 4, 512], F32, R + 128 * KB)
        pT = at("pT", [P, 4, 4, P], F32, R + 144 * KB)
        oT_h = at("oT_h", [P, KT, T], F32R, R + 128 * KB)
        oT_l = at("oT_l", [P, KT, T], F32R, R + 144 * KB)
        cs = at("cs", [P, 2, QT, DH], F32, R + 160 * KB)
        mask = at("mask", [P, QT, P], F32, R + 161 * KB)
        rt = at("rt", [P, 2, 512], F32, R + 162 * KB)
        silu_c = at("silu_c", [P, KT, 2], F32, R + 166 * KB)
        lam_v = at("lam_v", [P, 4, DH], F32, R + 166 * KB + 128)
        st = at("st", [P, 8, 64], F32, R + 52 * KB + 20 * KB)
        nsink = at("nsink", [P, 2, SWA_HEADS], F32, R + 167 * KB + 128)
        lam = at("lam", [P, 8], F32, R + 167 * KB + 256)
        zeros = at("zeros", [P, 512], BF16, R + 162 * KB)

        sq2 = at("sq2", [P, KT, T], F32, R + 32 * KB)
        yb2 = at("yb2", [P, 4, T], F32, R + 80 * KB)
        h2_h = at("h2_h", [P, KT, T], F32R, R + 128 * KB)
        h2_l = at("h2_l", [P, KT, T], F32R, R + 144 * KB)
        qpT = at("qpT", [P, KT, T], F32, R)
        skT = at("skT", [P, KT, P], F32, R + 24 * KB)
        sc = at("sc", [P, QT, KT, P], F32, R + 64 * KB)

        A = at("A", [P, NE_TILES, T], F32, R)
        tk = 80 * KB + R
        sc2 = at("sc2", [P, P], F32, tk)
        v16 = at("v16", [P, KT, TOPK], F32, tk + 1 * KB)
        ix16 = at("ix16", [P, KT, TOPK], U32, tk + 2 * KB)
        if16 = at("if16", [P, KT, TOPK], F32, tk + 3 * KB)
        cand = at("cand", [P, HEADS, 256], F32, tk + 4 * KB)
        cand2 = at("cand2", [P, 256], F32, tk + 12 * KB)
        tops = at("tops", [P, QT, HEADS, TOPK], F32, R + 160 * KB)
        pos = at("pos", [P, HEADS, TOPK], U32, tk + 14 * KB)
        pab = at("pab", [P, 2, HEADS * TOPK], U32, tk + 15 * KB)
        pabf = at("pabf", [P, 2, HEADS * TOPK], F32, tk + 16 * KB)
        hit = at("hit", [P, HEADS * TOPK, 16], F32, tk + 17 * KB)
        sel = at("sel", [P, QT, 3, HEADS * TOPK], F32, R + 163 * KB)
        gs = at("gs", [P, QT, 2, HEADS], F32, R + 166 * KB)
        ge = at("ge", [P, QT, HEADS, TOPK], F32, R + 161 * KB)
        hotA = at("hotA", [P, 4, P], F32, R + 160 * KB)
        hotB = at("hotB", [P, 4, P], F32, R + 163 * KB)
        gtmp = at("gtmp", [P, 2, T], F32, R + 165 * KB)
        x2 = at("x2", [P, KT, T], F32, R + 136 * KB)
        p_hi = at("p_hi", [P, 2, T], F32R, R + 152 * KB)
        p_lo = at("p_lo", [P, 2, T], F32R, R + 154 * KB)
        x3 = at("x3", [P, KT, T], F32, R)
        sq3 = at("sq3", [P, KT, T], F32, R + 16 * KB)
        ot = at("ot", [P, KT, T], F32, R + 32 * KB)
        ones_sq = at("ones_sq", [P, P], F32, R + 167 * KB + 512)
        PS = ctx.enter_context(nc.psum_tensor("PS", [P, 8, 512], F32))

        def region(dt):
            return PS[:, dt // 2, (dt % 2) * T:(dt % 2) * T + T]

        parv = {n: par[:, a:b] for n, (a, b) in PAR.items()}
        conv = {n: con[:, a:b] for n, (a, b) in CON.items()}
        SMALL_LOADS = [(silu_c[:], parv["cc"].rearrange("p (k c) -> p k c", c=2)), (b_ada[:], parv["b_ada"]),
                       (norms[:], par[:, PAR["norm_attn"][0]:PAR["head_gain"][1]]),
                       (nsink[:, 0, :], parv["sink"]), (lam_v[:], parv["lam_qk"].rearrange("p (a d) -> p a d", a=4)),
                       (ident[:], conv["ident"]), (iota[:], conv["iota"]), (iota16[:], conv["iota16"]),
                       (cs[:, 0], conv["cos"].rearrange("p (q d) -> p q d", q=QT)),
                       (cs[:, 1], conv["sin"].rearrange("p (q d) -> p q d", q=QT)),
                       (mask[:], conv["mask"].rearrange("p (q d) -> p q d", q=QT))]
        N_SMALL = 16 * (len(SMALL_LOADS) - 1)

        block = ctx.enter_context(nc.Block())

        @block.sync
        def _(sp):
            sp.dma_start(*SMALL_LOADS[0]).then_inc(S["cc_in"], 16)

            def load_ada(n_slot, chunk, kt):
                sp.dma_start(ada[:, n_slot, :], w_ada[chunk, kt]).then_inc(ada_in[n_slot], 16)

            def load_unit(src, slot):
                sp.dma_start(raw[:, slot, :], src).then_inc(raw_in[slot], 16)

            w_ada_flat = w_ada.rearrange("c k p n -> (c k) p n")
            for j in range(ADA):
                sp.dma_start(ada[:, j, :], w_ada_flat[j]).then_inc(ada_in[j], 16)
            sp.dma_start(x_c[:], x_ctx).then_inc(S["xc_in"], 16)
            for dst, src in SMALL_LOADS[1:]:
                sp.dma_start(dst, src).then_inc(S["par_in"], 16)
            sp.dma_start(x[:], x_lat).then_inc(S["x_in"], 16)
            with sp.Fori(1, 16) as b:
                for j in range(ADA):
                    sp.wait_ge(S["ada1_used"], 4 * b + (j - 3))
                    sp.dma_start(ada[:, j, :], w_ada_flat[4 * b + j]).then_inc(ada_in[j], 16)

            def ada2(b, first=False):
                for j in range(ADA):
                    if first:
                        sp.wait_ge(S["ada1_used"], 61 + j)
                    else:
                        sp.wait_ge(S["ada2_used"], 4 * b + (j - 3))
                    sp.dma_start(ada[:, j, :], w_ada_flat[4 * b + 64 + j]).then_inc(ada_in[j], 16)

            def units(src, b, first_unit, first=False):
                for j in range(RAW):
                    if not first:
                        sp.wait_ge(S["w_low"], 8 * b + 2 * (first_unit + j - 3))
                    sp.dma_start(raw[:, j, :], src[4 * b + j]).then_inc(raw_in[j], 16)

            units(w_in, 0, U_IN, first=True)
            ada2(0, first=True)
            ada2(1)
            with sp.Fori(1, 10) as b:
                units(w_in, b, U_IN)
                ada2(2 * b)
                ada2(2 * b + 1)
            with sp.Fori(0, 4) as b:
                ada2(b + 20)
                units(w_in, 2 * b + 10, U_IN)
                units(w_in, 2 * b + 11, U_IN)
            with sp.Fori(0, 4) as b:
                ada2(b + 24)
                units(w_out, 2 * b, U_OUT)
                units(w_out, 2 * b + 1, U_OUT)
            with sp.Fori(0, 4) as b:
                ada2(b + 28)
                units(w_q, 2 * b, U_Q)
                units(w_q, 2 * b + 1, U_Q)
            sp.wait_ge(S["attn_out"], 1)
            sp.dma_start(skT[:], sk).then_inc(S["keys_in"], 16)
            sp.wait_ge(S["x2_ready"], KT)
            sp.dma_start(x2_dram, x[:]).then_inc(S["x2_out"], 16)
            with sp.Fori(0, N_U // 4) as b:
                units(u, b, U_U)
            sp.wait_ge(S["x2_out"], 16)
            sp.wait_ge(S["w_free"], 2 * U_V + SPLIT)
            sp.dma_start(x2[:], x2_dram).then_inc(S["x2_in"], 16)
            with sp.Fori(0, N_V // 4) as b:
                units(v, b, U_V)
            for g in range(4):
                sp.wait_ge(S["tail_y"], 4 * g + 4)
                sp.dma_start(out[:, 4 * g:4 * g + 4, :], ot[:, 4 * g:4 * g + 4, :]).then_inc(S["out_done"], 16)
            sp.wait_ge(S["out_done"], 64)

        @block.gpsimd
        def _(pool):
            nc.gpsimd.memset(eps[:], EPS).then_inc(S["const_ready"], 1)
            nc.gpsimd.memset(ones[:], 1.0).then_inc(S["const_ready"], 1)
            nc.gpsimd.memset(ones_sq[:], 1.0).then_inc(S["const_ready"], 1)
            for c in range(8):
                if c == 7:
                    pool.wait_ge(S["evac_d"], EVAC_D)
                    nc.gpsimd.memset(zeros[:], 0.0).then_inc(S["const_ready"], 1)
                if c >= 2:
                    pool.wait_ge(S["ada_col"], c)
                nc.gpsimd.memset(acc[:, c % 2, :], 0.0).then_inc(S["ada_zeroed"], 1)
            pool.wait_ge(S["top_s_ready"], 1)
            pool.wait_ge(S["x2_out"], 16)
            for i in range(2 * ROUTE_AT, NE_TILES, 8):
                nc.gpsimd.memset(A[:, i:i + 8, :], 1.0).then_inc(S["tiles_one"], 1)
            pool.wait_ge(S["gates_kept"], 6)

            def distance(t0):
                nc.gpsimd.tensor_tensor(hotB[:], iota[:].unsqueeze(1).broadcast_to([P, 4, P]),
                                        i2T[:, bass.ds(t0, 4)].unsqueeze(2).broadcast_to([P, 4, P]),
                                        ALU.subtract).then_inc(S["dist_b"], 1)

            distance(0)
            with pool.Fori(1, T // 4) as g:
                pool.wait_ge(S["route_used"], g)
                distance(4 * g)

        @block.scalar
        def _(act):
            def split_high(b, j):
                act.wait_ge(raw_in[j], 16 * b + 16)
                for hf in range(2):
                    act.wait_ge(S["w_free"], 8 * b + (2 * j + hf + 1))
                    nc.scalar.activation(w_hi[:, (2 * j + hf) % SPLIT, :], raw[:, j, hf * HALF:(hf + 1) * HALF],
                                         ACT.Copy).then_inc(S["w_high"], 1)

            act.wait_ge(S["cc_in"], 16)
            nc.scalar.activation(silu_c[:], silu_c[:], ACT.Silu).then_inc(S["silu"], 1)

            def squares(xin, dst, waits):
                for k in range(KT):
                    waits(k)
                    nc.scalar.activation(dst[:, k, :], xin[:, k, :], ACT.Square).then_inc(S["sq_ready"], 1)

            def inv_root(r):
                act.wait_ge(S["norm_sum"], r + 1)
                nc.scalar.activation(rstd[:], PS[:, NORM_BANK[r], 0:T], ACT.Sqrt, bias=eps[:, 0:1],
                                     scale=1.0 / D).then_inc(S["norm_sqrt"], 1)

            def shift_high(r, out_h, shift, yb_):
                for k in range(KT):
                    act.wait_ge(S["norm_y"], k + 1)
                    nc.scalar.activation(out_h[:, k, :], yb_[:, k % 4, :], ACT.Identity,
                                         bias=shift[:, k:k + 1]).then_inc(S["norm_h"], 1)

            act.wait_ge(S["xc_in"], 16)
            nc.scalar.activation(sq[:], x_c[:], ACT.Square).then_inc(S["sq_ready"], 1)
            act.wait_ge(S["lam_ready"], 1)
            nc.scalar.activation(lam[:, 2:4], lam[:, 0:2], ACT.Exp).then_inc(S["lam_exp"], 1)
            act.wait_ge(S["const_ready"], 3)
            act.wait_ge(S["x_in"], 16)
            act.wait_ge(S["kt_summed"], 1)
            nc.scalar.activation(sq[:], x[:], ACT.Square).then_inc(S["sq_ready"], 1)

            def keep_row(c):
                act.wait_ge(S["ada1_used"], KT * (c + 1))
                nc.scalar.activation(modrow[:, c * UNIT:(c + 1) * UNIT].rearrange("p (a n) -> p a n", a=2),
                                     PS[0:2, 2 * (c % 2):2 * (c % 2) + 2, :], ACT.Copy).then_inc(S["ada_row_kept"], 1)

            inv_root(0)
            keep_row(0)
            act.wait_ge(S["xhat_ready"], 1)
            inv_root(1)
            for c in range(1, 4):
                keep_row(c)
            split_high(0, 0)
            split_high(0, 1)
            act.wait_ge(S["scl_ready"], 1)
            for u_ in range(8):
                for k in (2 * u_, 2 * u_ + 1):
                    for xh, h_, sc_, sh_ in ((x_c, hc_h, scl[:, KT:2 * KT], modc), (sq, hl_h, scl, mod)):
                        nc.scalar.activation(h_[:, k, :], xh[:, k, :], ACT.Identity, scale=sc_[:, k:k + 1],
                                             bias=sh_[:, k:k + 1]).then_inc(S["norm_h"], 1)
                if 1 <= u_ <= 6:
                    split_high((u_ + 1) // 4, (u_ + 1) % 4)

            def evac_copy(dst, src):
                nc.scalar.activation(dst, src, ACT.Copy).then_inc(S["evac_a"], 1)

            def evac(c):
                act.wait_ge(S["w_free"], 16 * (c + 1) + SPLIT)
                kind, banks = CHUNKS[c], BANKS[c]
                for t in range(NTOK if kind != "q" else 0):
                    src = PS[:, banks[t], :]
                    if kind == "k" and t < QT:
                        evac_copy(Kt[:, t, c * 512:c * 512 + 512], src)
                    if kind == "kv":
                        if t < QT:
                            evac_copy(Kt[:, t, 1024:1280], src[:, 0:256])
                        evac_copy(V[:, t, 1024:1280], src[:, 256:512])
                    if kind == "v":
                        evac_copy(V[:, t, (c - 3) * 512:(c - 3) * 512 + 512], src)

            def keep_k(k):
                act.wait_ge(S["turn_k"], k + 1)
                nc.scalar.activation(kT[:, k, :], PS[:, k % 4, :], ACT.Copy).then_inc(S["turn_k_kept"], 1)

            def keep_q(c):
                dst = (qTd, qTs)[c // 2]
                for a in range(2):
                    act.wait_ge(S["turn_q"], 2 * c + a + 1)
                    at_ = 4 * (c % 2) + 2 * a
                    nc.scalar.activation(dst[:, at_:at_ + 2, :],
                                         PS[:, TURN_Q_BANK[c] + a, :].rearrange("p (a t) -> p a t", a=2),
                                         ACT.Copy).then_inc(S["turn_q_kept"], 1)

            for c in range(9):
                for b in (2 * c, 2 * c + 1):
                    for j in range(RAW):
                        if b > 1:
                            split_high(b, j)
                        if c and b == 2 * c and j == 1:
                            evac(c - 1)
                        if c >= 6 and b == 2 * c and j == 1:
                            if c == 6:
                                for k in range(10):
                                    keep_k(k)
                            else:
                                keep_q(c - 7)
            split_high(18, 0)
            split_high(18, 1)
            evac(8)
            keep_q(2)
            keep_q(3)

            def exp_tile(n):
                m, slot = n // 4, n % 4
                act.wait_ge(S["biased"], n + 1)
                if m >= 2 and slot == 0:
                    act.wait_ge(S["turned"], turned_after(m - 2))
                nc.scalar.activation(pr[:, m % 2, slot, :], PS[:, slot, :], ACT.Exp, bias=st[:, 1, n:n + 1],
                                     scale=SCALE, accum_out=st[:, 2, n:n + 1]).then_inc(S["exp_done"], 1)
                if m >= 8 and slot == 3:
                    act.wait_ge(S["sink_in"], m - 7)
                    nc.scalar.activation(st[:, 3, 4 * m:4 * m + 4], st[:, 3, 4 * m:4 * m + 4], ACT.Exp
                                         ).then_inc(S["sink_exp"], 1)

            def keep_turned(s):
                act.wait_ge(S["turned"], s + 1)
                if s >= 4:
                    act.wait_ge(S["pv_done"], s - 3)
                nc.scalar.activation(pT[:, s % 4], PS[:, 4 + s % 2, :].rearrange("p (a q) -> p a q", a=4),
                                     ACT.Copy).then_inc(S["turned_kept"], 1)

            def square_out(s):
                act.wait_ge(S["o_stored"], s + 1)
                m, slot = turned_tile(s)
                if s < 16:
                    cols, w = slice(m * P, (m + 1) * P), P
                else:
                    h = swa_head(m, slot % 2)
                    cols, w = slice(1024 + h * DH, 1024 + (h + 1) * DH), DH
                if s >= 4:
                    act.wait_ge(S["o_squared"], s - 3)
                nc.scalar.activation(rt[:, 1, (s % 4) * P:(s % 4) * P + w], O[:, slot // 2, cols], ACT.Square,
                                     accum_out=st[:, 6, s:s + 1]).then_inc(S["o_squared"], 1)

            for m in range(17):
                seq = heads_seq(m - 1) if m else []
                for a in range(4):
                    if a < len(seq):
                        keep_turned(seq[a])
                    if m < 16:
                        exp_tile(4 * m + a)
                for s in heads_seq(m - 2) if m > 1 else []:
                    square_out(s)
            for s in heads_seq(15):
                square_out(s)
            act.wait_ge(S["head_sum"], 1)
            nc.scalar.activation(st[:, 6, 0:48], st[:, 6, 0:48], ACT.Sqrt).then_inc(S["head_sqrt"], 1)
            for k in range(KT):
                act.wait_ge(S["o_turned"], k // 2 + 1)
                nc.scalar.activation(oT_h[:, k, :], region(k), ACT.Copy, scale=norms[:, 3 * KT + k:3 * KT + k + 1]
                                     ).then_inc(S["o_high"], 1)

            def stream_high(b0, n):
                with act.Fori(0, n) as b:
                    split_high(b + b0, 2)
                    split_high(b + b0, 3)
                    split_high(b + (b0 + 1), 0)
                    split_high(b + (b0 + 1), 1)

            stream_high(18, 8)
            squares(x, sq2, lambda k: act.wait_ge(S["x2_ready"], k + 1))
            inv_root(2)
            shift_high(2, h2_h, mod[:, 3 * KT:], yb2)
            stream_high(26, 8)
            for k in range(KT // 2):
                act.wait_ge(S["qp_done"], 1)
                nc.scalar.activation(qpT[:, 2 * k:2 * k + 2, :], PS[:, k, :].rearrange("p (a t) -> p a t", a=2),
                                     ACT.Copy).then_inc(S["qp_kept"], 1)
            for k in range(8):
                act.wait_ge(S["sc_done"], k + 1)
                nc.scalar.activation(sc[:, k // 4, 4 * (k % 4):4 * (k % 4) + 4, :],
                                     PS[:, k, :].rearrange("p (a n) -> p a n", a=4), ACT.Copy
                                     ).then_inc(S["sc_kept"], 1)

            def gelu(i, bank):
                act.wait_ge(S["w_free"], 4 * i + (2 * U_U + 4 + SPLIT))
                nc.scalar.activation(A[:, bass.ds(i, 1), :].rearrange("p a t -> p (a t)"), PS[:, bank, 0:T],
                                     ACT.Gelu_apprx_tanh).then_inc(S["gelu_done"], 1)

            def gelu_aside(i, bank):
                act.wait_ge(S["w_free"], 4 * i + (2 * U_U + 4 + SPLIT))
                act.wait_ge(S["gelu_in"], i - (2 * ROUTE_AT - 1))
                nc.scalar.activation(gtmp[:, bank, :], PS[:, bank, 0:T], ACT.Gelu_apprx_tanh
                                     ).then_inc(S["gelu_done"], 1)

            def one_hot_b(g):
                act.wait_ge(S["dist_b"], g + 1)
                nc.scalar.activation(hotB[:], hotB[:], ACT.Square).then_inc(S["dist_b2"], 1)
                act.wait_ge(S["dist_b2"], g + 1)
                nc.scalar.activation(hotB[:], hotB[:], ACT.Relu, scale=-1.0, bias=ones[:, 0:1]).then_inc(S["hot_b"], 1)

            def u_tiles(b0, n):
                with act.Fori(b0, b0 + n) as b:
                    split_high(b + 34, 2)
                    split_high(b + 34, 3)
                    gelu(2 * b, 0)
                    split_high(b + 35, 0)
                    split_high(b + 35, 1)
                    gelu(2 * b + 1, 1)

            u_tiles(0, GATES_AT)
            act.wait_ge(S["top_s_ready"], 1)
            nc.scalar.activation(ge[:], tops[:], ACT.Exp).then_inc(S["top_exp"], 1)
            u_tiles(GATES_AT, ROUTE_AT - GATES_AT)
            with act.Fori(ROUTE_AT, 64) as b:
                one_hot_b(2 * b - 2 * ROUTE_AT)
                split_high(b + 34, 2)
                split_high(b + 34, 3)
                gelu_aside(2 * b, 0)
                one_hot_b(2 * b - (2 * ROUTE_AT - 1))
                split_high(b + 35, 0)
                split_high(b + 35, 1)
                gelu_aside(2 * b + 1, 1)

            def p_high(i, s):
                act.wait_ge(S["w_free"], 4 * i + (2 * U_V - 4 + SPLIT))
                nc.scalar.activation(p_hi[:, s, :], A[:, bass.ds(i, 1), :].rearrange("p a t -> p (a t)"),
                                     ACT.Copy).then_inc(S["p_high"], 1)

            act.wait_ge(S["routed"], T // 4 + 2)
            act.wait_ge(S["gelu_in"], NE_TILES - 2 * ROUTE_AT + 2)
            p_high(0, 0)
            p_high(1, 1)
            with act.Fori(0, N_V // 4 - 1) as b:
                split_high(b + 98, 2)
                split_high(b + 98, 3)
                p_high(2 * b + 2, 0)
                split_high(b + 99, 0)
                split_high(b + 99, 1)
                p_high(2 * b + 3, 1)
            split_high(161, 2)
            split_high(161, 3)
            squares(x3, sq3, lambda k: act.wait_ge(S["x3_ready"], k + 1))
            inv_root(3)

        @block.tensor
        def _(pe):
            mm = nc.tensor.matmul

            def used(ins):
                ins.then_inc(S["w_free"], 1)

            pe.sem_inc(S["w_free"], SPLIT)

            def sum_squares(r, s, n0):
                for k in range(KT):
                    pe.wait_ge(S["sq_ready"], n0 + k + 1)
                    ins = mm(PS[:, NORM_BANK[r], 0:T], ones_sq[:], s[:, k, :], start=(k == 0), stop=(k == KT - 1))
                ins.then_inc(S["norm_sum"], 1)

            def sum_partitions(r):
                pe.wait_ge(S["kt_summed"], r + 1)
                mm(PS[:, NORM_BANK[r], 0:T], ones_sq[:], ksum[:, r, :], start=True, stop=True).then_inc(S["norm_sum"], 1)

            pe.wait_ge(S["const_ready"], 3)
            pe.wait_ge(S["silu"], 1)
            for c in range(4):
                if c >= 2:
                    pe.wait_ge(S["ada_row_kept"], c - 1)
                for kt in range(KT):
                    pe.wait_ge(ada_in[kt % ADA], 16 * (4 * c + kt // 4 + 1))
                    for half in range(2):
                        ins = mm(PS[0:2, 2 * (c % 2) + half, :], silu_c[:, kt, :], ada[:, kt % ADA, half * 512:half * 512 + 512],
                                 start=(kt == 0), stop=(kt == KT - 1))
                    ins.then_inc(S["ada1_used"], 1)
                if c < 2:
                    sum_partitions(c)
            pe.wait_ge(S["ada_row_kept"], 4)
            pe.wait_ge(S["par_in"], N_SMALL)
            for k in range(32):
                ins = nc.tensor.transpose(PS[:, 4, 2 * k:2 * k + 2], modrow[:, k * P:(k + 1) * P], ident[0:2, 0:2])
            ins.then_inc(S["ada_col"], 1)

            def three(out_, a_h, a_l, w, s, lhs_is_w, start, stop=False, check=False):
                wh, wl = w_hi[:, s, w], w_lo[:, s, w]
                pairs = ((a_h, wh), (a_h, wl), (a_l, wh)) if not lhs_is_w else ((wh, a_h), (wh, a_l), (wl, a_h))
                for q, (l_, r_) in enumerate(pairs):
                    ins = mm(out_, l_, r_, start=(start and q == 0), stop=(stop and q == 2), skip_group_check=check)
                return ins

            def ada_columns(c, bank):
                pe.wait_ge(S["ada_sum"], c + 1)
                for k in range(8):
                    ins = mm(PS[:, bank, k:k + 1], acc[:, c % 2, k * P:(k + 1) * P], ones[:], start=True, stop=True)
                ins.then_inc(S["ada_col"], 1)

            def turn_keys():
                pe.wait_ge(S["evac_a"], EVAC_A[5])
                pe.wait_ge(S["evac_d"], EVAC_DK)
                for k in range(10):
                    if k >= 4:
                        pe.wait_ge(S["turn_k_kept"], k - 3)
                    for t in range(NTOK):
                        ins = nc.tensor.transpose(PS[:, k % 4, t * P:(t + 1) * P], Kt[:, t, k * P:(k + 1) * P], ident[:])
                    ins.then_inc(S["turn_k"], 1)

            def turn_queries(c):
                pe.wait_ge(S["evac_d"], EVAC_DQ[c])
                if c == 0:
                    pe.wait_ge(S["turn_k_kept"], 10)
                if c >= 2:
                    pe.wait_ge(S["turn_q_kept"], 2 * (c - 1))
                for a in range(2):
                    for k in range(2):
                        for t in range(QT):
                            blk = 2 * a + k
                            ins = nc.tensor.transpose(PS[:, TURN_Q_BANK[c] + a, k * T + t * P:k * T + (t + 1) * P],
                                                      Qt[:, c % 2, t, blk * P:(blk + 1) * P], ident[:])
                    ins.then_inc(S["turn_q"], 1)

            for c in range(9):
                kind, banks = CHUNKS[c], BANKS[c]
                if c >= 2:
                    prev = 3 if c == 6 else c - 2
                    pe.wait_ge(S["evac_a"], EVAC_A[prev + 1])
                    pe.wait_ge(S["evac_d"], EVAC_DC[prev + 1])
                if c in ADA_AT:
                    ada_columns(c - 1, ADA_AT[c])
                    pe.wait_ge(S["ada_col_kept"], c)
                for u_ in range(8):
                    n = 8 * c + u_
                    if c == 0:
                        pe.wait_ge(S["norm_l"], 4 * u_ + 4)
                    for r in range(2):
                        pe.wait_ge(S["w_low"], 2 * n + r + 1)
                        k = 2 * u_ + r
                        for t in range(len(banks)):
                            tok = t if kind != "q" else t + QT
                            h_, l_ = (hc_h, hc_l) if tok < QT else (hl_h, hl_l)
                            cols = slice((tok % QT) * P, (tok % QT + 1) * P)
                            ins = three(PS[:, banks[t], :], h_[:, k, cols], l_[:, k, cols],
                                        slice(0, HALF), (2 * n + r) % SPLIT, False, k == 0, k == KT - 1)
                        used(ins)
                if c == 5:
                    turn_keys()
                if c >= 6:
                    turn_queries(c - 6)
            turn_queries(3)

            def score(n):
                m, qt, sub = n // 4, n // 2 % 2, n % 2
                if n >= 4:
                    pe.wait_ge(S["exp_done"], n - 3)
                q = (qTd if m < 8 else qTs)[sub * DH:(sub + 1) * DH, m % 8, qt * P:(qt + 1) * P]
                k = m if m < 8 else 8 + (m - 8) // 4
                mm(PS[:, n % 4, :], q, kT[sub * DH:(sub + 1) * DH, k, :], start=True, stop=True
                   ).then_inc(S["scored"], 1)

            def turn_probs(s):
                m, slot = turned_tile(s)
                if s < 16:
                    pe.wait_ge(S["combined"], s + 1)
                else:
                    pe.wait_ge(S["exp_done"], 4 * m + slot + 1)
                if s >= 2:
                    pe.wait_ge(S["turned_kept"], s - 1)
                for k in range(NTOK):
                    ins = nc.tensor.transpose(PS[:, 4 + s % 2, k * P:(k + 1) * P], pr[:, m % 2, slot, k * P:(k + 1) * P],
                                              ident[:])
                ins.then_inc(S["turned"], 1)

            def weigh_values(s):
                m, slot = turned_tile(s)
                pe.wait_ge(S["turned_kept"], s + 1)
                if s >= 2:
                    pe.wait_ge(S["o_stored"], s - 1)
                c0 = m * P if s < 16 else 1024 + (m - 8) // 4 * P
                for k in range(NTOK):
                    ins = mm(PS[:, 6 + s % 2, 0:P], pT[:, s % 4, k, :], V[:, k, c0:c0 + P], start=(k == 0),
                             stop=(k == NTOK - 1))
                ins.then_inc(S["pv_done"], 1)

            pe.wait_ge(S["turn_q_kept"], 8)
            late = None
            for m in range(17):
                seq = heads_seq(m - 1) if m else []
                for a in range(4):
                    if m < 16:
                        score(4 * m + a)
                    if late is not None:
                        weigh_values(late)
                        late = None
                    if a < len(seq):
                        turn_probs(seq[a])
                    if 1 <= a <= len(seq):
                        weigh_values(seq[a - 1])
                if len(seq) == 4:
                    late = seq[3]
            weigh_values(late)
            for k in range(KT):
                pe.wait_ge(S["head_scaled"], 1 if k < 8 else 2)
                for t in range(QT):
                    ins = nc.tensor.transpose(PS[:, k // 2, (k % 2) * T + t * P:(k % 2) * T + (t + 1) * P],
                                              O[:, t, k * P:(k + 1) * P], ident[:])
                if k % 2:
                    ins.then_inc(S["o_turned"], 1)

            pe.wait_ge(S["const_ready"], 4)

            def open_banks(ready):
                for k in range(8):
                    ready(k)
                    mm(PS[:, k, :], zeros[:, 0:P], zeros[:], start=True, stop=False)

            def close_banks():
                for k in range(8):
                    ins = mm(PS[:, k, :], zeros[:, 0:P], zeros[:], start=False, stop=True)
                return ins

            def project(b0, a_h, a_l, n, rows=None):
                with pe.Fori(0, n) as b:
                    for h in range(8):
                        k = 2 * b + h // 4
                        if rows is not None and h % 4 == 0:
                            pe.wait_ge(S["norm_l"], 2 * b + (rows + h // 4 + 1))
                        pe.wait_ge(S["w_low"], 8 * b + (8 * b0 + h + 1))
                        for q in range(4):
                            ins = three(region(4 * (h % 4) + q), a_h[:, bass.ds(k, 1), :].rearrange("p a t -> p (a t)"),
                                        a_l[:, bass.ds(k, 1), :].rearrange("p a t -> p (a t)"),
                                        slice(q * P, (q + 1) * P), h % SPLIT, True, False, check=True)
                        used(ins)

            def head_rows_out(k):
                pe.wait_ge(S["o_high"], 2 * k + 2)
                pe.wait_ge(S["o_low"], 2 * k + 2)

            open_banks(head_rows_out)
            project(18, oT_h, oT_l, 8)
            close_banks().then_inc(S["attn_out"], 1)
            pe.wait_ge(S["x2_ready"], 2)
            sum_squares(2, sq2, 2)
            ada_cols = ((5, 1), (6, 2))
            for c, bank in ada_cols:
                pe.wait_ge(S["x2_ready"], 2 * bank + 2)
                ada_columns(c, bank)

            def norm_out(k):
                pe.wait_ge(S["x2_ready"], 2 * k + 2)
                if k == 0:
                    pe.wait_ge(S["norm_sqrt"], 3)
                if k in (1, 2):
                    pe.wait_ge(S["ada_col_kept"], 5 + k)

            open_banks(norm_out)
            project(26, h2_h, h2_l, 8, rows=2 * KT)
            close_banks().then_inc(S["qp_done"], 1)
            pe.wait_ge(S["keys_in"], 16)
            for t in range(QT):
                for k in range(KT):
                    n = t * 4 + k // 4
                    if k % 4 == 0:
                        pe.wait_ge(S["qp_kept"], 8)
                    ins = mm(PS[:, n, (k % 4) * P:(k % 4 + 1) * P], qpT[:, k, t * P:(t + 1) * P], skT[:, k, :],
                             start=True, stop=True)
                    if k % 4 == 3:
                        ins.then_inc(S["sc_done"], 1)
            pe.wait_ge(S["sc_kept"], 8)
            ada_columns(7, 7)

            def route(g, s):
                pe.wait_ge(S["hot_a"], g + 1)
                pe.wait_ge(S["hot_b"], g + 1)
                pe.wait_ge(S["routed"], g + 1)
                for q in range(4):
                    ins = mm(PS[:, 4 + s, q * P:(q + 1) * P], hotB[:, q, :], hotA[:, q, :], start=True, stop=True)
                ins.then_inc(S["route_used"], 1)

            def first_product(b0, n, routing):
                with pe.Fori(b0, b0 + n) as b:
                    for h in range(8):
                        i = h // 4
                        pe.wait_ge(S["w_low"], 8 * b + (2 * U_U + h + 1))
                        if h % 4 == 0:
                            pe.wait_ge(S["gelu_done"], 2 * b + (i + 1))
                        for q in range(4):
                            k = 4 * (h % 4) + q
                            ins = three(PS[:, i, 0:T], h2_h[:, k, :], h2_l[:, k, :], slice(q * P, (q + 1) * P),
                                        h % SPLIT, True, k == 0, k == KT - 1)
                        used(ins)
                        if routing and h % 4 == 1:
                            route(2 * b + (i - 2 * b0), i)

            pe.sem_inc(S["gelu_done"], 2)
            pe.sem_inc(S["routed"], 2)
            first_product(0, ROUTE_AT, False)
            pe.wait_ge(S["gates_ready"], 1)
            for t in range(QT):
                for q in range(3):
                    ins = nc.tensor.transpose(PS[:, 2 + t, q * P:(q + 1) * P], sel[:, t, q, :], ident[:])
            ins.then_inc(S["gates_turned"], 1)
            first_product(ROUTE_AT, 64 - ROUTE_AT, True)

            def experts_in(k):
                pe.wait_ge(S["gelu_done"], NE_TILES + 2)
                if k == 4:
                    pe.wait_ge(S["routed"], T // 4 + 2)

            open_banks(experts_in)
            with pe.Fori(0, N_V // 4) as b:
                for h in range(8):
                    i = h // 4
                    pe.wait_ge(S["w_low"], 8 * b + (2 * U_V + h + 1))
                    if h % 4 == 0:
                        pe.wait_ge(S["p_low"], 2 * b + (i + 1))
                    for q in range(4):
                        ins = three(region(4 * (h % 4) + q), p_hi[:, i, :], p_lo[:, i, :], slice(q * P, (q + 1) * P),
                                    h % SPLIT, True, False, check=True)
                    used(ins)
            close_banks().then_inc(S["v_done"], 1)
            pe.wait_ge(S["x3_ready"], 2)
            sum_squares(3, sq3, 2 + KT)

        @block.vector
        def _(dve):
            V_ = nc.vector
            chain = {"n": 0}

            def link(ins):
                ins.then_inc(S["dve"], 1)
                chain["n"] += 1
                dve.wait_ge(S["dve"], chain["n"])

            def half_low(b, h):
                dve.wait_ge(S["w_high"], 8 * b + (h + 1))
                at_ = (h % 2) * HALF
                V_.tensor_tensor(w_lo[:, h % SPLIT, :], raw[:, h // 2 % RAW, at_:at_ + HALF],
                                 w_hi[:, h % SPLIT, :].bitcast(F32), ALU.subtract).then_inc(S["w_low"], 1)

            def split_low(b, j):
                half_low(b, 2 * j)
                half_low(b, 2 * j + 1)

            def ada_add(c, kt, last):
                n = 16 * c + kt
                dve.wait_ge(ada_in[kt % ADA], 16 * (16 + n // 4 + 1))
                if kt == 0:
                    dve.wait_ge(S["ada_zeroed"], c + 1)
                else:
                    dve.wait_ge(S["ada2_used"], n)
                ins = V_.scalar_tensor_tensor(acc[:, c % 2, :], ada[:, kt % ADA, :], silu_c[:, kt, 0:1],
                                              acc[:, c % 2, :], ALU.mult, ALU.add)
                ins.then_inc(S["ada2_used"], 1)
                if last:
                    dve.wait_ge(S["ada2_used"], n + 1)
                    dve.sem_inc(S["ada_sum"], 1)

            def norm_inverse(r):
                dve.wait_ge(S["norm_sqrt"], r + 1)
                link(V_.reciprocal(rstd[:], rstd[:]))

            def scale_and_low(xin, scale, shift, out_h, out_l, yb_):
                def low(k):
                    dve.wait_ge(S["norm_h"], 2 * KT + k + 1)
                    V_.scalar_tensor_tensor(out_l[:, k, :], yb_[:, k % 4, :], shift[:, k:k + 1],
                                            out_h[:, k, :].bitcast(F32), ALU.add, ALU.subtract
                                            ).then_inc(S["norm_l"], 1)
                for k in range(KT):
                    if k >= 4:
                        dve.wait_ge(S["norm_l"], 2 * KT + k - 3)
                    V_.scalar_tensor_tensor(yb_[:, k % 4, :], xin[:, k, :], scale[:, k:k + 1], rstd[:],
                                            ALU.mult, ALU.mult).then_inc(S["norm_y"], 1)
                    if k >= 2:
                        low(k - 2)
                low(KT - 2)
                low(KT - 1)

            def sum_tiles(r):
                dve.wait_ge(S["sq_ready"], r + 1)
                V_.reduce_sum(ksum[:, r, :], sq[:].rearrange("p k t -> p t k"), AX).then_inc(S["kt_summed"], 1)

            sum_tiles(0)
            dve.wait_ge(S["par_in"], N_SMALL)
            link(V_.tensor_tensor(lam_v[:, 0, :], lam_v[:, 0, :], lam_v[:, 1, :], ALU.mult))
            link(V_.tensor_tensor(lam_v[:, 2, :], lam_v[:, 2, :], lam_v[:, 3, :], ALU.mult))
            link(V_.reduce_sum(lam[:, 0:1], lam_v[:, 0, :], AX))
            V_.reduce_sum(lam[:, 1:2], lam_v[:, 2, :], AX).then_inc(S["lam_ready"], 1)
            link(V_.tensor_scalar(nsink[:, 1, :], nsink[:, 0, :], -1.0, None, ALU.mult))
            link(V_.tensor_scalar(norms[:, 3 * KT:3 * KT + 8], norms[:, 3 * KT:3 * KT + 8], 1.0 - LAM_INIT, None,
                                  ALU.mult))
            dve.wait_ge(S["silu"], 1)
            sum_tiles(1)
            norm_inverse(0)
            link(V_.tensor_tensor(x_c[:], x_c[:], rstd[:].unsqueeze(1).broadcast_to([P, KT, T]), ALU.mult))
            dve.sem_inc(S["xhat_ready"], 1)
            norm_inverse(1)
            link(V_.tensor_tensor(sq[:], x[:], rstd[:].unsqueeze(1).broadcast_to([P, KT, T]), ALU.mult))
            dve.wait_ge(S["ada_col"], 1)
            cols = PS[:, 4, 0:64].rearrange("p (k c) -> p k c", c=2)
            link(V_.tensor_tensor(mod[:, 0:32], cols[:, :, 0], b_ada[:, 0:32], ALU.add))
            link(V_.tensor_tensor(modc[:], cols[:, :, 1], b_ada[:, 0:32], ALU.add))
            link(V_.scalar_tensor_tensor(scl[:, 0:KT], mod[:, KT:2 * KT], 1.0, norms[:, 0:KT], ALU.add, ALU.mult))
            link(V_.scalar_tensor_tensor(scl[:, KT:2 * KT], modc[:, KT:2 * KT], 1.0, norms[:, 0:KT], ALU.add, ALU.mult))
            dve.sem_inc(S["scl_ready"], 1)
            split_low(0, 0)
            split_low(0, 1)

            def rope(dst, src, q, n):
                hv = src.rearrange("p (h d) -> p h d", d=DH)
                t0 = rt[:, 0, 0:n]
                t1 = rt[:, 1, 0:n]
                cosb = cs[:, 0, q, :].unsqueeze(1).broadcast_to([P, n // DH, DH])
                V_.tensor_tensor(t0.rearrange("p (h d) -> p h d", d=DH), hv, cosb, ALU.mult)
                s4 = src.rearrange("p (h s d) -> p h s d", s=2, d=ROPE_PAIRS)
                d4 = t1.rearrange("p (h s d) -> p h s d", s=2, d=ROPE_PAIRS)
                sn = cs[:, 1, q, :].rearrange("p (a s d) -> p a s d", s=2, d=ROPE_PAIRS)
                for s in range(2):
                    for a in range(2):
                        sv = s4.rearrange("p (h a) s d -> p h a s d", a=2)[:, :, a, 1 - s, :]
                        dv = d4.rearrange("p (h a) s d -> p h a s d", a=2)[:, :, a, s, :]
                        ins = V_.tensor_tensor(dv, sv, sn[:, a, s, :].unsqueeze(1).broadcast_to([P, n // DH, ROPE_PAIRS]),
                                               ALU.mult)
                link(ins)
                link(V_.tensor_tensor(dst, t0, t1, ALU.add))
                dve.sem_inc(S["evac_d"], 1)

            def evac(c):
                kind, banks = CHUNKS[c], BANKS[c]
                dve.wait_ge(S["w_free"], 16 * (c + 1) + SPLIT)
                if kind == "k":
                    for q in range(QT):
                        rope(Kt[:, QT + q, c * 512:c * 512 + 512], PS[:, banks[QT + q], :], q, 512)
                if kind == "kv":
                    dve.wait_ge(S["evac_a"], EVAC_A[c + 1])
                    for q in range(QT):
                        rope(Kt[:, QT + q, 1024:1280], PS[:, banks[QT + q], 0:256], q, 256)
                if kind == "q":
                    if c - 5 >= 2:
                        dve.wait_ge(S["turn_q"], 2 * (c - 5 - 1))
                    for q in range(QT):
                        rope(Qt[:, (c - 5) % 2, q, :], PS[:, banks[q], :], q, 512)

            def ada_keep(c, bank):
                dve.wait_ge(S["ada_col"], c + 2)
                V_.tensor_tensor(mod[:, 32 + 8 * c:40 + 8 * c], PS[:, bank, 0:8], b_ada[:, 32 + 8 * c:40 + 8 * c],
                                 ALU.add).then_inc(S["ada_col_kept"], 1)

            for u_ in range(8):
                for k in (2 * u_, 2 * u_ + 1):
                    for a, (xh, h_, l_, sc_, sh_) in enumerate(((x_c, hc_h, hc_l, scl[:, KT:2 * KT], modc),
                                                                 (sq, hl_h, hl_l, scl, mod))):
                        n = 2 * k + a
                        if n >= 4:
                            dve.wait_ge(S["norm_l"], n - 3)
                        V_.tensor_scalar(yb[:, n % 4, :], xh[:, k, :], sc_[:, k:k + 1], sh_[:, k:k + 1], ALU.mult, ALU.add
                                         ).then_inc(S["norm_t"], 1)
                        dve.wait_ge(S["norm_t"], n + 1)
                        dve.wait_ge(S["norm_h"], n + 1)
                        V_.tensor_tensor(l_[:, k, :], yb[:, n % 4, :], h_[:, k, :].bitcast(F32), ALU.subtract
                                         ).then_inc(S["norm_l"], 1)
                if 1 <= u_ <= 6:
                    split_low((u_ + 1) // 4, (u_ + 1) % 4)
                ada_add(0, 2 * u_, False)
                ada_add(0, 2 * u_ + 1, u_ == 7)
            for c in range(1, 9):
                n_ada = 0
                for b in (2 * c, 2 * c + 1):
                    for j in range(RAW):
                        split_low(b, j)
                        if c < 5:
                            for _ in range(2):
                                ada_add(c, n_ada, n_ada == 15)
                                n_ada += 1
                        elif j % 2 == 1:
                            kt = 4 * (c - 5) + (b % 2) * 2 + j // 2
                            ada_add(5, kt, kt == 15)
                        if c and b == 2 * c and j == 1:
                            if c in ADA_AT:
                                ada_keep(c - 1, ADA_AT[c])
                            evac(c - 1)
            split_low(18, 0)
            split_low(18, 1)
            evac(8)

            dve.wait_ge(S["lam_exp"], 1)
            link(V_.scalar_tensor_tensor(lam[:, 4:5], lam[:, 3:4], -LAM_INIT, lam[:, 2:3], ALU.add, ALU.subtract))

            def stats(n):
                m, qt, slot = n // 4, n // 2 % 2, n % 4
                dve.wait_ge(S["scored"], n + 1)
                if m >= 8:
                    keys = slice(T + P, T + 2 * P) if qt == 0 else slice(T, T + P)
                    link(V_.tensor_tensor(PS[:, slot, keys], PS[:, slot, keys], mask[:, qt, :], ALU.add))
                link(V_.reduce_max(st[:, 0, n:n + 1], PS[:, slot, :], AX))
                if m < 8:
                    V_.tensor_scalar(st[:, 1, n:n + 1], st[:, 0, n:n + 1], -SCALE, None, ALU.mult).then_inc(S["biased"], 1)
                else:
                    h = swa_head(m, n % 2)
                    V_.tensor_scalar(st[:, 1, n:n + 1], st[:, 0, n:n + 1], -SCALE, nsink[:, 1, h:h + 1],
                                     ALU.mult, ALU.min).then_inc(S["biased"], 1)

            def sink_bias(m):
                h = swa_head(m, 0)
                dve.wait_ge(S["biased"], 4 * m + 4)
                V_.tensor_tensor(st[:, 3, 4 * m:4 * m + 4].rearrange("p (q s) -> p q s", s=2),
                                 st[:, 1, 4 * m:4 * m + 4].rearrange("p (q s) -> p q s", s=2),
                                 nsink[:, 0, h:h + 5:4].unsqueeze(1).broadcast_to([P, 2, 2]), ALU.add
                                 ).then_inc(S["sink_in"], 1)

            def combine(s):
                m, slot = turned_tile(s)
                n = 4 * m + slot
                if s < 16:
                    dve.wait_ge(S["exp_done"], n + 2)
                    link(V_.reciprocal(st[:, 4, n:n + 2], st[:, 2, n:n + 2]))
                    link(V_.scalar_tensor_tensor(st[:, 5, n:n + 1], st[:, 2, n:n + 1], lam[:, 4:5], st[:, 4, n + 1:n + 2],
                                                 ALU.mult, ALU.mult))
                    V_.scalar_tensor_tensor(pr[:, m % 2, slot, :], pr[:, m % 2, slot + 1, :], st[:, 5, n:n + 1],
                                            pr[:, m % 2, slot, :], ALU.mult, ALU.add).then_inc(S["combined"], 1)
                elif slot == 0:
                    dve.wait_ge(S["exp_done"], n + 4)
                    dve.wait_ge(S["sink_exp"], m - 7)
                    link(V_.tensor_tensor(st[:, 4, n:n + 4], st[:, 2, n:n + 4], st[:, 3, n:n + 4], ALU.add))
                    V_.reciprocal(st[:, 4, n:n + 4], st[:, 4, n:n + 4]).then_inc(S["combined"], 4)

            def store_out(s):
                m, slot = turned_tile(s)
                n, qt = 4 * m + slot, slot // 2
                dve.wait_ge(S["combined"], s + 1)
                dve.wait_ge(S["pv_done"], s + 1)
                if s < 16:
                    dst, src = O[:, qt, m * P:(m + 1) * P], PS[:, 6 + s % 2, 0:P]
                else:
                    h, c0 = swa_head(m, slot % 2), slot % 2 * DH
                    dst, src = O[:, qt, 1024 + h * DH:1024 + (h + 1) * DH], PS[:, 6 + s % 2, c0:c0 + DH]
                V_.tensor_scalar(dst, src, st[:, 4, n:n + 1], None, ALU.mult).then_inc(S["o_stored"], 1)

            waiting = []
            for m in range(17):
                seq = heads_seq(m - 1) if m else []
                for a in range(4):
                    if m < 16:
                        stats(4 * m + a)
                    if a == 0 and 1 <= m <= 8:
                        combine(2 * (m - 1) + 1)
                    if a == 1 and m >= 9:
                        combine(seq[0])
                    if a < 2 and waiting:
                        store_out(waiting.pop(0))
                    if a >= 2 and a - 2 < len(seq):
                        store_out(seq[a - 2])
                if len(seq) == 4:
                    waiting = seq[2:]
                if m < 8:
                    combine(2 * m)
                elif m < 16:
                    sink_bias(m)
            for s in waiting:
                store_out(s)
            dve.wait_ge(S["o_squared"], 48)
            link(V_.tensor_scalar(st[:, 6, 0:16], st[:, 6, 0:16], 1.0 / P, EPS, ALU.mult, ALU.add))
            link(V_.tensor_scalar(st[:, 6, 16:48], st[:, 6, 16:48], 1.0 / DH, EPS, ALU.mult, ALU.add))
            dve.sem_inc(S["head_sum"], 1)
            dve.wait_ge(S["head_sqrt"], 1)
            link(V_.reciprocal(st[:, 7, 0:48], st[:, 6, 0:48]))
            dve.wait_ge(S["o_stored"], 48)
            for part in range(2):
                for t in range(QT):
                    if part == 0:
                        ov = O[:, t, 0:1024].rearrange("p (h d) -> p h d", d=P)
                        rs = st[:, 7, 0:16].rearrange("p (h t) -> p h t", t=2)[:, :, t].unsqueeze(2).broadcast_to([P, 8, P])
                        link(V_.tensor_tensor(ov, ov, rs, ALU.mult))
                    else:
                        for g in range(2):
                            for sub in range(2):
                                h0 = 8 * g + 4 * sub
                                ov = O[:, t, 1024 + h0 * DH:1024 + (h0 + 4) * DH].rearrange("p (h d) -> p h d", d=DH)
                                rs = st[:, 7, 16:48].rearrange("p (m t s) -> p m t s", t=2, s=2)[
                                    :, 4 * g:4 * g + 4, t, sub].unsqueeze(2).broadcast_to([P, 4, DH])
                                link(V_.tensor_tensor(ov, ov, rs, ALU.mult))
                dve.sem_inc(S["head_scaled"], 1)
            for k in range(KT):
                dve.wait_ge(S["o_high"], 2 * (k // 2) + 2)
                V_.scalar_tensor_tensor(oT_l[:, k, :], region(k), norms[:, 3 * KT + k:3 * KT + k + 1],
                                        oT_h[:, k, :].bitcast(F32), ALU.mult, ALU.subtract).then_inc(S["o_low"], 1)

            def stream_low(b0, n_turns, c):
                dve.wait_ge(S["ada_zeroed"], c + 1)
                with dve.Fori(0, n_turns) as b:
                    for q in range(4):
                        dve.wait_ge(ada_in[q], 16 * b + 16 * (16 + 4 * c + 1))
                        dve.wait_ge(S["ada2_used"], 4 * b + (16 * c + q))
                        V_.scalar_tensor_tensor(acc[:, c % 2, :], ada[:, q, :],
                                                silu_c[:, bass.ds(4 * b + q, 1), 0:1].rearrange("p a c -> p (a c)"),
                                                acc[:, c % 2, :], ALU.mult, ALU.add).then_inc(S["ada2_used"], 1)
                        for j in ((2, 3), (4, 5))[q % 2]:
                            split_low(2 * b + (b0 + q // 2 + j // RAW), j % RAW)
                dve.wait_ge(S["ada2_used"], 16 * c + 16)
                dve.sem_inc(S["ada_sum"], 1)

            stream_low(18, 4, 6)
            dve.wait_ge(S["attn_out"], 1)
            for k in range(KT):
                V_.scalar_tensor_tensor(x[:, k, :], region(k), mod[:, 32 + k:33 + k], x[:, k, :],
                                        ALU.mult, ALU.add).then_inc(S["x2_ready"], 1)
            ada_keep(5, 1)
            ada_keep(6, 2)
            dve.wait_ge(S["ada_col_kept"], 7)
            link(V_.scalar_tensor_tensor(scl[:, 2 * KT:3 * KT], mod[:, 4 * KT:5 * KT], 1.0, norms[:, KT:2 * KT],
                                         ALU.add, ALU.mult))
            norm_inverse(2)
            scale_and_low(x, scl[:, 2 * KT:3 * KT], mod[:, 3 * KT:4 * KT], h2_h, h2_l, yb2)
            stream_low(26, 4, 7)

            ada_keep(7, 7)

            def top16(vals, idx, src, tmp):
                link(V_.max(vals[:, 0:8], src))
                V_.max_index(idx[:, 0:8], vals[:, 0:8], src)
                link(V_.match_replace(tmp, vals[:, 0:8], src, LOWEST))
                link(V_.max(vals[:, 8:16], tmp))
                link(V_.max_index(idx[:, 8:16], vals[:, 8:16], tmp))

            half = [2 * (U_U + 2)]

            def next_low(n):
                for _ in range(n):
                    half_low(half[0] // 8, half[0] % 8)
                    half[0] += 1

            dve.wait_ge(S["sc_kept"], 8)
            for t in range(QT):
                for k in range(KT):
                    top16(v16[:, k, :], ix16[:, k, :], sc[:, t, k, :], sc2[:])
                    next_low(3)
                link(V_.tensor_copy(if16[:], ix16[:]))
                for h in range(HEADS):
                    link(V_.tensor_tensor(cand[:, h, :].rearrange("p (a b) -> p a b", b=TOPK),
                                          v16[:, 2 * h, :].unsqueeze(2).broadcast_to([P, TOPK, TOPK]),
                                          v16[:, 2 * h + 1, :].unsqueeze(1).broadcast_to([P, TOPK, TOPK]), ALU.add))
                    top16(tops[:, t, h, :], pos[:, h, :], cand[:, h, :], cand2[:])
                    next_low(5)
                pf = pos[:].rearrange("p h k -> p (h k)")
                V_.tensor_scalar(pab[:, 0, :], pf, 4, None, ALU.logical_shift_right)
                link(V_.tensor_scalar(pab[:, 1, :], pf, 15, None, ALU.bitwise_and))
                link(V_.tensor_copy(pabf[:], pab[:]))
                for side in range(2):
                    link(V_.tensor_tensor(hit[:], pabf[:, side, :].unsqueeze(2).broadcast_to([P, P, 16]),
                                          iota16[:].unsqueeze(1).broadcast_to([P, P, 16]), ALU.is_equal))
                    next_low(4)
                    hv = hit[:].rearrange("p (h k) a -> p h k a", h=HEADS)
                    iv = if16[:].rearrange("p (h c) a -> p h c a", c=2)[:, :, side, :].unsqueeze(2).broadcast_to(
                        [P, HEADS, TOPK, 16])
                    link(V_.tensor_tensor(hv, hv, iv, ALU.mult))
                    next_low(4)
                    link(V_.reduce_sum(sel[:, t, side, :], hit[:], AX))
                    next_low(4)
            for t in range(QT):
                link(V_.tensor_copy(gs[:, t, 0, :], tops[:, t, :, 0]))
                link(V_.tensor_tensor(tops[:, t], tops[:, t], gs[:, t, 0, :].unsqueeze(2).broadcast_to([P, HEADS, TOPK]),
                                      ALU.subtract))
            dve.sem_inc(S["top_s_ready"], 1)
            next_low(2 * (U_U + 2 + 4 * GATES_AT + 2) - half[0])
            dve.wait_ge(S["top_exp"], 1)
            for t in range(QT):
                link(V_.reduce_sum(gs[:, t, 1, :], ge[:, t], AX))
                link(V_.reciprocal(gs[:, t, 1, :], gs[:, t, 1, :]))
                link(V_.tensor_tensor(sel[:, t, 2, :].rearrange("p (h k) -> p h k", h=HEADS), ge[:, t],
                                      gs[:, t, 1, :].unsqueeze(2).broadcast_to([P, HEADS, TOPK]), ALU.mult))
            dve.sem_inc(S["gates_ready"], 1)

            def low_turns(b0, n):
                with dve.Fori(b0, b0 + n) as b:
                    split_low(b, 2)
                    split_low(b, 3)
                    split_low(b + 1, 0)
                    split_low(b + 1, 1)

            next_low(2 * (U_U + 2 + 4 * (GATES_AT + 1)) - half[0])

            low_turns(34 + GATES_AT + 1, ROUTE_AT - GATES_AT - 1)
            dve.wait_ge(S["gates_turned"], 1)
            for t in range(QT):
                for q, dst in enumerate((i1T, i2T, gT)):
                    V_.tensor_copy(dst[:, t * P:(t + 1) * P], PS[:, 2 + t, q * P:(q + 1) * P]).then_inc(S["gates_kept"], 1)
            dve.wait_ge(S["gates_kept"], 6)
            dve.wait_ge(S["tiles_one"], (NE_TILES - 2 * ROUTE_AT) // 8)
            dve.wait_ge(S["gelu_done"], 2 * ROUTE_AT + 2)

            def hot_a(g):
                for q in range(4):
                    ins = V_.tensor_scalar(hotA[:, q, :], iota[:], i1T[:, bass.ds(4 * g + q, 1)],
                                           gT[:, bass.ds(4 * g + q, 1)], ALU.is_equal, ALU.mult)
                ins.then_inc(S["hot_a"], 1)

            def route_in(g, s):
                dve.wait_ge(S["route_used"], g + 1)
                dve.wait_ge(S["gelu_in"], g + 2)
                av = A[:, :, bass.ds(4 * g, 4)].rearrange("p i t -> p t i")
                V_.tensor_tensor(av, av, PS[:, 4 + s, :].rearrange("p (t i) -> p t i", t=4), ALU.mult
                                 ).then_inc(S["routed"], 1)

            def gelu_in(i, s, g):
                dve.wait_ge(S["gelu_done"], i + 3)
                dve.wait_ge(S["routed"], g + 3)
                av = A[:, bass.ds(i, 1), :].rearrange("p a t -> p (a t)")
                V_.tensor_tensor(av, av, gtmp[:, s, :], ALU.mult).then_inc(S["gelu_in"], 1)

            dve.sem_inc(S["gelu_in"], 2)

            def routing_turn(b, last=False):
                for s in range(2):
                    g = 2 * b + (s - 2 * ROUTE_AT)
                    units = ((b + 34, 2), (b + 34, 3)) if s == 0 else ((b + 35, 0), (b + 35, 1))
                    split_low(*units[0])
                    route_in(g, s)
                    if not (last and s == 1):
                        hot_a(g + 1)
                    split_low(*units[1])
                    gelu_in(2 * b + s, s, g)

            hot_a(0)
            with dve.Fori(ROUTE_AT, 63) as b:
                routing_turn(b)
            routing_turn(63, last=True)

            def p_low(i, s):
                dve.wait_ge(S["p_high"], i + 1)
                V_.tensor_tensor(p_lo[:, s, :], A[:, bass.ds(i, 1), :].rearrange("p a t -> p (a t)"),
                                 p_hi[:, s, :].bitcast(F32), ALU.subtract).then_inc(S["p_low"], 1)

            dve.wait_ge(S["gelu_in"], NE_TILES - 2 * ROUTE_AT + 2)
            dve.wait_ge(S["routed"], T // 4 + 2)
            p_low(0, 0)
            p_low(1, 1)
            with dve.Fori(0, N_V // 4 - 1) as b:
                split_low(b + 98, 2)
                split_low(b + 98, 3)
                p_low(2 * b + 2, 0)
                split_low(b + 99, 0)
                split_low(b + 99, 1)
                p_low(2 * b + 3, 1)
            split_low(161, 2)
            split_low(161, 3)

            dve.wait_ge(S["v_done"], 1)
            dve.wait_ge(S["x2_in"], 16)
            for k in range(KT):
                V_.scalar_tensor_tensor(x3[:, k, :], region(k), mod[:, 5 * KT + k:5 * KT + k + 1], x2[:, k, :],
                                        ALU.mult, ALU.add).then_inc(S["x3_ready"], 1)
            norm_inverse(3)
            for k in range(KT):
                V_.scalar_tensor_tensor(ot[:, k, :], x3[:, k, :], norms[:, 2 * KT + k:2 * KT + k + 1], rstd[:],
                                        ALU.mult, ALU.mult).then_inc(S["tail_y"], 1)


def heads_seq(m):
    return list(range(2 * m, 2 * m + 2)) if m < 8 else list(range(16 + 4 * (m - 8), 20 + 4 * (m - 8)))


def turned_tile(s):
    return (s // 2, 2 * (s % 2)) if s < 16 else (8 + (s - 16) // 4, (s - 16) % 4)


def turned_after(m):
    return heads_seq(m)[-1] + 1


def swa_head(m, sub):
    return 8 * ((m - 8) // 4) + 4 * sub + (m - 8) % 4


GATES_AT = 29
ROUTE_AT = 32
NORM_BANK = [5, 6, 0, 0]
TURN_Q_BANK = [0, 2, 0, 2]
EVAC_A = [0]
EVAC_DC = [0]
for _c in CHUNKS:
    EVAC_A.append(EVAC_A[-1] + {"k": 2, "kv": 6, "v": 4, "q": 0}[_c])
    EVAC_DC.append(EVAC_DC[-1] + {"k": 2, "kv": 2, "v": 0, "q": 2}[_c])
EVAC_DK = EVAC_DC[3]
EVAC_DQ = [EVAC_DC[6 + _c] for _c in range(4)]
EVAC_D = EVAC_DC[-1]


def rope_tables():
    pos = np.arange(T, dtype=np.float32)
    row, col = np.floor(pos / GRID_W), pos % GRID_W
    freqs = np.float32(ROPE_THETA) ** (-np.arange(ROPE_PAIRS, dtype=np.float32) / np.float32(ROPE_PAIRS))
    cos, sin = np.zeros((T, DH), np.float32), np.zeros((T, DH), np.float32)
    for a, p in enumerate((row, col)):
        ang = (p[:, None] * freqs).astype(np.float32)
        for s in range(2):
            at = slice(32 * a + 16 * s, 32 * a + 16 * s + 16)
            cos[:, at] = np.cos(ang)
            sin[:, at] = np.sin(ang) * (-1.0 if s == 0 else 1.0)
    return cos, sin


def constants():
    cos, sin = rope_tables()
    tiles = lambda a: np.concatenate([a[q * P:(q + 1) * P] for q in range(QT)], axis=1)
    a = np.arange(P)
    mask = np.concatenate([np.where(a[None, :] > a[:, None], NEG, 0.0), np.where(a[:, None] > a[None, :], NEG, 0.0)], 1)
    row = lambda n: np.tile(np.arange(n, dtype=np.float32), (P, 1))
    return np.ascontiguousarray(np.concatenate([np.eye(P), row(P), row(16), tiles(cos), tiles(sin), mask], 1).astype(np.float32))


def kernel(**inp):
    import concourse.bacc as bacc
    from concourse.bass_utils import run_bass_kernel_spmd as run

    g = {k: np.asarray(a) for k, a in inp.items()}
    col = lambda a: a.reshape(-1, P).T
    feat = lambda a: np.ascontiguousarray(a.reshape(T, KT, P).transpose(2, 1, 0))
    wide = lambda a: np.broadcast_to(a.reshape(1, -1), (P, a.size))
    cc = np.stack([col(g["c"][0]), col(g["c_ctx"])], 2).reshape(P, -1)
    par = np.concatenate([
        cc, col(g["b_ada"][0]), col(g["norm_attn"][0]), col(g["norm_ffn"][0]), col(g["final_norm"]),
        col(np.concatenate([g["diff_norm"][0], g["swa_norm"][0]])), wide(g["swa_sink"][0]),
        wide(g["diff_lambda_q1"][0]), wide(g["diff_lambda_k1"][0]), wide(g["diff_lambda_q2"][0]),
        wide(g["diff_lambda_k2"][0])], 1)
    w = g["w_in"][0]
    dq, dk, dv, sq_, sk_, sv = np.split(w, [1024, 2048, 3072, 4096, 4352], axis=1)
    heads = [8 * (m // 4) + 4 * sub + m % 4 for m in range(8) for sub in range(2)]
    sq_ = np.concatenate([sq_[:, h * DH:(h + 1) * DH] for h in heads], 1)
    w = np.concatenate([dk, sk_, sv, dv, dq, sq_], 1)
    arrays = {
        "x_lat": feat(g["x"][0]), "x_ctx": feat(g["ctx"][0]),
        "par": np.ascontiguousarray(par), "con": constants(),
        "w_ada": np.ascontiguousarray(g["w_ada"][0].reshape(KT, P, 12, UNIT).transpose(2, 0, 1, 3)),
        "w_in": np.ascontiguousarray(w.reshape(8, 2, P, 9, 512).transpose(3, 0, 2, 1, 4)).reshape(N_IN, P, UNIT),
        "w_out": np.ascontiguousarray(g["w_out"][0].reshape(KT, P, 2, UNIT).transpose(0, 2, 1, 3)).reshape(N_OUT, P, UNIT),
        "w_q": np.ascontiguousarray(g["peer_w_q"][0].reshape(KT, P, 2, UNIT).transpose(0, 2, 1, 3)).reshape(N_Q, P, UNIT),
        "sk": np.ascontiguousarray(g["peer_sub_keys"][0].reshape(16, P, P).transpose(2, 0, 1)),
        "u": np.ascontiguousarray(g["peer_u"][0].reshape(NE_TILES, P, 2, 8, P).transpose(0, 2, 4, 3, 1)).reshape(N_U, P, UNIT),
        "v": np.ascontiguousarray(g["peer_v"][0].reshape(NE_TILES, P, 2, UNIT).transpose(0, 2, 1, 3)).reshape(N_V, P, UNIT),
    }
    nc = bacc.Bacc("TRN2", target_bir_lowering=False, num_devices=1)
    args = [nc.dram_tensor(n, a.shape, F32, kind="ExternalInput").ap() for n, a in arrays.items()]
    x2_dram = nc.dram_tensor("x2_scratch", [P, KT, T], F32, kind="Internal").ap()
    out = nc.dram_tensor("outT", [P, KT, T], F32, kind="ExternalOutput").ap()
    block_program(nc, *args, x2_dram, out)
    r = run(nc, [arrays], core_ids=[0])
    o = r.results[0]["outT"]
    return np.ascontiguousarray(o.transpose(2, 1, 0).reshape(1, T, D))
```

```python
from contextlib import ExitStack

import numpy as np
import concourse.bass as bass
from concourse import mybir

F32 = mybir.dt.float32
F32R = mybir.dt.float32r
BF16 = mybir.dt.bfloat16
U32 = mybir.dt.uint32
ALU = mybir.AluOpType
ACT = mybir.ActivationFunctionType
AX = mybir.AxisListType.X

P = 128
D = 2048
KT = D // P
T = 256
QT = T // P
NTOK = 2 * QT
DIFF_HEADS, SWA_HEADS, DH, SWA_KV = 8, 16, 64, 4
GRID_W, ROPE_PAIRS, ROPE_THETA, WINDOW = 64, 16, 10000.0, 128
HEADS, TOPK, NKEYS = 8, 16, 128
NE_TILES = NKEYS
EPS = 1e-6
SCALE = DH ** -0.5
LAM_INIT = 0.2
NEG = -1e30
LOWEST = -3.0e38
UNIT = 1024
HALF = UNIT // 2
RAW, SPLIT, ADA = 4, 4, 4

N_IN, N_OUT, N_Q, N_U, N_V = 72, 32, 32, 256, 256
U_IN, U_OUT = 0, N_IN
U_Q = U_OUT + N_OUT
U_U = U_Q + N_Q
U_V = U_U + N_U
U_END = U_V + N_V

PARAMS = [("cc", KT * 2), ("b_ada", 96), ("norm_attn", KT), ("norm_ffn", KT), ("final_norm", KT),
          ("head_gain", KT), ("sink", SWA_HEADS), ("lam_qk", 4 * DH)]
CONSTS = [("ident", P), ("iota", P), ("iota16", 16), ("cos", QT * DH), ("sin", QT * DH), ("mask", QT * P)]


def offsets(cols):
    at, out = 0, {}
    for name, n in cols:
        out[name] = (at, at + n)
        at += n
    return out, at


PAR, NPAR = offsets(PARAMS)
CON, NCON = offsets(CONSTS)

CHUNKS = ["k", "k", "kv", "v", "v", "q", "q", "q", "q"]
BANKS = [(0, 1, 2, 3), (4, 5, 6, 7), (0, 1, 2, 3), (4, 5, 6, 7), (0, 1, 2, 3), (4, 5), (6, 7), (4, 5), (6, 7)]
ADA_AT = {2: 7, 3: 3, 4: 5, 5: 7}
GROUPS = 4
GT = KT // GROUPS


def block_program(nc, x_lat, x_ctx, par, con, w_ada, stream, sk, x2_dram, out):
    with ExitStack() as ctx:
        sem_names = ("cc_in par_in x_in xc_in keys_in x2_in x2_out out_done "
                     "silu silu_low ada1_high ada1_low_pool ada1_low_dve ada1_used ada1_col ada2_used ada_row_kept ada_col ada_col_kept ada_zeroed ada_sum "
                     "mod_ready sq_ready norm_sum norm_sqrt norm_y norm_h norm_l norm_t tail_y kt_summed scl_ready sink_in sink_exp "
                     "dve act pool const_ready lam_ready lam_exp "
                     "w_high w_low w_free evac_a evac_d turn_k turn_k_kept turn_q turn_q_kept "
                     "scored biased exp_done combined turned turned_kept pv_done o_stored o_squared "
                     "head_sum head_sqrt head_scaled o_turned o_high o_low "
                     "attn_out x2_ready qp_done qp_kept qp_kept_d sc_done sc_kept "
                     "top_s_ready top_exp gates_ready gates_turned gates_kept gelu_done gelu_in tiles_one "
                     "dist_b dist_b2 hot_a hot_b routed route_used p_high p_low v_done x3_ready").split()
        S = {n: ctx.enter_context(nc.semaphore(n)) for n in sem_names}
        raw_in = [ctx.enter_context(nc.semaphore(f"raw_in{i}")) for i in range(RAW)]
        ada_in = [ctx.enter_context(nc.semaphore(f"ada_in{i}")) for i in range(ADA)]

        base = 16512
        KB = 1024
        slab = nc.sbuf_usable_end - base - 64

        def at(name, shape, dt, offset):
            return nc.alloc_sbuf_tensor_at(name, shape, dt, offset=base + offset)

        raw = at("raw", [P, RAW, UNIT], F32, 0)
        w_hi = at("w_hi", [P, SPLIT, HALF], F32R, 16 * KB)
        w_lo = at("w_lo", [P, SPLIT, HALF], F32R, 24 * KB)
        o = 32 * KB
        small = {}
        for name, shape, dt in [("ident", [P, P], F32), ("iota", [P, P], F32), ("iota16", [P, 16], F32),
                                ("b_ada", [P, 96], F32), ("norms", [P, 4 * KT], F32), ("mod", [P, 96], F32),
                                ("modc", [P, 32], F32), ("eps", [P, 1], F32), ("scl", [P, 4 * KT], F32),
                                ("i1T", [P, T], F32), ("i2T", [P, T], F32), ("gT", [P, T], F32),
                                ("rstd", [P, T], F32), ("ones", [P, 1], F32),
                                ("ones_sq", [P, P], F32)]:
            small[name] = at(name, shape, dt, o)
            o += 4 * int(np.prod(shape[1:]))
            o = (o + 31) // 32 * 32
        ident, iota, iota16, b_ada, norms, mod, modc, eps, scl, i1T, i2T, gT, rstd, ones, ones_sq = (
            small[n] for n in ("ident iota iota16 b_ada norms mod modc eps scl i1T i2T gT rstd ones ones_sq").split())
        R = (o + 1023) // 1024 * 1024
        assert base + R + 168 * KB + 512 <= nc.sbuf_usable_end, (R, nc.sbuf_usable_end - base - R)

        hc_h = at("hc_h", [P, KT, T], F32R, R)
        hc_l = at("hc_l", [P, KT, T], F32R, R + 16 * KB)
        kT = at("kT", [P, 10, NTOK * P], F32, R)
        qTd = at("qTd", [P, 8, T], F32, R + 20 * KB)
        Kt = at("Kt", [P, NTOK, 1280], F32, R + 32 * KB)
        O = at("O", [P, QT, D], F32, R + 32 * KB)
        V = at("V", [P, NTOK, 1280], F32, R + 52 * KB)
        Qt = at("Qt", [P, 2, QT, 512], F32, R + 72 * KB)
        qTs = at("qTs", [P, 8, T], F32, R + 80 * KB)
        x_c = at("x_c", [P, KT, T], F32, R + 32 * KB)
        sq = at("sq", [P, KT, T], F32, R + 48 * KB)
        modrow = at("modrow", [4, 2, UNIT], F32, R + 64 * KB)
        ksum = at("ksum", [P, 2, T], F32, R + 84 * KB)
        rstd_l = at("rstd_l", [P, T], F32, R + 86 * KB)
        silu_hl = at("silu_hl", [P, KT, 4], F32R, R + 87 * KB)
        ada_hi = [at(f"ada_hi{i}", [P, UNIT], F32R, R + (72, 76, 104, 108)[i] * KB) for i in range(4)]
        ada_lo = [at(f"ada_lo{i}", [P, UNIT], F32R, R + (12, 28, 140, 156)[i] * KB) for i in range(4)]
        yb = at("yb", [P, 4, T], F32, R + 80 * KB)
        ada = at("ada", [P, ADA, UNIT], F32, R + 88 * KB)
        acc = at("acc", [P, 2, UNIT], F32, R + 104 * KB)
        x = at("x", [P, KT, T], F32, R + 112 * KB)
        hl_h = at("hl_h", [P, KT, T], F32R, R + 128 * KB)
        hl_l = at("hl_l", [P, KT, T], F32R, R + 144 * KB)
        pr = at("pr", [P, 2, 4, 512], F32, R + 128 * KB)
        pT = at("pT", [P, 4, 4, P], F32, R + 144 * KB)
        oT_h = at("oT_h", [P, KT, T], F32R, R + 128 * KB)
        oT_l = at("oT_l", [P, KT, T], F32R, R + 144 * KB)
        cs = at("cs", [P, 2, QT, DH], F32, R + 160 * KB)
        mask = at("mask", [P, QT, P], F32, R + 161 * KB)
        rt = at("rt", [P, 2, 512], F32, R + 162 * KB)
        silu_c = at("silu_c", [P, KT, 2], F32, R + 166 * KB)
        lam_v = at("lam_v", [P, 4, DH], F32, R + 166 * KB + 128)
        st = at("st", [P, 8, 64], F32, R + 52 * KB + 20 * KB)
        nsink = at("nsink", [P, 2, SWA_HEADS], F32, R + 167 * KB + 128)
        lam = at("lam", [P, 8], F32, R + 167 * KB + 256)
        zeros = at("zeros", [P, T], BF16, R + 168 * KB)

        sq2 = at("sq2", [P, KT, T], F32, R + 32 * KB)
        yb2 = at("yb2", [P, 4, T], F32, R + 80 * KB)
        h2_h = at("h2_h", [P, KT, T], F32R, R + 128 * KB)
        h2_l = at("h2_l", [P, KT, T], F32R, R + 144 * KB)
        qpT = at("qpT", [P, KT, T], F32, R)
        skT = at("skT", [P, KT, P], F32, R + 24 * KB)
        sc = at("sc", [P, QT, KT, P], F32, R + 64 * KB)

        A = at("A", [P, NE_TILES, T], F32, R)
        tk = 80 * KB + R
        sc2 = at("sc2", [P, P], F32, tk)
        v16 = at("v16", [P, KT, TOPK], F32, tk + 1 * KB)
        ix16 = at("ix16", [P, KT, TOPK], U32, tk + 2 * KB)
        if16 = at("if16", [P, KT, TOPK], F32, tk + 3 * KB)
        cand = at("cand", [P, HEADS, 256], F32, tk + 4 * KB)
        cand2 = at("cand2", [P, 256], F32, tk + 12 * KB)
        tops = at("tops", [P, QT, HEADS, TOPK], F32, R + 160 * KB)
        pos = at("pos", [P, HEADS, TOPK], U32, tk + 14 * KB)
        pab = at("pab", [P, 2, HEADS * TOPK], U32, tk + 15 * KB)
        pabf = at("pabf", [P, 2, HEADS * TOPK], F32, tk + 16 * KB)
        hit = at("hit", [P, HEADS * TOPK, 16], F32, tk + 17 * KB)
        sel = at("sel", [P, QT, 3, HEADS * TOPK], F32, R + 163 * KB)
        gs = at("gs", [P, QT, 2, HEADS], F32, R + 166 * KB)
        ge = at("ge", [P, QT, HEADS, TOPK], F32, R + 161 * KB)
        hotA = at("hotA", [P, 4, P], F32, R + 160 * KB)
        hotB = at("hotB", [P, 4, P], F32, R + 162 * KB)
        gtmp = at("gtmp", [P, 2, T], F32, R + 166 * KB)
        x2 = at("x2", [P, KT, T], F32, R + 136 * KB)
        p_hi = at("p_hi", [P, 2, T], F32R, R + 152 * KB)
        p_lo = at("p_lo", [P, 2, T], F32R, R + 154 * KB)
        x3 = at("x3", [P, KT, T], F32, R)
        sq3 = at("sq3", [P, KT, T], F32, R + 16 * KB)
        ot = at("ot", [P, KT, T], F32, R + 32 * KB)
        PS = ctx.enter_context(nc.psum_tensor("PS", [P, 8, 512], F32))

        def region(dt):
            return PS[:, dt // 2, (dt % 2) * T:(dt % 2) * T + T]

        parv = {n: par[:, a:b] for n, (a, b) in PAR.items()}
        conv = {n: con[:, a:b] for n, (a, b) in CON.items()}
        SMALL_LOADS = [(silu_c[:], parv["cc"].rearrange("p (k c) -> p k c", c=2)), (b_ada[:], parv["b_ada"]),
                       (norms[:], par[:, PAR["norm_attn"][0]:PAR["head_gain"][1]]),
                       (nsink[:, 0, :], parv["sink"]), (lam_v[:], parv["lam_qk"].rearrange("p (a d) -> p a d", a=4)),
                       (ident[:], conv["ident"]), (iota[:], conv["iota"]), (iota16[:], conv["iota16"]),
                       (cs[:, 0], conv["cos"].rearrange("p (q d) -> p q d", q=QT)),
                       (cs[:, 1], conv["sin"].rearrange("p (q d) -> p q d", q=QT)),
                       (mask[:], conv["mask"].rearrange("p (q d) -> p q d", q=QT))]
        N_SMALL = 16 * (len(SMALL_LOADS) - 1)

        def ada1_low_wait(engine, n):
            mine = [k for k in range(n + 1) if low_on_pool(k) == low_on_pool(n)]
            engine.wait_ge(S["ada1_low_pool" if low_on_pool(n) else "ada1_low_dve"], len(mine))

        block = ctx.enter_context(nc.Block())

        @block.sync
        def _(sp):
            sp.dma_start(*SMALL_LOADS[0]).then_inc(S["cc_in"], 16)

            w_ada_flat = w_ada.rearrange("c k p n -> (c k) p n")

            def ada1(b, first=False):
                for j in range(ADA):
                    if not first:
                        ada1_low_wait(sp, 4 * b + j - 4)
                    sp.dma_start(ada[:, j, :], w_ada_flat[4 * b + j]).then_inc(ada_in[j], 16)

            def ada2(b, j, first=False):
                if first:
                    ada1_low_wait(sp, 60 + j)
                else:
                    sp.wait_ge(S["ada2_used"], 4 * b + (j - 3))
                sp.dma_start(ada[:, j, :], w_ada_flat[4 * b + (64 + j)]).then_inc(ada_in[j], 16)

            def unit(b, j, first=False):
                if not first:
                    sp.wait_ge(S["w_low"], 8 * b + 2 * (j - 3))
                sp.dma_start(raw[:, j, :], stream[4 * b + j]).then_inc(raw_in[j], 16)

            def units(b, first=False):
                for j in range(RAW):
                    unit(b, j, first)

            ada1(0, first=True)
            sp.dma_start(x_c[:], x_ctx).then_inc(S["xc_in"], 16)
            ada1(1)
            sp.dma_start(x[:], x_lat).then_inc(S["x_in"], 16)
            ada1(2)
            for dst, src in SMALL_LOADS[1:]:
                sp.dma_start(dst, src).then_inc(S["par_in"], 16)
            ada1(3)
            for g in range(1, GROUPS):
                ada1(4 * g)
                ada1(4 * g + 1)
                unit((g - 1) // 2, 2 * (g - 1) % 4, first=g < 3)
                unit((g - 1) // 2, 2 * (g - 1) % 4 + 1, first=g < 3)
                ada1(4 * g + 2)
                ada1(4 * g + 3)
            unit(1, 2)
            unit(1, 3)

            def key_units(b, first=False):
                for j in range(RAW):
                    unit(b, j)
                    ada2(2 * b + (j // 2 - 4), 2 * j % 4, first=first and j < 2)
                    ada2(2 * b + (j // 2 - 4), 2 * j % 4 + 1, first=first and j < 2)

            key_units(2, first=True)
            with sp.Fori(3, 10) as b:
                key_units(b)
            with sp.Fori(0, 4) as c:
                for h in range(4):
                    unit(2 * c + (10 + h // 2), 2 * h % 4)
                    unit(2 * c + (10 + h // 2), 2 * h % 4 + 1)
                    ada2(c + 16, h)
            units(U_OUT // 4)
            with sp.Fori(20, 24) as b:
                for j in range(ADA):
                    ada2(b, j)

            def middle_units(ada_block, first_block):
                with sp.Fori(0, 4) as b:
                    for q in range(4):
                        ada2(b + ada_block, q)
                        unit(2 * b + (first_block + q // 2), 2 * q % 4)
                        unit(2 * b + (first_block + q // 2), 2 * q % 4 + 1)

            middle_units(24, U_OUT // 4 + 1)
            sp.wait_ge(S["attn_out"], 1)
            sp.dma_start(skT[:], sk).then_inc(S["keys_in"], 16)
            sp.wait_ge(S["x2_ready"], KT)
            sp.dma_start(x2_dram, x[:]).then_inc(S["x2_out"], 16)
            middle_units(28, U_Q // 4 + 1)
            with sp.Fori(U_U // 4 + 1, U_V // 4 + 4) as b:
                units(b)
            sp.wait_ge(S["x2_out"], 16)
            sp.wait_ge(S["w_free"], 2 * U_V + SPLIT)
            sp.dma_start(x2[:], x2_dram).then_inc(S["x2_in"], 16)
            with sp.Fori(U_V // 4 + 4, U_END // 4) as b:
                units(b)
            for g in range(4):
                sp.wait_ge(S["tail_y"], 4 * g + 4)
                sp.dma_start(out[:, 4 * g:4 * g + 4, :], ot[:, 4 * g:4 * g + 4, :]).then_inc(S["out_done"], 16)
            sp.wait_ge(S["out_done"], 64)

        @block.gpsimd
        def _(pool):
            nc.gpsimd.memset(eps[:], EPS).then_inc(S["const_ready"], 1)
            nc.gpsimd.memset(ones[:], 1.0).then_inc(S["const_ready"], 1)
            nc.gpsimd.memset(ones_sq[:], 1.0).then_inc(S["const_ready"], 1)
            nc.gpsimd.memset(zeros[:], 0.0).then_inc(S["const_ready"], 1)
            def ada_low(n, j):
                pool.wait_ge(S["ada1_high"], n + 1)
                nc.gpsimd.tensor_tensor(ada_lo[j][:], ada[:, j, :], ada_hi[j][:].bitcast(F32), ALU.subtract
                                        ).then_inc(S["ada1_low_pool"], 1)

            with pool.Fori(0, KT // 4) as b:
                for j in range(3):
                    ada_low(4 * b + j, j)
            with pool.Fori(KT // 4, GROUPS * KT // 4) as b:
                for j in (0, 2):
                    ada_low(4 * b + j, j)
            pool.wait_ge(S["ada1_used"], GROUPS * KT)
            for c in range(8):
                if c >= 2:
                    pool.wait_ge(S["ada_col"], c - 1)
                nc.gpsimd.memset(acc[:, c % 2, :], 0.0).then_inc(S["ada_zeroed"], 1)
                if c in (5, 7):
                    pool.wait_ge(S["ada_zeroed"], c + 1)
                    for kt in range(KT):
                        n = KT * c + kt
                        pool.wait_ge(ada_in[kt % ADA], 16 * (16 + n // 4 + 1))
                        row = ada[:, kt % ADA, :]
                        nc.gpsimd.tensor_tensor(row, row, silu_c[:, kt, 0:1].broadcast_to([P, UNIT]), ALU.mult
                                                ).then_inc(S["pool"], 1)
                        pool.wait_ge(S["pool"], (c - 5) // 2 * KT + kt + 1)
                        pool.wait_ge(S["ada2_used"], n)
                        nc.gpsimd.tensor_tensor(acc[:, c % 2, :], acc[:, c % 2, :], row, ALU.add
                                                ).then_inc(S["ada2_used"], 1)
                    pool.wait_ge(S["ada2_used"], KT * (c + 1))
                    pool.sem_inc(S["ada_sum"], 1)
            pool.wait_ge(S["top_s_ready"], 1)
            pool.wait_ge(S["x2_out"], 16)
            for i in range(2 * ROUTE_AT, NE_TILES, 8):
                nc.gpsimd.memset(A[:, i:i + 8, :], 1.0).then_inc(S["tiles_one"], 1)
            pool.wait_ge(S["gates_kept"], 6)

            def distance(t0):
                nc.gpsimd.tensor_tensor(hotB[:], iota[:].unsqueeze(1).broadcast_to([P, 4, P]),
                                        i2T[:, bass.ds(t0, 4)].unsqueeze(2).broadcast_to([P, 4, P]),
                                        ALU.subtract).then_inc(S["dist_b"], 1)

            distance(0)
            with pool.Fori(1, T // 4) as g:
                pool.wait_ge(S["route_used"], g)
                distance(4 * g)

        @block.scalar
        def _(act):
            def half_high(b, j, hf):
                act.wait_ge(S["w_free"], 8 * b + (2 * j + hf + 1))
                nc.scalar.activation(w_hi[:, (2 * j + hf) % SPLIT, :], raw[:, j, hf * HALF:(hf + 1) * HALF],
                                     ACT.Copy).then_inc(S["w_high"], 1)

            def split_high(b, j):
                act.wait_ge(raw_in[j], 16 * b + 16)
                half_high(b, j, 0)
                half_high(b, j, 1)

            act.wait_ge(S["cc_in"], 16)
            nc.scalar.activation(silu_c[:], silu_c[:], ACT.Silu).then_inc(S["silu"], 1)

            def squares(xin, dst, waits):
                for k in range(KT):
                    waits(k)
                    nc.scalar.activation(dst[:, k, :], xin[:, k, :], ACT.Square).then_inc(S["sq_ready"], 1)

            def inv_root(r, dst=rstd):
                act.wait_ge(S["norm_sum"], r + 1)
                nc.scalar.activation(dst[:], PS[:, NORM_BANK[r], 0:T], ACT.Sqrt, bias=eps[:, 0:1],
                                     scale=1.0 / D).then_inc(S["norm_sqrt"], 1)

            def shift_high(r, out_h, shift, yb_):
                for k in range(KT):
                    if k in QUERY_UNIT_AT:
                        n = U_Q + 2 + QUERY_UNIT_AT.index(k)
                        split_high(n // RAW, n % RAW)
                    act.wait_ge(S["norm_y"], k + 1)
                    nc.scalar.activation(out_h[:, k, :], yb_[:, k % 4, :], ACT.Identity,
                                         bias=shift[:, k:k + 1]).then_inc(S["norm_h"], 1)

            act.wait_ge(S["silu"], 1)
            nc.scalar.activation(silu_hl[:, :, 0:2], silu_c[:], ACT.Copy).then_inc(S["silu"], 1)

            def ada_high(lo, hi):
                for n in range(lo, hi):
                    act.wait_ge(ada_in[n % 4], 16 * (n // 4 + 1))
                    if n >= 4:
                        act.wait_ge(S["ada1_used"], n - 3)
                    nc.scalar.activation(ada_hi[n % 4][:], ada[:, n % 4, :], ACT.Copy).then_inc(S["ada1_high"], 1)

            def keep_row(g):
                act.wait_ge(S["ada1_used"], KT * (g + 1))
                if g >= 2:
                    act.wait_ge(S["ada1_col"], g - 1)
                nc.scalar.activation(modrow[:, g % 2, :].rearrange("p (a n) -> p a n", a=2),
                                     PS[0:4, ADA1_BANK[g % 2]:ADA1_BANK[g % 2] + 2, :], ACT.Copy
                                     ).then_inc(S["ada_row_kept"], 1)

            def modulate_high(k):
                for xh, h_, sc_, sh_ in ((x_c, hc_h, scl[:, KT:2 * KT], modc), (sq, hl_h, scl, mod)):
                    nc.scalar.activation(h_[:, k, :], xh[:, k, :], ACT.Identity, scale=sc_[:, k:k + 1],
                                         bias=sh_[:, k:k + 1]).then_inc(S["norm_h"], 1)

            def modulate_and_split(k):
                if k % GT == 0:
                    act.wait_ge(S["scl_ready"], k // GT + 1)
                modulate_high(k)
                if k % 2 == 0:
                    act.wait_ge(raw_in[k // 2 % RAW], 16 * (k // 8) + 16)
                half_high(k // 8, k // 2 % RAW, k % 2)

            ada_high(0, 4)
            act.wait_ge(S["xc_in"], 16)
            nc.scalar.activation(sq[:], x_c[:], ACT.Square).then_inc(S["sq_ready"], 1)
            ada_high(4, 8)
            act.wait_ge(S["x_in"], 16)
            act.wait_ge(S["kt_summed"], 1)
            nc.scalar.activation(sq[:], x[:], ACT.Square).then_inc(S["sq_ready"], 1)
            ada_high(8, 12)
            act.wait_ge(S["const_ready"], 3)
            inv_root(0)
            ada_high(12, 14)
            inv_root(1, rstd_l)
            ada_high(14, 16)
            for g in range(1, GROUPS):
                n = KT * g
                ada_high(n, n + 4)
                keep_row(g - 1)
                ada_high(n + 4, n + 8)
                for a in range(GT):
                    modulate_and_split(GT * (g - 1) + a)
                    ada_high(n + 8 + a, n + 9 + a)
                ada_high(n + 12, n + 16)
            keep_row(GROUPS - 1)
            for k in range(KT - GT, KT):
                modulate_and_split(k)
            act.wait_ge(S["lam_ready"], 1)
            nc.scalar.activation(lam[:, 2:4], lam[:, 0:2], ACT.Exp).then_inc(S["lam_exp"], 1)

            def evac_copy(dst, src):
                nc.scalar.activation(dst, src, ACT.Copy).then_inc(S["evac_a"], 1)

            def evac(c):
                act.wait_ge(S["w_free"], 16 * (c + 1) + SPLIT)
                kind, banks = CHUNKS[c], BANKS[c]
                for t in range(NTOK if kind != "q" else 0):
                    src = PS[:, banks[t], :]
                    if kind == "k" and t < QT:
                        evac_copy(Kt[:, t, c * 512:c * 512 + 512], src)
                    if kind == "kv":
                        if t < QT:
                            evac_copy(Kt[:, t, 1024:1280], src[:, 0:256])
                        evac_copy(V[:, t, 1024:1280], src[:, 256:512])
                    if kind == "v":
                        evac_copy(V[:, t, (c - 3) * 512:(c - 3) * 512 + 512], src)

            def keep_k(k):
                act.wait_ge(S["turn_k"], k + 1)
                nc.scalar.activation(kT[:, k, :], PS[:, k % 4, :], ACT.Copy).then_inc(S["turn_k_kept"], 1)

            def keep_q(c):
                dst = (qTd, qTs)[c // 2]
                for a in range(2):
                    act.wait_ge(S["turn_q"], 2 * c + a + 1)
                    at_ = 4 * (c % 2) + 2 * a
                    nc.scalar.activation(dst[:, at_:at_ + 2, :],
                                         PS[:, TURN_Q_BANK[c] + a, :].rearrange("p (a t) -> p a t", a=2),
                                         ACT.Copy).then_inc(S["turn_q_kept"], 1)

            for c in range(9):
                for b in (2 * c, 2 * c + 1):
                    for j in range(RAW):
                        if b > 1:
                            split_high(b, j)
                        if c and b == 2 * c and j == 1:
                            evac(c - 1)
                        if c >= 6 and b == 2 * c and j == 1:
                            if c == 6:
                                for k in range(10):
                                    keep_k(k)
                            else:
                                keep_q(c - 7)
            split_high(18, 0)
            split_high(18, 1)
            evac(8)
            keep_q(2)
            keep_q(3)

            def exp_tile(n):
                m, slot = n // 4, n % 4
                act.wait_ge(S["biased"], n + 1)
                if m >= 2 and slot == 0:
                    act.wait_ge(S["turned"], turned_after(m - 2))
                nc.scalar.activation(pr[:, m % 2, slot, :], PS[:, slot, :], ACT.Exp, bias=st[:, 1, n:n + 1],
                                     scale=SCALE, accum_out=st[:, 2, n:n + 1]).then_inc(S["exp_done"], 1)
                if m >= 8 and slot == 3:
                    act.wait_ge(S["sink_in"], m - 7)
                    nc.scalar.activation(st[:, 3, 4 * m:4 * m + 4], st[:, 3, 4 * m:4 * m + 4], ACT.Exp
                                         ).then_inc(S["sink_exp"], 1)

            def keep_turned(s):
                act.wait_ge(S["turned"], s + 1)
                if s >= 4:
                    act.wait_ge(S["pv_done"], s - 3)
                nc.scalar.activation(pT[:, s % 4], PS[:, 4 + s % 2, :].rearrange("p (a q) -> p a q", a=4),
                                     ACT.Copy).then_inc(S["turned_kept"], 1)

            def square_out(s):
                act.wait_ge(S["o_stored"], s + 1)
                m, slot = turned_tile(s)
                if s < 16:
                    cols, w = slice(m * P, (m + 1) * P), P
                else:
                    h = swa_head(m, slot % 2)
                    cols, w = slice(1024 + h * DH, 1024 + (h + 1) * DH), DH
                if s >= 4:
                    act.wait_ge(S["o_squared"], s - 3)
                nc.scalar.activation(rt[:, 1, (s % 4) * P:(s % 4) * P + w], O[:, slot // 2, cols], ACT.Square,
                                     accum_out=st[:, 6, s:s + 1]).then_inc(S["o_squared"], 1)

            for m in range(17):
                seq = heads_seq(m - 1) if m else []
                for a in range(4):
                    if len(seq) == 4:
                        keep_turned(seq[a])
                    if m < 16:
                        exp_tile(4 * m + a)
                    if len(seq) == 2 and a < 2:
                        keep_turned(seq[a])
                for s in heads_seq(m - 2) if m > 1 else []:
                    square_out(s)
                if m == 12:
                    act.wait_ge(S["head_sum"], 1)
                    nc.scalar.activation(st[:, 6, 0:16], st[:, 6, 0:16], ACT.Sqrt).then_inc(S["head_sqrt"], 1)
            for s in heads_seq(15):
                square_out(s)
            act.wait_ge(S["head_sum"], 2)
            nc.scalar.activation(st[:, 6, 16:48], st[:, 6, 16:48], ACT.Sqrt).then_inc(S["head_sqrt"], 1)
            for k in range(KT):
                act.wait_ge(S["o_turned"], k // 2 + 1)
                nc.scalar.activation(oT_h[:, k, :], region(k), ACT.Copy, scale=norms[:, 3 * KT + k:3 * KT + k + 1]
                                     ).then_inc(S["o_high"], 1)

            def stream_high(b0, n):
                with act.Fori(0, n) as b:
                    split_high(b + b0, 2)
                    split_high(b + b0, 3)
                    split_high(b + (b0 + 1), 0)
                    split_high(b + (b0 + 1), 1)

            stream_high(18, 8)
            squares(x, sq2, lambda k: act.wait_ge(S["x2_ready"], k + 1))
            inv_root(2)
            shift_high(2, h2_h, mod[:, 3 * KT:], yb2)
            stream_high(28, 6)
            act.wait_ge(S["qp_done"], 1)
            for k in range(0, KT // 2, 2):
                nc.scalar.activation(qpT[:, 2 * k:2 * k + 2, :], PS[:, k, :].rearrange("p (a t) -> p a t", a=2),
                                     ACT.Copy).then_inc(S["qp_kept"], 1)
            for k in range(8):
                act.wait_ge(S["sc_done"], k + 1)
                nc.scalar.activation(sc[:, k // 4, 4 * (k % 4):4 * (k % 4) + 4, :],
                                     PS[:, k, :].rearrange("p (a n) -> p a n", a=4), ACT.Copy
                                     ).then_inc(S["sc_kept"], 1)

            def gelu(i, bank):
                act.wait_ge(S["w_free"], 4 * i + (2 * U_U + 4 + SPLIT))
                nc.scalar.activation(A[:, bass.ds(i, 1), :].rearrange("p a t -> p (a t)"), PS[:, bank, 0:T],
                                     ACT.Gelu_apprx_tanh).then_inc(S["gelu_done"], 1)

            def gelu_aside(i, bank):
                act.wait_ge(S["w_free"], 4 * i + (2 * U_U + 4 + SPLIT))
                act.wait_ge(S["gelu_in"], i - (2 * ROUTE_AT - 1))
                nc.scalar.activation(gtmp[:, bank, :], PS[:, bank, 0:T], ACT.Gelu_apprx_tanh
                                     ).then_inc(S["gelu_done"], 1)

            def one_hot_b(g):
                act.wait_ge(S["dist_b"], g + 1)
                nc.scalar.activation(hotB[:], hotB[:], ACT.Square).then_inc(S["dist_b2"], 1)
                act.wait_ge(S["dist_b2"], g + 1)
                nc.scalar.activation(hotB[:], hotB[:], ACT.Relu, scale=-1.0, bias=ones[:, 0:1]).then_inc(S["hot_b"], 1)

            def u_tiles(b0, n):
                with act.Fori(b0, b0 + n) as b:
                    split_high(b + 34, 2)
                    split_high(b + 34, 3)
                    gelu(2 * b, 0)
                    split_high(b + 35, 0)
                    split_high(b + 35, 1)
                    gelu(2 * b + 1, 1)

            u_tiles(0, GATES_AT)
            act.wait_ge(S["top_s_ready"], 1)
            nc.scalar.activation(ge[:], tops[:], ACT.Exp).then_inc(S["top_exp"], 1)
            u_tiles(GATES_AT, ROUTE_AT - GATES_AT)
            with act.Fori(ROUTE_AT, 64) as b:
                one_hot_b(2 * b - 2 * ROUTE_AT)
                split_high(b + 34, 2)
                split_high(b + 34, 3)
                gelu_aside(2 * b, 0)
                one_hot_b(2 * b - (2 * ROUTE_AT - 1))
                split_high(b + 35, 0)
                split_high(b + 35, 1)
                gelu_aside(2 * b + 1, 1)

            def p_high(i, s):
                act.wait_ge(S["w_free"], 4 * i + (2 * U_V - 4 + SPLIT))
                nc.scalar.activation(p_hi[:, s, :], A[:, bass.ds(i, 1), :].rearrange("p a t -> p (a t)"),
                                     ACT.Copy).then_inc(S["p_high"], 1)

            act.wait_ge(S["routed"], T // 4 + 2)
            act.wait_ge(S["gelu_in"], NE_TILES - 2 * ROUTE_AT + 2)
            p_high(0, 0)
            p_high(1, 1)
            with act.Fori(0, N_V // 4 - 1) as b:
                split_high(b + 98, 2)
                split_high(b + 98, 3)
                p_high(2 * b + 2, 0)
                split_high(b + 99, 0)
                split_high(b + 99, 1)
                p_high(2 * b + 3, 1)
            split_high(161, 2)
            split_high(161, 3)
            squares(x3, sq3, lambda k: act.wait_ge(S["x3_ready"], k + 1))
            inv_root(3)

        @block.tensor
        def _(pe):
            mm = nc.tensor.matmul

            def used(ins):
                ins.then_inc(S["w_free"], 1)

            pe.sem_inc(S["w_free"], SPLIT)

            def sum_squares(r, s, n0):
                for k in range(KT):
                    pe.wait_ge(S["sq_ready"], n0 + k + 1)
                    ins = mm(PS[:, NORM_BANK[r], 0:T], ones_sq[:], s[:, k, :], start=(k == 0), stop=(k == KT - 1))
                ins.then_inc(S["norm_sum"], 1)

            def sum_partitions(r):
                pe.wait_ge(S["kt_summed"], r + 1)
                mm(PS[:, NORM_BANK[r], 0:T], ones_sq[:], ksum[:, r, :], start=True, stop=True).then_inc(S["norm_sum"], 1)

            pe.wait_ge(S["const_ready"], 4)
            pe.wait_ge(S["silu_low"], 1)
            def three(out_, a_h, a_l, w, s, lhs_is_w, start, stop=False, check=False):
                wh, wl = w_hi[:, s, w], w_lo[:, s, w]
                pairs = ((a_h, wh), (a_h, wl), (a_l, wh)) if not lhs_is_w else ((wh, a_h), (wh, a_l), (wl, a_h))
                for q, (l_, r_) in enumerate(pairs):
                    ins = mm(out_, l_, r_, start=(start and q == 0), stop=(stop and q == 2), skip_group_check=check)
                return ins

            def ada_columns(c, bank):
                pe.wait_ge(S["ada_sum"], c + 1)
                for k in range(8):
                    ins = mm(PS[:, bank, k:k + 1], acc[:, c % 2, k * P:(k + 1) * P], ones[:], start=True, stop=True)
                ins.then_inc(S["ada_col"], 1)

            def turn_keys():
                pe.wait_ge(S["evac_a"], EVAC_A[5])
                pe.wait_ge(S["evac_d"], EVAC_DK)
                for k in range(10):
                    if k >= 4:
                        pe.wait_ge(S["turn_k_kept"], k - 3)
                    for t in range(NTOK):
                        ins = nc.tensor.transpose(PS[:, k % 4, t * P:(t + 1) * P], Kt[:, t, k * P:(k + 1) * P], ident[:])
                    ins.then_inc(S["turn_k"], 1)

            def turn_queries(c):
                pe.wait_ge(S["evac_d"], EVAC_DQ[c])
                if c == 0:
                    pe.wait_ge(S["turn_k_kept"], 10)
                if c >= 2:
                    pe.wait_ge(S["turn_q_kept"], 2 * (c - 1))
                for a in range(2):
                    for k in range(2):
                        for t in range(QT):
                            blk = 2 * a + k
                            ins = nc.tensor.transpose(PS[:, TURN_Q_BANK[c] + a, k * T + t * P:k * T + (t + 1) * P],
                                                      Qt[:, c % 2, t, blk * P:(blk + 1) * P], ident[:])
                    ins.then_inc(S["turn_q"], 1)

            def ada_products(lo, hi):
                for n in range(lo, hi):
                    g, kt = n // KT, n % KT
                    ada1_low_wait(pe, n)
                    if n == KT:
                        pe.wait_ge(S["norm_sqrt"], 2)
                    if kt == 0 and g >= 2:
                        pe.wait_ge(S["scl_ready"], g - 1)
                    for half in range(2):
                        dst = PS[0:4, ADA1_BANK[g % 2] + half, :]
                        for q, part in enumerate((ada_hi, ada_lo)):
                            ins = mm(dst, silu_hl[:, kt, :], part[n % 4][:, half * 512:half * 512 + 512],
                                     start=(kt == 0 and q == 0), stop=(kt == KT - 1 and q == 1))
                    ins.then_inc(S["ada1_used"], 1)

            def ada_turn(g):
                pe.wait_ge(S["ada_row_kept"], g + 1)
                if g == 0:
                    pe.wait_ge(S["par_in"], N_SMALL)
                for k in range(2 * GT):
                    ins = nc.tensor.transpose(PS[:, ADA1_BANK[g % 2], 4 * k:4 * k + 4], modrow[:, g % 2, k * P:(k + 1) * P],
                                              ident[0:4, 0:4])
                ins.then_inc(S["ada1_col"], 1)

            def project_half(c, k):
                kind, banks = CHUNKS[c], BANKS[c]
                h = 16 * c + k
                if c == 0:
                    pe.wait_ge(S["norm_l"], 2 * k + 2)
                pe.wait_ge(S["w_low"], h + 1)
                for t in range(len(banks)):
                    tok = t if kind != "q" else t + QT
                    h_, l_ = (hc_h, hc_l) if tok < QT else (hl_h, hl_l)
                    cols = slice((tok % QT) * P, (tok % QT + 1) * P)
                    ins = three(PS[:, banks[t], :], h_[:, k, cols], l_[:, k, cols],
                                slice(0, HALF), h % SPLIT, False, k == 0, k == KT - 1)
                used(ins)

            ada_products(0, 8)
            sum_partitions(0)
            ada_products(8, 12)
            sum_partitions(1)
            ada_products(12, 16)
            for g in range(1, GROUPS):
                n = KT * g
                ada_products(n, n + 4)
                ada_turn(g - 1)
                ada_products(n + 4, n + 8)
                k0 = GT * (g - 1)
                last = g == GROUPS - 1
                for a in range(2 if last else GT):
                    project_half(0, k0 + a)
                    ada_products(n + 8 + 2 * a, n + 10 + 2 * a)
                if last:
                    ada_products(n + 12, n + 16)
            project_half(0, KT - GT - 2)
            ada_turn(GROUPS - 1)
            for k in range(KT - GT - 1, KT):
                project_half(0, k)

            for c in range(1, 9):
                if c == 1:
                    pe.wait_ge(S["scl_ready"], GROUPS)
                if c >= 2:
                    prev = 3 if c == 6 else c - 2
                    pe.wait_ge(S["evac_a"], EVAC_A[prev + 1])
                    pe.wait_ge(S["evac_d"], EVAC_DC[prev + 1])
                if c - 1 in ADA_AT:
                    pe.wait_ge(S["ada_col_kept"], c - 2)
                for k in range(KT):
                    if c in ADA_AT and k == 10:
                        pe.wait_ge(S["evac_a"], EVAC_A[c])
                        pe.wait_ge(S["evac_d"], EVAC_DC[c])
                        ada_columns(c - 2, ADA_AT[c])
                    project_half(c, k)
                if c == 5:
                    turn_keys()
                if c >= 6:
                    turn_queries(c - 6)
            turn_queries(3)
            ada_columns(4, 4)

            def score(n):
                m, qt, sub = n // 4, n // 2 % 2, n % 2
                if n >= 4:
                    pe.wait_ge(S["exp_done"], n - 3)
                q = (qTd if m < 8 else qTs)[sub * DH:(sub + 1) * DH, m % 8, qt * P:(qt + 1) * P]
                k = m if m < 8 else 8 + (m - 8) // 4
                mm(PS[:, n % 4, :], q, kT[sub * DH:(sub + 1) * DH, k, :], start=True, stop=True
                   ).then_inc(S["scored"], 1)

            def turn_probs(s):
                m, slot = turned_tile(s)
                if s == 0:
                    pe.wait_ge(S["ada_col_kept"], 5)
                if s < 16:
                    pe.wait_ge(S["combined"], s + 1)
                else:
                    pe.wait_ge(S["exp_done"], 4 * m + slot + 1)
                if s >= 2:
                    pe.wait_ge(S["turned_kept"], s - 1)
                for k in range(NTOK):
                    ins = nc.tensor.transpose(PS[:, 4 + s % 2, k * P:(k + 1) * P], pr[:, m % 2, slot, k * P:(k + 1) * P],
                                              ident[:])
                ins.then_inc(S["turned"], 1)

            def weigh_values(s):
                m, slot = turned_tile(s)
                pe.wait_ge(S["turned_kept"], s + 1)
                if s >= 2:
                    pe.wait_ge(S["o_stored"], s - 1)
                c0 = m * P if s < 16 else 1024 + (m - 8) // 4 * P
                for k in range(NTOK):
                    ins = mm(PS[:, 6 + s % 2, 0:P], pT[:, s % 4, k, :], V[:, k, c0:c0 + P], start=(k == 0),
                             stop=(k == NTOK - 1))
                ins.then_inc(S["pv_done"], 1)

            pe.wait_ge(S["turn_q_kept"], 8)
            late = None
            for m in range(17):
                seq = heads_seq(m - 1) if m else []
                for a in range(4):
                    if m < 16:
                        score(4 * m + a)
                    if late is not None:
                        weigh_values(late)
                        late = None
                    if len(seq) == 4:
                        turn_probs(seq[a])
                        if a:
                            weigh_values(seq[a - 1])
                if len(seq) == 4:
                    late = seq[3]
                elif seq:
                    turn_probs(seq[0])
                    turn_probs(seq[1])
                    weigh_values(seq[0])
                    weigh_values(seq[1])
            weigh_values(late)
            for k in range(KT):
                if k == 0:
                    pe.wait_ge(S["exp_done"], 64)
                if k == 8:
                    pe.wait_ge(S["turned_kept"], 48)
                if k == 12:
                    pe.wait_ge(S["o_stored"], 48)
                pe.wait_ge(S["head_scaled"], 1 if k < 8 else k // 4)
                for t in range(QT):
                    ins = nc.tensor.transpose(PS[:, k // 2, (k % 2) * T + t * P:(k % 2) * T + (t + 1) * P],
                                              O[:, t, k * P:(k + 1) * P], ident[:])
                if k % 2:
                    ins.then_inc(S["o_turned"], 1)

            zeros_bank = zeros[:].unsqueeze(1).broadcast_to([P, 2, T])

            def open_banks(ready):
                for k in range(8):
                    ready(k)
                    mm(PS[:, k, :], zeros[:, 0:P], zeros_bank, start=True, stop=False)

            def close_banks():
                for k in range(8):
                    ins = mm(PS[:, k, :], zeros[:, 0:P], zeros_bank, start=False, stop=True)
                return ins

            def project(b0, a_h, a_l, n, rows=None):
                with pe.Fori(0, n) as b:
                    for h in range(8):
                        k = 2 * b + h // 4
                        if rows is not None and h % 4 == 0:
                            pe.wait_ge(S["norm_l"], 2 * b + (rows + h // 4 + 1))
                        pe.wait_ge(S["w_low"], 8 * b + (8 * b0 + h + 1))
                        for q in range(4):
                            ins = three(region(4 * (h % 4) + q), a_h[:, bass.ds(k, 1), :].rearrange("p a t -> p (a t)"),
                                        a_l[:, bass.ds(k, 1), :].rearrange("p a t -> p (a t)"),
                                        slice(q * P, (q + 1) * P), h % SPLIT, True, False, check=True)
                        used(ins)

            def head_rows_out(k):
                pe.wait_ge(S["o_high"], 2 * k + 2)
                pe.wait_ge(S["o_low"], 2 * k + 2)

            open_banks(head_rows_out)
            project(18, oT_h, oT_l, 8)
            close_banks().then_inc(S["attn_out"], 1)
            pe.wait_ge(S["x2_ready"], 2)
            sum_squares(2, sq2, 2)
            ada_cols = ((5, 1), (6, 2))
            for c, bank in ada_cols:
                pe.wait_ge(S["x2_ready"], 2 * bank + 2)
                ada_columns(c, bank)

            def norm_out(k):
                pe.wait_ge(S["x2_ready"], 2 * k + 2)
                if k == 0:
                    pe.wait_ge(S["norm_sqrt"], 3)
                if k in (1, 2):
                    pe.wait_ge(S["ada_col_kept"], 5 + k)

            open_banks(norm_out)
            project(26, h2_h, h2_l, 8, rows=2 * KT)
            close_banks().then_inc(S["qp_done"], 1)
            pe.wait_ge(S["keys_in"], 16)
            for t in range(QT):
                for k in range(KT):
                    n = t * 4 + k // 4
                    if k % 4 == 0 and t == 0:
                        pe.wait_ge(S["qp_kept"], k // 4 + 1)
                        pe.wait_ge(S["qp_kept_d"], k // 4 + 1)
                    if n == 4 and k == 0:
                        ada_columns(7, 7)
                    if n == 7 and k == 12:
                        pe.wait_ge(S["ada_col_kept"], 8)
                    ins = mm(PS[:, n, (k % 4) * P:(k % 4 + 1) * P], qpT[:, k, t * P:(t + 1) * P], skT[:, k, :],
                             start=True, stop=True)
                    if k % 4 == 3:
                        ins.then_inc(S["sc_done"], 1)
            pe.wait_ge(S["sc_kept"], 2)

            def route(g, s):
                pe.wait_ge(S["hot_a"], g + 1)
                pe.wait_ge(S["hot_b"], g + 1)
                pe.wait_ge(S["routed"], g + 1)
                for q in range(4):
                    ins = mm(PS[:, 4 + s, q * P:(q + 1) * P], hotB[:, q, :], hotA[:, q, :], start=True, stop=True)
                ins.then_inc(S["route_used"], 1)

            def first_product(b0, n, routing):
                with pe.Fori(b0, b0 + n) as b:
                    for h in range(8):
                        i = h // 4
                        pe.wait_ge(S["w_low"], 8 * b + (2 * U_U + h + 1))
                        if h % 4 == 0:
                            pe.wait_ge(S["gelu_done"], 2 * b + (i + 1))
                        for q in range(4):
                            k = 4 * (h % 4) + q
                            ins = three(PS[:, i, 0:T], h2_h[:, k, :], h2_l[:, k, :], slice(q * P, (q + 1) * P),
                                        h % SPLIT, True, k == 0, k == KT - 1)
                        used(ins)
                        if routing and h % 4 == 1:
                            route(2 * b + (i - 2 * b0), i)

            pe.sem_inc(S["gelu_done"], 2)
            pe.sem_inc(S["routed"], 2)
            first_product(0, ROUTE_AT, False)
            pe.wait_ge(S["sc_kept"], 8)
            pe.wait_ge(S["gates_ready"], 1)
            for t in range(QT):
                for q in range(3):
                    ins = nc.tensor.transpose(PS[:, 2 + t, q * P:(q + 1) * P], sel[:, t, q, :], ident[:])
            ins.then_inc(S["gates_turned"], 1)
            first_product(ROUTE_AT, 64 - ROUTE_AT, True)

            def experts_in(k):
                pe.wait_ge(S["gelu_done"], NE_TILES + 2)
                if k == 4:
                    pe.wait_ge(S["routed"], T // 4 + 2)

            open_banks(experts_in)
            with pe.Fori(0, N_V // 4) as b:
                for h in range(8):
                    i = h // 4
                    pe.wait_ge(S["w_low"], 8 * b + (2 * U_V + h + 1))
                    if h % 4 == 0:
                        pe.wait_ge(S["p_low"], 2 * b + (i + 1))
                    for q in range(4):
                        ins = three(region(4 * (h % 4) + q), p_hi[:, i, :], p_lo[:, i, :], slice(q * P, (q + 1) * P),
                                    h % SPLIT, True, False, check=True)
                    used(ins)
            close_banks().then_inc(S["v_done"], 1)
            pe.wait_ge(S["x3_ready"], 2)
            sum_squares(3, sq3, 2 + KT)

        @block.vector
        def _(dve):
            V_ = nc.vector
            chain = {"n": 0}

            def link(ins):
                ins.then_inc(S["dve"], 1)
                chain["n"] += 1
                dve.wait_ge(S["dve"], chain["n"])

            def half_low(b, h):
                dve.wait_ge(S["w_high"], 8 * b + (h + 1))
                at_ = (h % 2) * HALF
                V_.tensor_tensor(w_lo[:, h % SPLIT, :], raw[:, h // 2 % RAW, at_:at_ + HALF],
                                 w_hi[:, h % SPLIT, :].bitcast(F32), ALU.subtract).then_inc(S["w_low"], 1)

            def split_low(b, j):
                half_low(b, 2 * j)
                half_low(b, 2 * j + 1)

            def ada_add(c, kt, last):
                n = 16 * c + kt
                dve.wait_ge(ada_in[kt % ADA], 16 * (16 + n // 4 + 1))
                if kt == 0:
                    dve.wait_ge(S["ada_zeroed"], c + 1)
                else:
                    dve.wait_ge(S["ada2_used"], n)
                ins = V_.scalar_tensor_tensor(acc[:, c % 2, :], ada[:, kt % ADA, :], silu_c[:, kt, 0:1],
                                              acc[:, c % 2, :], ALU.mult, ALU.add)
                ins.then_inc(S["ada2_used"], 1)
                if last:
                    dve.wait_ge(S["ada2_used"], n + 1)
                    dve.sem_inc(S["ada_sum"], 1)

            def norm_inverse(r, root=rstd):
                dve.wait_ge(S["norm_sqrt"], r + 1)
                link(V_.reciprocal(root[:], root[:]))

            def scale_and_low(xin, scale, shift, out_h, out_l, yb_):
                def low(k):
                    dve.wait_ge(S["norm_h"], 2 * KT + k + 1)
                    V_.scalar_tensor_tensor(out_l[:, k, :], yb_[:, k % 4, :], shift[:, k:k + 1],
                                            out_h[:, k, :].bitcast(F32), ALU.add, ALU.subtract
                                            ).then_inc(S["norm_l"], 1)
                for k in range(KT):
                    if k >= 4:
                        dve.wait_ge(S["norm_l"], 2 * KT + k - 3)
                    V_.scalar_tensor_tensor(yb_[:, k % 4, :], xin[:, k, :], scale[:, k:k + 1], rstd[:],
                                            ALU.mult, ALU.mult).then_inc(S["norm_y"], 1)
                    if k >= 2:
                        low(k - 2)
                        if k in QUERY_UNIT_AT:
                            n = U_Q + 2 + QUERY_UNIT_AT.index(k)
                            split_low(n // RAW, n % RAW)
                low(KT - 2)
                low(KT - 1)

            def sum_tiles(r):
                dve.wait_ge(S["sq_ready"], r + 1)
                V_.reduce_sum(ksum[:, r, :], sq[:].rearrange("p k t -> p t k"), AX).then_inc(S["kt_summed"], 1)

            dve.wait_ge(S["silu"], 2)
            V_.tensor_tensor(silu_hl[:, :, 2:4], silu_c[:], silu_hl[:, :, 0:2].bitcast(F32), ALU.subtract
                             ).then_inc(S["silu_low"], 1)

            def ada_low(*ns):
                for n in ns:
                    dve.wait_ge(S["ada1_high"], n + 1)
                    V_.tensor_tensor(ada_lo[n % 4][:], ada[:, n % 4, :], ada_hi[n % 4][:].bitcast(F32), ALU.subtract
                                     ).then_inc(S["ada1_low_dve"], 1)

            def over_root(dst, src, root):
                link(V_.tensor_tensor(dst[:], src[:], root[:].unsqueeze(1).broadcast_to([P, KT, T]), ALU.mult))

            def modulation(g):
                dve.wait_ge(S["ada1_col"], g + 1)
                if g == 0:
                    dve.wait_ge(S["par_in"], N_SMALL)
                cols = PS[:, ADA1_BANK[g % 2], 0:8 * GT].rearrange("p (h k c) -> p h k c", h=2, c=4)
                view = lambda a: a[:, 0:2 * KT].rearrange("p (h k) -> p h k", h=2)[:, :, GT * g:GT * g + GT]
                for a, m_ in enumerate((mod, modc)):
                    ins = V_.tensor_tensor(view(m_), cols[:, :, :, a], view(b_ada), ALU.add)
                link(ins)
                for a, m_ in enumerate((mod, modc)):
                    ins = V_.tensor_tensor(view(m_), cols[:, :, :, 2 + a], view(m_), ALU.add)
                link(ins)
                lo = GT * g
                for a, m_ in enumerate((mod, modc)):
                    ins = V_.scalar_tensor_tensor(scl[:, KT * a + lo:KT * a + lo + GT], m_[:, KT + lo:KT + lo + GT], 1.0,
                                                  norms[:, lo:lo + GT], ALU.add, ALU.mult)
                ins.then_inc(S["scl_ready"], 1)

            def modulate_low(k):
                for a, (xh, h_, l_, sc_, sh_) in enumerate(((x_c, hc_h, hc_l, scl[:, KT:2 * KT], modc),
                                                             (sq, hl_h, hl_l, scl, mod))):
                    n = 2 * k + a
                    if n >= 4:
                        dve.wait_ge(S["norm_l"], n - 3)
                    V_.tensor_scalar(yb[:, n % 4, :], xh[:, k, :], sc_[:, k:k + 1], sh_[:, k:k + 1], ALU.mult, ALU.add
                                     ).then_inc(S["norm_t"], 1)
                    dve.wait_ge(S["norm_t"], n + 1)
                    dve.wait_ge(S["norm_h"], n + 1)
                    V_.tensor_tensor(l_[:, k, :], yb[:, n % 4, :], h_[:, k, :].bitcast(F32), ALU.subtract
                                     ).then_inc(S["norm_l"], 1)

            def modulate_and_split(k):
                if k % GT == 0:
                    dve.wait_ge(S["scl_ready"], k // GT + 1)
                modulate_low(k)
                half_low(k // 8, k % 8)

            ada_low(3)
            sum_tiles(0)
            ada_low(7)
            sum_tiles(1)
            ada_low(11)
            norm_inverse(0)
            over_root(x_c, x_c, rstd)
            ada_low(15)
            norm_inverse(1, rstd_l)
            over_root(sq, x, rstd_l)
            for g in range(1, GROUPS):
                n, k0 = KT * g, GT * (g - 1)
                ada_low(n + 1, n + 3)
                modulation(g - 1)
                ada_low(n + 5)
                modulate_and_split(k0)
                ada_low(n + 7)
                modulate_and_split(k0 + 1)
                ada_low(n + 9)
                modulate_and_split(k0 + 2)
                modulate_and_split(k0 + 3)
                ada_low(n + 11, n + 13, n + 15)
            modulation(GROUPS - 1)
            for k in range(KT - GT, KT):
                modulate_and_split(k)
            link(V_.tensor_tensor(lam_v[:, 0, :], lam_v[:, 0, :], lam_v[:, 1, :], ALU.mult))
            link(V_.tensor_tensor(lam_v[:, 2, :], lam_v[:, 2, :], lam_v[:, 3, :], ALU.mult))
            link(V_.reduce_sum(lam[:, 0:1], lam_v[:, 0, :], AX))
            V_.reduce_sum(lam[:, 1:2], lam_v[:, 2, :], AX).then_inc(S["lam_ready"], 1)
            link(V_.tensor_scalar(nsink[:, 1, :], nsink[:, 0, :], -1.0, None, ALU.mult))
            link(V_.tensor_scalar(norms[:, 3 * KT:3 * KT + 8], norms[:, 3 * KT:3 * KT + 8], 1.0 - LAM_INIT, None,
                                  ALU.mult))

            def rope(dst, src, q, n):
                hv = src.rearrange("p (h d) -> p h d", d=DH)
                t0 = rt[:, 0, 0:n]
                t1 = rt[:, 1, 0:n]
                cosb = cs[:, 0, q, :].unsqueeze(1).broadcast_to([P, n // DH, DH])
                V_.tensor_tensor(t0.rearrange("p (h d) -> p h d", d=DH), hv, cosb, ALU.mult)
                s4 = src.rearrange("p (h s d) -> p h s d", s=2, d=ROPE_PAIRS)
                d4 = t1.rearrange("p (h s d) -> p h s d", s=2, d=ROPE_PAIRS)
                sn = cs[:, 1, q, :].rearrange("p (a s d) -> p a s d", s=2, d=ROPE_PAIRS)
                for s in range(2):
                    for a in range(2):
                        sv = s4.rearrange("p (h a) s d -> p h a s d", a=2)[:, :, a, 1 - s, :]
                        dv = d4.rearrange("p (h a) s d -> p h a s d", a=2)[:, :, a, s, :]
                        ins = V_.tensor_tensor(dv, sv, sn[:, a, s, :].unsqueeze(1).broadcast_to([P, n // DH, ROPE_PAIRS]),
                                               ALU.mult)
                link(ins)
                link(V_.tensor_tensor(dst, t0, t1, ALU.add))
                dve.sem_inc(S["evac_d"], 1)

            def evac(c):
                kind, banks = CHUNKS[c], BANKS[c]
                dve.wait_ge(S["w_free"], 16 * (c + 1) + SPLIT)
                if kind == "k":
                    for q in range(QT):
                        rope(Kt[:, QT + q, c * 512:c * 512 + 512], PS[:, banks[QT + q], :], q, 512)
                if kind == "kv":
                    dve.wait_ge(S["evac_a"], EVAC_A[c + 1])
                    for q in range(QT):
                        rope(Kt[:, QT + q, 1024:1280], PS[:, banks[QT + q], 0:256], q, 256)
                if kind == "q":
                    if c - 5 >= 2:
                        dve.wait_ge(S["turn_q"], 2 * (c - 5 - 1))
                    for q in range(QT):
                        rope(Qt[:, (c - 5) % 2, q, :], PS[:, banks[q], :], q, 512)

            def ada_keep(c, bank):
                dve.wait_ge(S["ada_col"], c + 1)
                V_.tensor_tensor(mod[:, 32 + 8 * c:40 + 8 * c], PS[:, bank, 0:8], b_ada[:, 32 + 8 * c:40 + 8 * c],
                                 ALU.add).then_inc(S["ada_col_kept"], 1)

            for c in range(1, 9):
                n_ada = 0
                for b in (2 * c, 2 * c + 1):
                    for j in range(RAW):
                        split_low(b, j)
                        if c < 5:
                            for _ in range(2):
                                ada_add(c - 1, n_ada, n_ada == 15)
                                n_ada += 1
                        elif j % 2 == 1:
                            kt = 4 * (c - 5) + (b % 2) * 2 + j // 2
                            ada_add(4, kt, kt == 15)
                        if b == 2 * c and j == 1:
                            evac(c - 1)
                        if c in ADA_AT and b == 2 * c + 1 and j == 1:
                            ada_keep(c - 2, ADA_AT[c])
            split_low(18, 0)
            split_low(18, 1)
            evac(8)

            ada_keep(4, 4)
            dve.wait_ge(S["lam_exp"], 1)
            link(V_.scalar_tensor_tensor(lam[:, 4:5], lam[:, 3:4], -LAM_INIT, lam[:, 2:3], ALU.add, ALU.subtract))

            def stats(n):
                m, qt, slot = n // 4, n // 2 % 2, n % 4
                dve.wait_ge(S["scored"], n + 1)
                if m >= 8:
                    keys = slice(T + P, T + 2 * P) if qt == 0 else slice(T, T + P)
                    link(V_.tensor_tensor(PS[:, slot, keys], PS[:, slot, keys], mask[:, qt, :], ALU.add))
                link(V_.reduce_max(st[:, 0, n:n + 1], PS[:, slot, :], AX))
                if m < 8:
                    V_.tensor_scalar(st[:, 1, n:n + 1], st[:, 0, n:n + 1], -SCALE, None, ALU.mult).then_inc(S["biased"], 1)
                else:
                    h = swa_head(m, n % 2)
                    V_.tensor_scalar(st[:, 1, n:n + 1], st[:, 0, n:n + 1], -SCALE, nsink[:, 1, h:h + 1],
                                     ALU.mult, ALU.min).then_inc(S["biased"], 1)

            def sink_bias(m):
                h = swa_head(m, 0)
                dve.wait_ge(S["biased"], 4 * m + 4)
                V_.tensor_tensor(st[:, 3, 4 * m:4 * m + 4].rearrange("p (q s) -> p q s", s=2),
                                 st[:, 1, 4 * m:4 * m + 4].rearrange("p (q s) -> p q s", s=2),
                                 nsink[:, 0, h:h + 5:4].unsqueeze(1).broadcast_to([P, 2, 2]), ALU.add
                                 ).then_inc(S["sink_in"], 1)

            def combine(s):
                m, slot = turned_tile(s)
                n = 4 * m + slot
                if s < 16:
                    dve.wait_ge(S["exp_done"], n + 2)
                    link(V_.reciprocal(st[:, 4, n:n + 2], st[:, 2, n:n + 2]))
                    link(V_.scalar_tensor_tensor(st[:, 5, n:n + 1], st[:, 2, n:n + 1], lam[:, 4:5], st[:, 4, n + 1:n + 2],
                                                 ALU.mult, ALU.mult))
                    V_.scalar_tensor_tensor(pr[:, m % 2, slot, :], pr[:, m % 2, slot + 1, :], st[:, 5, n:n + 1],
                                            pr[:, m % 2, slot, :], ALU.mult, ALU.add).then_inc(S["combined"], 1)
                elif slot == 0:
                    dve.wait_ge(S["exp_done"], n + 4)
                    dve.wait_ge(S["sink_exp"], m - 7)
                    link(V_.tensor_tensor(st[:, 4, n:n + 4], st[:, 2, n:n + 4], st[:, 3, n:n + 4], ALU.add))
                    V_.reciprocal(st[:, 4, n:n + 4], st[:, 4, n:n + 4]).then_inc(S["combined"], 4)

            def store_out(s):
                m, slot = turned_tile(s)
                n, qt = 4 * m + slot, slot // 2
                dve.wait_ge(S["combined"], s + 1)
                dve.wait_ge(S["pv_done"], s + 1)
                if s < 16:
                    dst, src = O[:, qt, m * P:(m + 1) * P], PS[:, 6 + s % 2, 0:P]
                else:
                    h, c0 = swa_head(m, slot % 2), slot % 2 * DH
                    dst, src = O[:, qt, 1024 + h * DH:1024 + (h + 1) * DH], PS[:, 6 + s % 2, c0:c0 + DH]
                V_.tensor_scalar(dst, src, st[:, 4, n:n + 1], None, ALU.mult).then_inc(S["o_stored"], 1)

            def head_means(part):
                dve.wait_ge(S["o_squared"], (16, 48)[part])
                cols = (slice(0, 16), slice(16, 48))[part]
                link(V_.tensor_scalar(st[:, 6, cols], st[:, 6, cols], 1.0 / (P, DH)[part], EPS, ALU.mult, ALU.add))
                dve.sem_inc(S["head_sum"], 1)

            def scale_heads(part):
                dve.wait_ge(S["head_sqrt"], part + 1)
                cols = (slice(0, 16), slice(16, 48))[part]
                link(V_.reciprocal(st[:, 7, cols], st[:, 6, cols]))
                dve.wait_ge(S["o_stored"], (16, 48)[part])
                if part == 0:
                    for t in range(QT):
                        ov = O[:, t, 0:1024].rearrange("p (h d) -> p h d", d=P)
                        rs = st[:, 7, 0:16].rearrange("p (h t) -> p h t", t=2)[:, :, t].unsqueeze(2).broadcast_to([P, 8, P])
                        ins = V_.tensor_tensor(ov, ov, rs, ALU.mult)
                    link(ins)
                    dve.sem_inc(S["head_scaled"], 1)
                for g in range(2 if part else 0):
                    for t in range(QT):
                        for sub in range(2):
                            h0 = 8 * g + 4 * sub
                            ov = O[:, t, 1024 + h0 * DH:1024 + (h0 + 4) * DH].rearrange("p (h d) -> p h d", d=DH)
                            rs = st[:, 7, 16:48].rearrange("p (m t s) -> p m t s", t=2, s=2)[
                                :, 4 * g:4 * g + 4, t, sub].unsqueeze(2).broadcast_to([P, 4, DH])
                            ins = V_.tensor_tensor(ov, ov, rs, ALU.mult)
                    link(ins)
                    dve.sem_inc(S["head_scaled"], 1)

            waiting = []
            for m in range(17):
                seq = heads_seq(m - 1) if m else []
                if len(seq) == 2:
                    while waiting:
                        store_out(waiting.pop(0))
                    combine(seq[0])
                    combine(seq[1])
                for a in range(4):
                    if m < 16:
                        stats(4 * m + a)
                    if len(seq) == 4:
                        if a == 1:
                            combine(seq[0])
                        store_out((waiting + seq[:2])[a])
                waiting = seq[-2:]
                if m == 11:
                    head_means(0)
                if m == 13:
                    scale_heads(0)
                if 8 <= m < 16:
                    sink_bias(m)
            for s in waiting:
                store_out(s)
            head_means(1)
            scale_heads(1)
            for k in range(KT):
                dve.wait_ge(S["o_high"], 2 * (k // 2) + 2)
                V_.scalar_tensor_tensor(oT_l[:, k, :], region(k), norms[:, 3 * KT + k:3 * KT + k + 1],
                                        oT_h[:, k, :].bitcast(F32), ALU.mult, ALU.subtract).then_inc(S["o_low"], 1)

            def stream_low(b0, n_turns, c):
                dve.wait_ge(S["ada_zeroed"], c + 1)
                with dve.Fori(0, n_turns) as b:
                    for q in range(4):
                        dve.wait_ge(ada_in[q], 16 * b + 16 * (16 + 4 * c + 1))
                        dve.wait_ge(S["ada2_used"], 4 * b + (16 * c + q))
                        V_.scalar_tensor_tensor(acc[:, c % 2, :], ada[:, q, :],
                                                silu_c[:, bass.ds(4 * b + q, 1), 0:1].rearrange("p a c -> p (a c)"),
                                                acc[:, c % 2, :], ALU.mult, ALU.add).then_inc(S["ada2_used"], 1)
                        for j in ((2, 3), (4, 5))[q % 2]:
                            split_low(2 * b + (b0 + q // 2 + j // RAW), j % RAW)
                dve.wait_ge(S["ada2_used"], 16 * c + 16)
                dve.sem_inc(S["ada_sum"], 1)

            stream_low(18, 4, 6)
            dve.wait_ge(S["attn_out"], 1)
            for k in range(KT):
                V_.scalar_tensor_tensor(x[:, k, :], region(k), mod[:, 32 + k:33 + k], x[:, k, :],
                                        ALU.mult, ALU.add).then_inc(S["x2_ready"], 1)
            ada_keep(5, 1)
            dve.wait_ge(S["ada_col_kept"], 6)
            link(V_.scalar_tensor_tensor(scl[:, 2 * KT:3 * KT], mod[:, 4 * KT:5 * KT], 1.0, norms[:, KT:2 * KT],
                                         ALU.add, ALU.mult))
            norm_inverse(2)
            ada_keep(6, 2)
            scale_and_low(x, scl[:, 2 * KT:3 * KT], mod[:, 3 * KT:4 * KT], h2_h, h2_l, yb2)
            def low_turns(b0, n):
                with dve.Fori(b0, b0 + n) as b:
                    split_low(b, 2)
                    split_low(b, 3)
                    split_low(b + 1, 0)
                    split_low(b + 1, 1)

            low_turns(U_Q // RAW + 2, 6)

            dve.wait_ge(S["qp_done"], 1)
            for k in range(1, KT // 2, 2):
                V_.tensor_copy(qpT[:, 2 * k:2 * k + 2, :], PS[:, k, :].rearrange("p (a t) -> p a t", a=2)
                               ).then_inc(S["qp_kept_d"], 1)

            ada_keep(7, 7)

            def top16(vals, idx, src, tmp):
                link(V_.max(vals[:, 0:8], src))
                V_.max_index(idx[:, 0:8], vals[:, 0:8], src)
                link(V_.match_replace(tmp, vals[:, 0:8], src, LOWEST))
                link(V_.max(vals[:, 8:16], tmp))
                link(V_.max_index(idx[:, 8:16], vals[:, 8:16], tmp))

            half = [2 * (U_U + 2)]

            def next_low(n):
                for _ in range(n):
                    half_low(half[0] // 8, half[0] % 8)
                    half[0] += 1

            dve.wait_ge(S["sc_kept"], 8)
            for t in range(QT):
                for k in range(KT):
                    top16(v16[:, k, :], ix16[:, k, :], sc[:, t, k, :], sc2[:])
                    next_low(3)
                link(V_.tensor_copy(if16[:], ix16[:]))
                for h in range(HEADS):
                    link(V_.tensor_tensor(cand[:, h, :].rearrange("p (a b) -> p a b", b=TOPK),
                                          v16[:, 2 * h, :].unsqueeze(2).broadcast_to([P, TOPK, TOPK]),
                                          v16[:, 2 * h + 1, :].unsqueeze(1).broadcast_to([P, TOPK, TOPK]), ALU.add))
                    top16(tops[:, t, h, :], pos[:, h, :], cand[:, h, :], cand2[:])
                    next_low(5)
                pf = pos[:].rearrange("p h k -> p (h k)")
                V_.tensor_scalar(pab[:, 0, :], pf, 4, None, ALU.logical_shift_right)
                link(V_.tensor_scalar(pab[:, 1, :], pf, 15, None, ALU.bitwise_and))
                link(V_.tensor_copy(pabf[:], pab[:]))
                for side in range(2):
                    link(V_.tensor_tensor(hit[:], pabf[:, side, :].unsqueeze(2).broadcast_to([P, P, 16]),
                                          iota16[:].unsqueeze(1).broadcast_to([P, P, 16]), ALU.is_equal))
                    next_low(4)
                    hv = hit[:].rearrange("p (h k) a -> p h k a", h=HEADS)
                    iv = if16[:].rearrange("p (h c) a -> p h c a", c=2)[:, :, side, :].unsqueeze(2).broadcast_to(
                        [P, HEADS, TOPK, 16])
                    link(V_.tensor_tensor(hv, hv, iv, ALU.mult))
                    next_low(4)
                    link(V_.reduce_sum(sel[:, t, side, :], hit[:], AX))
                    next_low(4)
            for t in range(QT):
                link(V_.tensor_copy(gs[:, t, 0, :], tops[:, t, :, 0]))
                link(V_.tensor_tensor(tops[:, t], tops[:, t], gs[:, t, 0, :].unsqueeze(2).broadcast_to([P, HEADS, TOPK]),
                                      ALU.subtract))
            dve.sem_inc(S["top_s_ready"], 1)
            next_low(2 * (U_U + 2 + 4 * GATES_AT + 2) - half[0])
            dve.wait_ge(S["top_exp"], 1)
            for t in range(QT):
                link(V_.reduce_sum(gs[:, t, 1, :], ge[:, t], AX))
                link(V_.reciprocal(gs[:, t, 1, :], gs[:, t, 1, :]))
                link(V_.tensor_tensor(sel[:, t, 2, :].rearrange("p (h k) -> p h k", h=HEADS), ge[:, t],
                                      gs[:, t, 1, :].unsqueeze(2).broadcast_to([P, HEADS, TOPK]), ALU.mult))
            dve.sem_inc(S["gates_ready"], 1)

            next_low(2 * (U_U + 2 + 4 * (GATES_AT + 1)) - half[0])

            low_turns(34 + GATES_AT + 1, ROUTE_AT - GATES_AT - 1)
            dve.wait_ge(S["gates_turned"], 1)
            for t in range(QT):
                for q, dst in enumerate((i1T, i2T, gT)):
                    V_.tensor_copy(dst[:, t * P:(t + 1) * P], PS[:, 2 + t, q * P:(q + 1) * P]).then_inc(S["gates_kept"], 1)
            dve.wait_ge(S["gates_kept"], 6)
            dve.wait_ge(S["tiles_one"], (NE_TILES - 2 * ROUTE_AT) // 8)
            dve.wait_ge(S["gelu_done"], 2 * ROUTE_AT + 2)

            def hot_a(g):
                for q in range(4):
                    ins = V_.tensor_scalar(hotA[:, q, :], iota[:], i1T[:, bass.ds(4 * g + q, 1)],
                                           gT[:, bass.ds(4 * g + q, 1)], ALU.is_equal, ALU.mult)
                ins.then_inc(S["hot_a"], 1)

            def route_in(g, s):
                dve.wait_ge(S["route_used"], g + 1)
                dve.wait_ge(S["gelu_in"], g + 2)
                av = A[:, :, bass.ds(4 * g, 4)].rearrange("p i t -> p t i")
                V_.tensor_tensor(av, av, PS[:, 4 + s, :].rearrange("p (t i) -> p t i", t=4), ALU.mult
                                 ).then_inc(S["routed"], 1)

            def gelu_in(i, s, g):
                dve.wait_ge(S["gelu_done"], i + 3)
                dve.wait_ge(S["routed"], g + 3)
                av = A[:, bass.ds(i, 1), :].rearrange("p a t -> p (a t)")
                V_.tensor_tensor(av, av, gtmp[:, s, :], ALU.mult).then_inc(S["gelu_in"], 1)

            dve.sem_inc(S["gelu_in"], 2)

            def routing_turn(b, last=False):
                for s in range(2):
                    g = 2 * b + (s - 2 * ROUTE_AT)
                    units = ((b + 34, 2), (b + 34, 3)) if s == 0 else ((b + 35, 0), (b + 35, 1))
                    split_low(*units[0])
                    route_in(g, s)
                    if not (last and s == 1):
                        hot_a(g + 1)
                    split_low(*units[1])
                    gelu_in(2 * b + s, s, g)

            hot_a(0)
            with dve.Fori(ROUTE_AT, 63) as b:
                routing_turn(b)
            routing_turn(63, last=True)

            def p_low(i, s):
                dve.wait_ge(S["p_high"], i + 1)
                V_.tensor_tensor(p_lo[:, s, :], A[:, bass.ds(i, 1), :].rearrange("p a t -> p (a t)"),
                                 p_hi[:, s, :].bitcast(F32), ALU.subtract).then_inc(S["p_low"], 1)

            dve.wait_ge(S["gelu_in"], NE_TILES - 2 * ROUTE_AT + 2)
            dve.wait_ge(S["routed"], T // 4 + 2)
            p_low(0, 0)
            p_low(1, 1)
            with dve.Fori(0, N_V // 4 - 1) as b:
                split_low(b + 98, 2)
                split_low(b + 98, 3)
                p_low(2 * b + 2, 0)
                split_low(b + 99, 0)
                split_low(b + 99, 1)
                p_low(2 * b + 3, 1)
            split_low(161, 2)
            split_low(161, 3)

            dve.wait_ge(S["v_done"], 1)
            dve.wait_ge(S["x2_in"], 16)
            for k in range(KT):
                V_.scalar_tensor_tensor(x3[:, k, :], region(k), mod[:, 5 * KT + k:5 * KT + k + 1], x2[:, k, :],
                                        ALU.mult, ALU.add).then_inc(S["x3_ready"], 1)
            norm_inverse(3)
            for k in range(KT):
                V_.scalar_tensor_tensor(ot[:, k, :], x3[:, k, :], norms[:, 2 * KT + k:2 * KT + k + 1], rstd[:],
                                        ALU.mult, ALU.mult).then_inc(S["tail_y"], 1)


def heads_seq(m):
    return list(range(2 * m, 2 * m + 2)) if m < 8 else list(range(16 + 4 * (m - 8), 20 + 4 * (m - 8)))


def turned_tile(s):
    return (s // 2, 2 * (s % 2)) if s < 16 else (8 + (s - 16) // 4, (s - 16) % 4)


def turned_after(m):
    return heads_seq(m)[-1] + 1


def swa_head(m, sub):
    return 8 * ((m - 8) // 4) + 4 * sub + (m - 8) % 4


def low_on_pool(n):
    return n % 4 != 3 if n < KT else n % 2 == 0


GATES_AT = 29
ROUTE_AT = 32
QUERY_UNIT_AT = (3, 4, 6, 7, 8, 9, 10, 12)
NORM_BANK = [6, 7, 0, 0]
ADA1_BANK = [4, 6]
TURN_Q_BANK = [0, 2, 0, 2]
EVAC_A = [0]
EVAC_DC = [0]
for _c in CHUNKS:
    EVAC_A.append(EVAC_A[-1] + {"k": 2, "kv": 6, "v": 4, "q": 0}[_c])
    EVAC_DC.append(EVAC_DC[-1] + {"k": 2, "kv": 2, "v": 0, "q": 2}[_c])
EVAC_DK = EVAC_DC[3]
EVAC_DQ = [EVAC_DC[6 + _c] for _c in range(4)]


def rope_tables():
    pos = np.arange(T, dtype=np.float32)
    row, col = np.floor(pos / GRID_W), pos % GRID_W
    freqs = np.float32(ROPE_THETA) ** (-np.arange(ROPE_PAIRS, dtype=np.float32) / np.float32(ROPE_PAIRS))
    cos, sin = np.zeros((T, DH), np.float32), np.zeros((T, DH), np.float32)
    for a, p in enumerate((row, col)):
        ang = (p[:, None] * freqs).astype(np.float32)
        for s in range(2):
            at = slice(32 * a + 16 * s, 32 * a + 16 * s + 16)
            cos[:, at] = np.cos(ang)
            sin[:, at] = np.sin(ang) * (-1.0 if s == 0 else 1.0)
    return cos, sin


def constants():
    cos, sin = rope_tables()
    tiles = lambda a: np.concatenate([a[q * P:(q + 1) * P] for q in range(QT)], axis=1)
    a = np.arange(P)
    mask = np.concatenate([np.where(a[None, :] > a[:, None], NEG, 0.0), np.where(a[:, None] > a[None, :], NEG, 0.0)], 1)
    row = lambda n: np.tile(np.arange(n, dtype=np.float32), (P, 1))
    return np.ascontiguousarray(np.concatenate([np.eye(P), row(P), row(16), tiles(cos), tiles(sin), mask], 1).astype(np.float32))


def kernel(**inp):
    import concourse.bacc as bacc
    from concourse.bass_utils import run_bass_kernel_spmd as run

    g = {k: np.asarray(a) for k, a in inp.items()}
    col = lambda a: a.reshape(-1, P).T
    feat = lambda a: np.ascontiguousarray(a.reshape(T, KT, P).transpose(2, 1, 0))
    wide = lambda a: np.broadcast_to(a.reshape(1, -1), (P, a.size))
    cc = np.stack([col(g["c"][0]), col(g["c_ctx"])], 2).reshape(P, -1)
    par = np.concatenate([
        cc, col(g["b_ada"][0]), col(g["norm_attn"][0]), col(g["norm_ffn"][0]), col(g["final_norm"]),
        col(np.concatenate([g["diff_norm"][0], g["swa_norm"][0]])), wide(g["swa_sink"][0]),
        wide(g["diff_lambda_q1"][0]), wide(g["diff_lambda_k1"][0]), wide(g["diff_lambda_q2"][0]),
        wide(g["diff_lambda_k2"][0])], 1)
    w = g["w_in"][0]
    dq, dk, dv, sq_, sk_, sv = np.split(w, [1024, 2048, 3072, 4096, 4352], axis=1)
    heads = [8 * (m // 4) + 4 * sub + m % 4 for m in range(8) for sub in range(2)]
    sq_ = np.concatenate([sq_[:, h * DH:(h + 1) * DH] for h in heads], 1)
    w = np.concatenate([dk, sk_, sv, dv, dq, sq_], 1)
    w_a = g["w_ada"][0].reshape(KT, P, 12 * UNIT)
    first = w_a[:, :, 0:2 * D].reshape(KT, P, 2, GROUPS, GT * P).transpose(3, 0, 1, 2, 4).reshape(GROUPS, KT, P, UNIT)
    rest = w_a[:, :, 2 * D:].reshape(KT, P, 8, UNIT).transpose(2, 0, 1, 3)
    stream = [w.reshape(8, 2, P, 9, 512).transpose(3, 0, 2, 1, 4),
              g["w_out"][0].reshape(KT, P, 2, UNIT).transpose(0, 2, 1, 3),
              g["peer_w_q"][0].reshape(KT, P, 2, UNIT).transpose(0, 2, 1, 3),
              g["peer_u"][0].reshape(NE_TILES, P, 2, 8, P).transpose(0, 2, 4, 3, 1),
              g["peer_v"][0].reshape(NE_TILES, P, 2, UNIT).transpose(0, 2, 1, 3)]
    arrays = {
        "x_lat": feat(g["x"][0]), "x_ctx": feat(g["ctx"][0]),
        "par": np.ascontiguousarray(par), "con": constants(),
        "w_ada": np.concatenate([first, rest]),
        "stream": np.concatenate([a.reshape(-1, P, UNIT) for a in stream]),
        "sk": np.ascontiguousarray(g["peer_sub_keys"][0].reshape(16, P, P).transpose(2, 0, 1)),
    }
    nc = bacc.Bacc("TRN2", target_bir_lowering=False, num_devices=1)
    args = [nc.dram_tensor(n, a.shape, F32, kind="ExternalInput").ap() for n, a in arrays.items()]
    x2_dram = nc.dram_tensor("x2_scratch", [P, KT, T], F32, kind="Internal").ap()
    out = nc.dram_tensor("outT", [P, KT, T], F32, kind="ExternalOutput").ap()
    block_program(nc, *args, x2_dram, out)
    r = run(nc, [arrays], core_ids=[0])
    o = r.results[0]["outT"]
    return np.ascontiguousarray(o.transpose(2, 1, 0).reshape(1, T, D))
```
